# Optimizing a Trainium2 kernel written in Bass

```python
import math
import jax, jax.numpy as jnp
from jax import lax
import numpy as np

D_MODEL = 1024
BATCH = 1
SEQ = 256
DEPTH = 2

MEM_TOKENS = 256
GRID_W = 64
A_HEADS = 4
A_HEAD_DIM = D_MODEL // 8
A_WIDTH = A_HEADS * A_HEAD_DIM
A_CONV = 5
A_CHUNK = 128
B_HEADS = 8
B_HEAD_DIM = D_MODEL // 16
B_WIDTH = B_HEADS * B_HEAD_DIM
NA_ROWS = 8
NA_COLS = 16
C_HEADS = 8
C_HEAD_DIM = D_MODEL // 16
C_WIDTH = C_HEADS * 2 * C_HEAD_DIM
Q_BLOCK = 128
X_HEADS = 4
X_HEAD_DIM = D_MODEL // X_HEADS
FFN_HIDDEN = -(-8 * D_MODEL // (3 * 256)) * 256
ROPE_THETA = 10000.0
LN_EPS = 1e-5
DEEPNORM_ALPHA = (2 * DEPTH) ** 0.25
DEEPNORM_BETA = (8 * DEPTH) ** -0.25
N_EVEN = (DEPTH + 1) // 2
N_ODD = DEPTH // 2
EVEN_IN = 4 * A_WIDTH + 4 * A_HEADS + 3 * B_WIDTH
STATE_NEG = -1e30


def layer_norm(x, g, b):
    xf = x.astype(jnp.float32)
    mu = jnp.mean(xf, axis=-1, keepdims=True)
    var = jnp.mean(jnp.square(xf - mu), axis=-1, keepdims=True)
    return ((xf - mu) * lax.rsqrt(var + LN_EPS)).astype(x.dtype) * g + b

def rms_norm(x, g):
    xf = x.astype(jnp.float32)
    y = xf * lax.rsqrt(jnp.mean(jnp.square(xf), axis=-1, keepdims=True) + LN_EPS)
    return y.astype(x.dtype) * g

def split_cols(t, widths):
    offs = np.cumsum(widths)[:-1].tolist()
    return jnp.split(t, offs, axis=-1)

def centred_depthwise_conv(x, w):
    K, C = w.shape
    return lax.conv_general_dilated(
        x, w.reshape(K, 1, C).astype(x.dtype), window_strides=(1,),
        padding=[(K // 2, K // 2)], dimension_numbers=('NWC', 'WIO', 'NWC'),
        feature_group_count=C)

def rope(t):
    S, d = t.shape[1], t.shape[-1]
    inv_freq = ROPE_THETA ** (-jnp.arange(0, d, 2, dtype=jnp.float32) / d)
    ang = jnp.arange(S, dtype=jnp.float32)[:, None] * inv_freq[None, :]
    cos = jnp.cos(ang)[:, None, :]
    sin = jnp.sin(ang)[:, None, :]
    tf = t.astype(jnp.float32)
    t1, t2 = tf[..., : d // 2], tf[..., d // 2:]
    return jnp.concatenate([t1 * cos - t2 * sin, t1 * sin + t2 * cos], axis=-1).astype(t.dtype)

def mlstm_chunkwise(q, k, v, log_i, log_f):
    N, H, S, d = q.shape
    L = min(A_CHUNK, S)
    NC = S // L
    qc = q.reshape(N, H, NC, L, d)
    kc = k.reshape(N, H, NC, L, d)
    vc = v.reshape(N, H, NC, L, d)
    ai = log_i.reshape(N, H, NC, L)
    b = jnp.cumsum(log_f.reshape(N, H, NC, L), axis=-1)
    g = b[..., -1]
    w_end = g[..., None] - b + ai
    m_loc = jnp.max(w_end, axis=-1)
    p = jnp.exp(w_end - m_loc[..., None])
    kv_loc = jnp.einsum('nhcl,nhcld,nhcle->nhcde', p, kc, vc)
    k_loc = jnp.einsum('nhcl,nhcld->nhcd', p, kc)

    def step(carry, inp):
        C, nv, m = carry
        g_c, m_c, kv_c, k_c = inp
        m_new = jnp.maximum(g_c + m, m_c)
        s_old = jnp.exp(g_c + m - m_new)
        s_new = jnp.exp(m_c - m_new)
        C_new = s_old[..., None, None] * C + s_new[..., None, None] * kv_c
        n_new = s_old[..., None] * nv + s_new[..., None] * k_c
        return (C_new, n_new, m_new), (C, nv, m)

    init = (jnp.zeros((N, H, d, d), jnp.float32), jnp.zeros((N, H, d), jnp.float32),
            jnp.full((N, H), STATE_NEG, jnp.float32))
    xs = (jnp.moveaxis(g, 2, 0), jnp.moveaxis(m_loc, 2, 0),
          jnp.moveaxis(kv_loc, 2, 0), jnp.moveaxis(k_loc, 2, 0))
    _, (C_in, n_in, m_in) = lax.scan(step, init, xs)
    C_in = jnp.moveaxis(C_in, 0, 2)
    n_in = jnp.moveaxis(n_in, 0, 2)
    m_in = jnp.moveaxis(m_in, 0, 2)
    upto = jnp.tril(jnp.ones((L, L), dtype=bool))
    D = jnp.where(upto, b[..., :, None] - b[..., None, :] + ai[..., None, :], -jnp.inf)
    m_inter = b + m_in[..., None]
    m = jnp.maximum(jnp.max(D, axis=-1), m_inter)
    Smat = jnp.einsum('nhcld,nhcsd->nhcls', qc, kc) * jnp.exp(D - m[..., None])
    s_inter = jnp.exp(m_inter - m)
    num = (jnp.einsum('nhcls,nhcse->nhcle', Smat, vc)
           + s_inter[..., None] * jnp.einsum('nhcld,nhcde->nhcle', qc, C_in))
    den = jnp.sum(Smat, axis=-1) + s_inter * jnp.einsum('nhcld,nhcd->nhcl', qc, n_in)
    h = num / jnp.maximum(jnp.abs(den), jnp.exp(-m))[..., None]
    return h.reshape(N, H, S, d)

def neighbourhood_attention(q, k, v, rpb):
    B_, S, H, d = q.shape
    R = S // GRID_W
    kr = min(NA_ROWS, R)
    q = q.reshape(B_, R, GRID_W, H, d) * (d ** -0.5)
    k = k.reshape(B_, R, GRID_W, H, d)
    v = v.reshape(B_, R, GRID_W, H, d)
    rows = jnp.arange(R)
    row_start = jnp.clip(rows - NA_ROWS // 2, 0, R - kr)
    key_rows = row_start[:, None] + jnp.arange(kr)[None, :]
    k_blk = k[:, key_rows]
    v_blk = v[:, key_rows]
    cols = jnp.arange(GRID_W)
    col_start = jnp.clip(cols - NA_COLS // 2, 0, GRID_W - NA_COLS)
    in_win = (cols[None, :] >= col_start[:, None]) & (cols[None, :] < col_start[:, None] + NA_COLS)
    rel_r = key_rows - rows[:, None] + (NA_ROWS - 1)
    rel_c = jnp.clip(cols[None, :] - cols[:, None] + (NA_COLS - 1), 0, 2 * NA_COLS - 2)
    bias = rpb[:, rel_r[:, None, :, None], rel_c[None, :, None, :]]
    s = jnp.einsum('brqhd,brikhd->bhrqik', q, k_blk).astype(jnp.float32) + bias.astype(jnp.float32)
    s = jnp.where(in_win[:, None, :], s, -jnp.inf)
    p = jax.nn.softmax(s.reshape(B_, H, R, GRID_W, kr * GRID_W), axis=-1)
    p = p.reshape(B_, H, R, GRID_W, kr, GRID_W).astype(v.dtype)
    out = jnp.einsum('bhrqik,brikhd->brqhd', p, v_blk)
    return out.reshape(B_, S, H * d)

def diff_attention(q, k, v, lam):
    B_, S, H, _, d = q.shape
    nb = S // Q_BLOCK
    qb = jnp.moveaxis(q.reshape(B_, nb, Q_BLOCK, H, 2, d), 1, 0)
    scale = d ** -0.5

    def block(qi):
        s = jnp.einsum('bqhcd,bkhcd->bhcqk', qi, k).astype(jnp.float32) * scale
        p = jax.nn.softmax(s, axis=-1)
        a = p[:, :, 0] - lam * p[:, :, 1]
        return jnp.einsum('bhqk,bkhe->bqhe', a.astype(v.dtype), v)

    out = lax.map(block, qb)
    return jnp.moveaxis(out, 0, 1).reshape(B_, S, H, 2 * d)

def memory_cross_attention(x, mem, wq, wkv, wo):
    B_, S, _ = x.shape
    M = mem.shape[1]
    q = (x @ wq).reshape(B_, S, X_HEADS, X_HEAD_DIM) * (X_HEAD_DIM ** -0.5)
    k, v = jnp.split(mem @ wkv, 2, axis=-1)
    k = k.reshape(B_, M, X_HEADS, X_HEAD_DIM)
    v = v.reshape(B_, M, X_HEADS, X_HEAD_DIM)
    p = jax.nn.softmax(jnp.einsum('bshd,bmhd->bhsm', q, k).astype(jnp.float32), axis=-1)
    o = jnp.einsum('bhsm,bmhd->bshd', p.astype(v.dtype), v)
    return o.reshape(B_, S, D_MODEL) @ wo

def swiglu(x, w_gu, w_down):
    gate, up = jnp.split(x @ w_gu, 2, axis=-1)
    return (jax.nn.silu(gate) * up) @ w_down

def even_mixer(x, w_in, gate_b, conv_w, rpb, w_out):
    B_, S, _ = x.shape
    a_qk, a_v, a_o, a_g, b_q, b_k, b_v = split_cols(
        x @ w_in, [2 * A_WIDTH, A_WIDTH, A_WIDTH, 4 * A_HEADS, B_WIDTH, B_WIDTH, B_WIDTH])
    a_qk = jax.nn.silu(centred_depthwise_conv(a_qk, conv_w))
    a_q, a_k = jnp.split(a_qk, 2, axis=-1)

    def heads(t):
        return t.reshape(B_, S, A_HEADS, A_HEAD_DIM).transpose(0, 2, 1, 3).astype(jnp.float32)

    q, k, v = heads(a_q), heads(a_k) * (A_HEAD_DIM ** -0.5), heads(a_v)
    gates = (a_g.astype(jnp.float32) + gate_b.astype(jnp.float32)).reshape(B_, S, 4, A_HEADS).transpose(2, 0, 3, 1)

    def both_dirs(t):
        return jnp.concatenate([t, jnp.flip(t, axis=2)], axis=0)

    log_i = jnp.concatenate([gates[0], jnp.flip(gates[1], axis=-1)], axis=0)
    log_f = jax.nn.log_sigmoid(jnp.concatenate([gates[2], jnp.flip(gates[3], axis=-1)], axis=0))
    h2 = mlstm_chunkwise(both_dirs(q), both_dirs(k), both_dirs(v), log_i, log_f)
    h = h2[:B_] + jnp.flip(h2[B_:], axis=2)
    h = h.transpose(0, 2, 1, 3).reshape(B_, S, A_WIDTH).astype(x.dtype)
    a_out = jax.nn.sigmoid(a_o) * h
    b_out = neighbourhood_attention(b_q.reshape(B_, S, B_HEADS, B_HEAD_DIM),
                                    b_k.reshape(B_, S, B_HEADS, B_HEAD_DIM),
                                    b_v.reshape(B_, S, B_HEADS, B_HEAD_DIM), rpb)
    return jnp.concatenate([a_out, b_out], axis=-1) @ w_out

def odd_mixer(x, w_in, lam_p, subln_g, w_out, lam_init):
    B_, S, _ = x.shape
    q, k, v = jnp.split(x @ w_in, 3, axis=-1)
    q = rope(q.reshape(B_, S, 2 * C_HEADS, C_HEAD_DIM)).reshape(B_, S, C_HEADS, 2, C_HEAD_DIM)
    k = rope(k.reshape(B_, S, 2 * C_HEADS, C_HEAD_DIM)).reshape(B_, S, C_HEADS, 2, C_HEAD_DIM)
    v = v.reshape(B_, S, C_HEADS, 2 * C_HEAD_DIM)
    lp = lam_p.astype(jnp.float32)
    lam = jnp.exp(jnp.sum(lp[0] * lp[1])) - jnp.exp(jnp.sum(lp[2] * lp[3])) + lam_init
    o = diff_attention(q, k, v, lam)
    o = rms_norm(o, subln_g) * (1.0 - lam_init)
    return o.reshape(B_, S, C_WIDTH) @ w_out

def first_inputs(seed: int = 0) -> dict:
    key = jax.random.key(seed)
    ks = jax.random.split(key, 20)

    def nrm(kk, shape, scale):
        return jax.random.normal(kk, shape, jnp.float32) * scale

    x = nrm(ks[0], (BATCH, SEQ, D_MODEL), 1.0)
    mem = nrm(ks[1], (BATCH, MEM_TOKENS, D_MODEL), 1.0)
    even_w_in = nrm(ks[2], (N_EVEN, D_MODEL, EVEN_IN), D_MODEL ** -0.5)
    i_bias = nrm(ks[3], (N_EVEN, 2 * A_HEADS), 0.1)
    f_lin = jnp.linspace(3.0, 6.0, A_HEADS, dtype=jnp.float32)
    f_bias = jnp.concatenate([f_lin, f_lin])[None, :] + nrm(ks[4], (N_EVEN, 2 * A_HEADS), 0.1)
    even_gate_b = jnp.concatenate([i_bias, f_bias], axis=-1)
    even_conv_w = nrm(ks[5], (N_EVEN, A_CONV, 2 * A_WIDTH), A_CONV ** -0.5)
    even_rpb = nrm(ks[6], (N_EVEN, B_HEADS, 2 * NA_ROWS - 1, 2 * NA_COLS - 1), 0.02)
    even_w_out = nrm(ks[7], (N_EVEN, A_WIDTH + B_WIDTH, D_MODEL), (A_WIDTH + B_WIDTH) ** -0.5 * DEEPNORM_BETA)
    odd_w_in = nrm(ks[8], (N_ODD, D_MODEL, 3 * C_WIDTH), D_MODEL ** -0.5)
    odd_lambda = nrm(ks[9], (N_ODD, 4, C_HEAD_DIM), 0.1)
    odd_subln_g = 1.0 + nrm(ks[10], (N_ODD, 2 * C_HEAD_DIM), 0.02)
    odd_w_out = nrm(ks[11], (N_ODD, C_WIDTH, D_MODEL), C_WIDTH ** -0.5 * DEEPNORM_BETA)
    mem_wq = nrm(ks[12], (DEPTH, D_MODEL, D_MODEL), D_MODEL ** -0.5)
    mem_wkv = nrm(ks[13], (DEPTH, D_MODEL, 2 * D_MODEL), D_MODEL ** -0.5)
    mem_wo = nrm(ks[14], (DEPTH, D_MODEL, D_MODEL), D_MODEL ** -0.5 * DEEPNORM_BETA)
    ffn_w_gu = nrm(ks[15], (DEPTH, D_MODEL, 2 * FFN_HIDDEN), D_MODEL ** -0.5)
    ffn_w_down = nrm(ks[16], (DEPTH, FFN_HIDDEN, D_MODEL), FFN_HIDDEN ** -0.5 * DEEPNORM_BETA)
    ln_g = 1.0 + nrm(ks[17], (DEPTH, 3, D_MODEL), 0.02)
    ln_b = nrm(ks[18], (DEPTH, 3, D_MODEL), 0.02)
    return {'x': x, 'mem': mem, 'even_w_in': even_w_in, 'even_gate_b': even_gate_b,
            'even_conv_w': even_conv_w, 'even_rpb': even_rpb, 'even_w_out': even_w_out,
            'odd_w_in': odd_w_in, 'odd_lambda': odd_lambda, 'odd_subln_g': odd_subln_g,
            'odd_w_out': odd_w_out, 'mem_wq': mem_wq, 'mem_wkv': mem_wkv, 'mem_wo': mem_wo,
            'ffn_w_gu': ffn_w_gu, 'ffn_w_down': ffn_w_down, 'ln_g': ln_g, 'ln_b': ln_b}

def first_block(x, mem, even_w_in, even_gate_b, even_conv_w, even_rpb, even_w_out,
              odd_w_in, odd_lambda, odd_subln_g, odd_w_out, mem_wq, mem_wkv, mem_wo,
              ffn_w_gu, ffn_w_down, ln_g, ln_b):
    for layer in range(DEPTH):
        j = layer // 2
        if layer % 2 == 0:
            mix = even_mixer(x, even_w_in[j], even_gate_b[j], even_conv_w[j], even_rpb[j], even_w_out[j])
        else:
            lam_init = 0.8 - 0.6 * math.exp(-0.3 * layer)
            mix = odd_mixer(x, odd_w_in[j], odd_lambda[j], odd_subln_g[j], odd_w_out[j], lam_init)
        x = layer_norm(DEEPNORM_ALPHA * x + mix, ln_g[layer, 0], ln_b[layer, 0])
        xa = memory_cross_attention(x, mem, mem_wq[layer], mem_wkv[layer], mem_wo[layer])
        x = layer_norm(DEEPNORM_ALPHA * x + xa, ln_g[layer, 1], ln_b[layer, 1])
        ff = swiglu(x, ffn_w_gu[layer], ffn_w_down[layer])
        x = layer_norm(DEEPNORM_ALPHA * x + ff, ln_g[layer, 2], ln_b[layer, 2])
    return x


MEM_LEN = 256
BLOCK_Q = 128
H_A = 8
DH_A = 64
DC_A = 128
H_IDX = 8
DH_IDX = 64
TOPK_MAX = 256
H_SB = 8
DH_SB = 64
C_CONV = 512
CONV_W = 3
W_A = H_A * DH_A
W_SB = H_SB * DH_SB
W_BRANCH = 512
N_BRANCH = 3
H_X = 4
DH_X = 128
D_FF = 2816
N_BUCKETS = 32
MAX_DISTANCE = 128
DN_ALPHA = (2 * DEPTH) ** 0.25
DN_BETA = (8 * DEPTH) ** -0.25
N_LN = 4
SPLITS = (W_A, DC_A, H_IDX * DH_IDX, DH_IDX, H_IDX, W_SB, W_SB, W_SB,
          C_CONV, C_CONV, C_CONV, D_MODEL, D_MODEL, D_MODEL)
P_TOTAL = sum(SPLITS)


def layer_norm_2(x, g, b):
    xf = x.astype(jnp.float32)
    mu = jnp.mean(xf, axis=-1, keepdims=True)
    var = jnp.mean(jnp.square(xf - mu), axis=-1, keepdims=True)
    y = (xf - mu) * lax.rsqrt(var + LN_EPS) * g.astype(jnp.float32) + b.astype(jnp.float32)
    return y.astype(x.dtype)

def rms_norm_2(x, g):
    xf = x.astype(jnp.float32)
    y = xf * lax.rsqrt(jnp.mean(jnp.square(xf), axis=-1, keepdims=True) + LN_EPS) * g.astype(jnp.float32)
    return y.astype(x.dtype)

def swiglu_ffn(x, w_in, w_out):
    a, b = jnp.split(x @ w_in, 2, axis=-1)
    return (jax.nn.silu(a) * b) @ w_out

def t5_bucket(n):
    max_exact = N_BUCKETS // 2
    n = jnp.maximum(n, 0)
    nf = jnp.maximum(n, 1).astype(jnp.float32)
    large = max_exact + (jnp.log(nf / max_exact) / math.log(MAX_DISTANCE / max_exact)
                         * (N_BUCKETS - max_exact)).astype(jnp.int32)
    large = jnp.minimum(large, N_BUCKETS - 1)
    return jnp.where(n < max_exact, n, large)

def dsa_branch(q, c_kv, iq, ik, iw, w_uk, w_uv, rel_bias):
    bsz, seq = q.shape[0], q.shape[1]
    k_top = min(TOPK_MAX, seq // 4)
    nblk = seq // BLOCK_Q
    q_lat = jnp.einsum('bshd,hdc->bshc', q, w_uk) * (DH_A ** -0.5)
    idx_scale = (H_IDX ** -0.5) * (DH_IDX ** -0.5)

    def to_blocks(a):
        return jnp.swapaxes(a.reshape((bsz, nblk, BLOCK_Q) + a.shape[2:]), 0, 1)

    starts = jnp.arange(nblk, dtype=jnp.int32) * BLOCK_Q
    key_pos = jnp.arange(seq, dtype=jnp.int32)

    def block(args):
        ql, iqb, iwb, start = args
        t = start + jnp.arange(BLOCK_Q, dtype=jnp.int32)
        causal = key_pos[None, :] <= t[:, None]
        dots = jnp.einsum('bqhd,bsd->bhqs', iqb, ik).astype(jnp.float32)
        score = jnp.einsum('bqh,bhqs->bqs', iwb.astype(jnp.float32) * idx_scale, jax.nn.relu(dots))
        score = jnp.where(causal[None], score, -jnp.inf)
        _, idx = lax.top_k(score, k_top)
        valid = idx <= t[None, :, None]
        kv_sel = jax.vmap(lambda c, i: c[i])(c_kv, idx)
        logits = jnp.einsum('bqhc,bqkc->bhqk', ql, kv_sel).astype(jnp.float32)
        bias = rel_bias[t5_bucket(t[None, :, None] - idx)]
        logits = logits + jnp.transpose(bias, (0, 3, 1, 2)).astype(jnp.float32)
        logits = jnp.where(valid[:, None], logits, -1e30)
        p = jax.nn.softmax(logits, axis=-1).astype(kv_sel.dtype)
        return jnp.einsum('bhqk,bqkc->bqhc', p, kv_sel)

    o_lat = lax.map(block, (to_blocks(q_lat), to_blocks(iq), to_blocks(iw), starts))
    o_lat = jnp.swapaxes(o_lat, 0, 1).reshape(bsz, seq, H_A, DC_A)
    o = jnp.einsum('bshc,hcd->bshd', o_lat, w_uv)
    return o.reshape(bsz, seq, W_A)

def stick_breaking_branch(q, k, v):
    bsz, seq = q.shape[0], q.shape[1]
    scale = DH_SB ** -0.5
    outs = []
    for i in range(seq // BLOCK_Q):
        q0 = i * BLOCK_Q
        end = q0 + BLOCK_Q
        z = jnp.einsum('bqhd,bshd->bhqs', q[:, q0:end], k[:, :end]).astype(jnp.float32) * scale
        t = q0 + jnp.arange(BLOCK_Q)
        s = jnp.arange(end)
        strict = (s[None, :] < t[:, None])[None, None]
        log_not = jnp.where(strict, jax.nn.log_sigmoid(-z), 0.0)
        later = lax.cumsum(log_not, axis=3, reverse=True) - log_not
        a = jnp.where(strict, jnp.exp(jax.nn.log_sigmoid(z) + later), 0.0)
        outs.append(jnp.einsum('bhqs,bshd->bqhd', a.astype(v.dtype), v[:, :end]))
    return jnp.concatenate(outs, axis=1).reshape(bsz, seq, W_SB)

def short_conv_branch(b_gate_in, c_gate_in, h, conv_w):
    z = c_gate_in * h
    y = lax.conv_general_dilated(z, conv_w[:, None, :].astype(z.dtype), window_strides=(1,),
                                 padding=((CONV_W - 1, 0),),
                                 dimension_numbers=('NWC', 'WIO', 'NWC'),
                                 feature_group_count=C_CONV)
    return b_gate_in * y

def mixer_sublayer(x, w_in, b_gate, kv_g, w_uk, w_uv, conv_w, w_branch, w_out, rel_bias):
    bsz, seq = x.shape[0], x.shape[1]
    offsets = [int(o) for o in np.cumsum(SPLITS)[:-1]]
    (qa, ckv, iq, ik, iw, qs, ks, vs, cb, cc, ch, ga, gb, gc) = jnp.split(x @ w_in, offsets, axis=-1)
    ckv = rms_norm_2(ckv, kv_g)
    y_a = dsa_branch(qa.reshape(bsz, seq, H_A, DH_A), ckv,
                     iq.reshape(bsz, seq, H_IDX, DH_IDX), ik, iw, w_uk, w_uv, rel_bias)
    hs = (bsz, seq, H_SB, DH_SB)
    y_b = stick_breaking_branch(qs.reshape(hs), ks.reshape(hs), vs.reshape(hs))
    y_c = short_conv_branch(cb, cc, ch, conv_w)
    merged = (jax.nn.sigmoid(ga + b_gate[0]) * (y_a @ w_branch[0])
              + jax.nn.sigmoid(gb + b_gate[1]) * (y_b @ w_branch[1])
              + jax.nn.sigmoid(gc + b_gate[2]) * (y_c @ w_branch[2]))
    return merged @ w_out

def memory_cross_attention_2(x, mem, wq, wkv, wo):
    bsz, seq = x.shape[0], x.shape[1]
    q = (x @ wq).reshape(bsz, seq, H_X, DH_X)
    k, v = jnp.split(mem @ wkv, 2, axis=-1)
    k = k.reshape(bsz, mem.shape[1], H_X, DH_X)
    v = v.reshape(bsz, mem.shape[1], H_X, DH_X)
    logits = jnp.einsum('bqhd,bmhd->bhqm', q, k).astype(jnp.float32) * (DH_X ** -0.5)
    p = jax.nn.softmax(logits, axis=-1).astype(v.dtype)
    o = jnp.einsum('bhqm,bmhd->bqhd', p, v).reshape(bsz, seq, H_X * DH_X)
    return o @ wo

def second_inputs(seed: int = 0) -> dict:
    key = jax.random.key(seed)
    ks = jax.random.split(key, 20)
    n = jax.random.normal
    f32 = jnp.float32
    return {
        "x": n(ks[0], (BATCH, SEQ, D_MODEL), f32),
        "mem": n(ks[1], (BATCH, MEM_LEN, D_MODEL), f32),
        "ln_g": 1.0 + 0.01 * n(ks[2], (DEPTH, N_LN, D_MODEL), f32),
        "ln_b": 0.01 * n(ks[3], (DEPTH, N_LN, D_MODEL), f32),
        "ffn_w_in": n(ks[4], (DEPTH, 2, D_MODEL, 2 * D_FF), f32) * D_MODEL ** -0.5,
        "ffn_w_out": n(ks[5], (DEPTH, 2, D_FF, D_MODEL), f32) * (D_FF ** -0.5 * DN_BETA),
        "w_mix_in": n(ks[6], (DEPTH, D_MODEL, P_TOTAL), f32) * D_MODEL ** -0.5,
        "b_gate": 0.01 * n(ks[7], (DEPTH, N_BRANCH, D_MODEL), f32),
        "kv_norm_g": 1.0 + 0.01 * n(ks[8], (DEPTH, DC_A), f32),
        "w_uk": n(ks[9], (DEPTH, H_A, DH_A, DC_A), f32) * DH_A ** -0.5,
        "w_uv": n(ks[10], (DEPTH, H_A, DC_A, DH_A), f32) * DC_A ** -0.5,
        "conv_w": n(ks[11], (DEPTH, CONV_W, C_CONV), f32) * CONV_W ** -0.5,
        "w_branch": n(ks[12], (DEPTH, N_BRANCH, W_BRANCH, D_MODEL), f32) * W_BRANCH ** -0.5,
        "w_mix_out": n(ks[13], (DEPTH, D_MODEL, D_MODEL), f32) * (D_MODEL ** -0.5 * DN_BETA),
        "xa_wq": n(ks[14], (DEPTH, D_MODEL, H_X * DH_X), f32) * D_MODEL ** -0.5,
        "xa_wkv": n(ks[15], (DEPTH, D_MODEL, 2 * H_X * DH_X), f32) * D_MODEL ** -0.5,
        "xa_wo": n(ks[16], (DEPTH, H_X * DH_X, D_MODEL), f32) * ((H_X * DH_X) ** -0.5 * DN_BETA),
        "rel_bias": 0.1 * n(ks[17], (N_BUCKETS, H_A), f32),
    }

def second_block(x, mem, ln_g, ln_b, ffn_w_in, ffn_w_out, w_mix_in, b_gate, kv_norm_g, w_uk, w_uv,
              conv_w, w_branch, w_mix_out, xa_wq, xa_wkv, xa_wo, rel_bias):
    for l in range(DEPTH):
        x = layer_norm_2(DN_ALPHA * x + 0.5 * swiglu_ffn(x, ffn_w_in[l, 0], ffn_w_out[l, 0]),
                       ln_g[l, 0], ln_b[l, 0])
        x = layer_norm_2(DN_ALPHA * x + mixer_sublayer(x, w_mix_in[l], b_gate[l], kv_norm_g[l], w_uk[l],
                                                     w_uv[l], conv_w[l], w_branch[l], w_mix_out[l],
                                                     rel_bias),
                       ln_g[l, 1], ln_b[l, 1])
        x = layer_norm_2(DN_ALPHA * x + memory_cross_attention_2(x, mem, xa_wq[l], xa_wkv[l], xa_wo[l]),
                       ln_g[l, 2], ln_b[l, 2])
        x = layer_norm_2(DN_ALPHA * x + 0.5 * swiglu_ffn(x, ffn_w_in[l, 1], ffn_w_out[l, 1]),
                       ln_g[l, 3], ln_b[l, 3])
    return x


def setup_inputs(seed=0):
    out = dict(first_inputs(seed))
    for name, value in second_inputs(seed + 1).items():
        if name != "x":
            out[name + "_2"] = value
    return out


def reference(
    x, mem, even_w_in, even_gate_b, even_conv_w, even_rpb, even_w_out, odd_w_in, odd_lambda,
    odd_subln_g, odd_w_out, mem_wq, mem_wkv, mem_wo, ffn_w_gu, ffn_w_down, ln_g, ln_b, mem_2,
    ln_g_2, ln_b_2, ffn_w_in_2, ffn_w_out_2, w_mix_in_2, b_gate_2, kv_norm_g_2, w_uk_2, w_uv_2,
    conv_w_2, w_branch_2, w_mix_out_2, xa_wq_2, xa_wkv_2, xa_wo_2, rel_bias_2,
):
    x = first_block(
        x, mem, even_w_in, even_gate_b, even_conv_w, even_rpb, even_w_out, odd_w_in, odd_lambda,
        odd_subln_g, odd_w_out, mem_wq, mem_wkv, mem_wo, ffn_w_gu, ffn_w_down, ln_g, ln_b,
    )
    return second_block(
        x, mem_2, ln_g_2, ln_b_2, ffn_w_in_2, ffn_w_out_2, w_mix_in_2, b_gate_2, kv_norm_g_2,
        w_uk_2, w_uv_2, conv_w_2, w_branch_2, w_mix_out_2, xa_wq_2, xa_wkv_2, xa_wo_2,
        rel_bias_2,
    )


_drawn_inputs = setup_inputs


def setup_inputs(seed=0):
    import zlib

    import numpy as np

    out = dict(_drawn_inputs(seed))
    spreads = {}
    factors = {'even_rpb': 8.0,
     'odd_lambda': 6.864,
     'odd_subln_g': 7.336,
     'b_gate_2': 8.0,
     'kv_norm_g_2': 8.0,
     'rel_bias_2': 8.0}
    for name, (base, spread) in spreads.items():
        noise = np.random.default_rng([zlib.crc32(name.encode()), seed]).standard_normal(out[name].shape)
        drawn = base * np.exp(spread * noise) if base else spread * noise
        out[name] = __import__('jax').numpy.asarray(drawn.astype(out[name].dtype))
    for name, factor in factors.items():
        out[name] = (out[name] * factor).astype(out[name].dtype)
    return out
```

```python
from contextlib import ExitStack

import numpy as np

import concourse.bass as bass
from concourse import mybir

F32 = mybir.dt.float32
F32R = mybir.dt.float32r
ALU = mybir.AluOpType
ACT = mybir.ActivationFunctionType
AX = mybir.AxisListType.X

P = 128
D = 1024
KC = D // P
S = 256
TB = S // P
TILE = 2048
RAW, PARTS = 3, 3
FFN = 2816
HC = FFN // P
ALPHA = 4.0 ** 0.25
EPS = 1e-5
NEG = -1e30
LAM_INIT = 0.8 - 0.6 * float(np.exp(-0.3))
TOPK = 64
FOUND = -3e38
BUCKETS = 32

ROWS = {"even_conv_w": 0, "b_gate_2": 40, "conv_w_2": 88, "kv_norm_g_2": 112, "odd_subln_g": 114}
N_ROWS = 115

CONST = {}
CONST_W = 0
for _name, _w in (("ident", 128), ("tri_le", 128), ("tri_ge", 128), ("na_mask", 256), ("causal_le", 128),
                  ("causal_ge", 128), ("rot", 128), ("cos", 256), ("sin", 256), ("topk_causal", 512),
                  ("strict", 512), ("strict_neg", 512), ("bucket", 512)):
    CONST[_name] = (CONST_W, _w)
    CONST_W += _w


def shape_constants():
    c = {}
    i = np.arange(P)
    c["ident"] = np.eye(P)
    c["tri_le"] = (i[:, None] <= i[None, :])
    c["tri_ge"] = (i[:, None] >= i[None, :])
    qc, kc = (i % 64)[:, None], (np.arange(S) % 64)[None, :]
    start = np.clip(qc - 8, 0, 48)
    c["na_mask"] = np.where((kc >= start) & (kc < start + 16), 0.0, NEG)
    c["causal_le"] = np.where(i[None, :] <= i[:, None], 0.0, NEG)
    c["causal_ge"] = np.where(i[None, :] >= i[:, None], 0.0, NEG)
    rot = np.zeros((P, P))
    for m in range(P):
        if m % 64 < 32:
            rot[m + 32, m] = -1.0
        else:
            rot[m - 32, m] = 1.0
    c["rot"] = rot
    inv = np.float32(10000.0) ** (-np.arange(0, 64, 2, dtype=np.float32) / np.float32(64))
    ang = np.arange(S, dtype=np.float32)[None, :] * inv.astype(np.float32)[:, None]
    c["cos"] = np.tile(np.cos(ang), (4, 1))
    c["sin"] = np.tile(np.sin(ang), (4, 1))
    t = (np.arange(TB)[None, :, None] * P + i[:, None, None])
    c["topk_causal"] = np.where(np.arange(S)[None, None, :] <= t, 0.0, NEG).reshape(P, 512)
    s = (np.arange(TB)[None, :, None] * P + i[:, None, None])
    strict = s < np.arange(S)[None, None, :]
    c["strict"] = strict.reshape(P, 512)
    c["strict_neg"] = np.where(strict, 0.0, NEG).reshape(P, 512)
    n = np.maximum(255 - np.arange(512), 0)
    nf = np.maximum(n, 1).astype(np.float32)
    large = 16 + (np.log(nf / np.float32(16)) / np.float32(np.log(8.0)) * 16).astype(np.int32)
    bucket = np.where(n < 16, n, np.minimum(large, BUCKETS - 1))
    onehot = np.zeros((P, 512))
    onehot[bucket, np.arange(512)] = 1.0
    c["bucket"] = onehot
    return np.concatenate([np.asarray(c[k], np.float32) for k in CONST], axis=1)


def program(nc, ctx, A, out, LAST=14):
    def sb(name, shape, dt=F32, on=None):
        return (on or ctx).enter_context(nc.sbuf_tensor(name, shape, dt))

    def sem(name):
        return ctx.enter_context(nc.semaphore(name))

    x = sb("x", [P, TB, D])
    z = sb("z", [P, TB, D])
    xh = sb("xh", [P, KC, S], F32R)
    xl = sb("xl", [P, KC, S], F32R)
    st = ExitStack()
    btab = sb("btab", [P, 8, 512], F32, st)
    st.close()
    st = ExitStack()
    gs = sb("gs", [P, 8, 512], F32, st)
    st.close()
    oh = sb("oh", [P, KC, S], F32R)
    ol = sb("ol", [P, KC, S], F32R)
    raw = sb("raw", [P, RAW, TILE])
    wh = sb("wh", [P, PARTS, TILE], F32R)
    wl = sb("wl", [P, PARTS, TILE], F32R)
    gb = sb("gb", [P, 2, D])
    ident = sb("ident", [P, P])
    ones = sb("ones", [P, P])
    prob = sb("prob", [P, 2, 512])
    probT = sb("probT", [P, 2, 512])
    logit = sb("logit", [P, 2, 512])
    pc = sb("pc", [P, P])
    stat = sb("stat", [P, TB, 4, 6])
    mv = sb("mv", [P, TB, 4])
    bm = sb("bm", [P, 2, 512])
    nmax = sb("nmax", [P, 2, 4])
    psum_e = sb("psum_e", [P, 2, 4])
    rden = sb("rden", [P, 2, 4])

    st = ExitStack()
    hh = sb("hh", [P, HC, S], F32R, st)
    hl = sb("hl", [P, HC, S], F32R, st)
    gate_s = sb("gate_s", [P, 2, 512], F32, st)
    hid = sb("hid", [P, 2, 512], F32, st)
    st.close()
    st = ExitStack()
    mh = sb("mh", [P, KC, S], F32R, st)
    ml = sb("ml", [P, KC, S], F32R, st)
    mem_n = sb("mem_n", [P, TB, D], F32, st)
    xq = sb("xq", [P, KC, S], F32, st)
    xk = sb("xk", [P, KC, S], F32, st)
    xv = sb("xv", [P, TB, D], F32, st)
    st.close()
    st = ExitStack()
    ec = sb("ec", [P, 768], F32, st)
    qkT = sb("qkT", [P, KC, S], F32, st)
    cpad = sb("cpad", [P, KC, S + 4], F32, st)
    av = sb("av", [P, TB, 4, 130], F32, st)
    ao = sb("ao", [P, 4, S], F32, st)
    bq = sb("bq", [P, 4, S], F32, st)
    bk = sb("bk", [P, 4, S], F32, st)
    bv = sb("bv", [P, TB, 512], F32, st)
    pk = sb("pk", [P, 2, 4, P], F32, st)
    cn = sb("cn", [P, 2, 4, 130], F32, st)
    gt = sb("gt", [P, 2, 16], F32, st)
    gbias = sb("gbias", [P, 16], F32, st)
    lf = sb("lf", [P, 4, TB, 8], F32, st)
    bs = sb("bs", [P, 32], F32, st)
    cc_ = sb("cc_", [P, TB, 8], F32, st)
    mm_ = sb("mm_", [P, 10, 2, 2, 4], F32, st)
    prow = sb("prow", [P, P], F32, st)
    boneh = sb("boneh", [P, 512], F32, st)
    brel0 = sb("brel0", [BUCKETS, 8], F32, st)
    rpad = sb("rpad", [64, 2, 7, P], F32, st)
    st.close()
    st = ExitStack()
    pad_a = sb("pad_a", [P, 768 + KC * S], F32, st)
    cm = sb("cm", [P, 2, 2, 4, P], F32, st)
    st.close()
    st = ExitStack()
    oc = sb("oc", [P, 640], F32, st)
    rq = sb("rq", [P, 16, S], F32, st)
    rt = sb("rt", [P, 3, 512], F32, st)
    rs = sb("rs", [P, 2, 512], F32, st)
    dv = sb("dv", [P, TB, D], F32, st)
    lamt = sb("lamt", [P, 4, 64], F32, st)
    lam = sb("lam", [P, 8], F32, st)
    on = sb("on", [P, 8, TB, P], F32, st)
    osq = sb("osq", [P, 2, TB * P], F32, st)
    oss = sb("oss", [P, 3, 8 * TB], F32, st)
    st.close()
    st = ExitStack()
    sc_ = sb("sc_", [P, 1536], F32, st)
    tge = sb("tge", [P, P], F32, st)
    qaT = sb("qaT", [P, 4, S], F32, st)
    iqT = sb("iqT", [P, 4, S], F32, st)
    ikT = sb("ikT", [P, S], F32, st)
    ckn = sb("ckn", [P, TB, P], F32, st)
    ckT = sb("ckT", [P, S], F32, st)
    iw = sb("iw", [P, TB, 8], F32, st)
    uk = sb("uk", [P, 4, P], F32, st)
    uv = sb("uv", [P, 8, 64], F32, st)
    ql = sb("ql", [P, 2, S], F32, st)
    vs = sb("vs", [P, TB, 512], F32, st)
    top8 = sb("top8", [P, 8], F32, st)
    selm = sb("selm", [P, TB, S], F32, st)
    zc = sb("zc", [P, 2, S + 2], F32, st)
    gth = sb("gth", [P, 2, 384], F32, st)
    olat = sb("olat", [P, 2, S], F32, st)
    yh = sb("yh", [P, 12, S], F32R, st)
    yl = sb("yl", [P, 12, S], F32R, st)
    cks = sb("cks", [P, 4], F32, st)
    st.close()
    score = bm[:, 0, :].rearrange("p (t s) -> p t s", t=TB)
    cksq = bm[:, 1, 0:2 * P].rearrange("p (t c) -> p t c", t=TB)
    qsT = z[:, 0, :].rearrange("p (c s) -> p c s", c=4)
    ksT = z[:, 1, :].rearrange("p (c s) -> p c s", c=4)
    smT = z[:, :, :].rearrange("p a (b h l) -> p a b h l", b=2, h=4)

    rpb_d = nc.dram_tensor("rpb_rows", [64, 8 * 7 * P], F32, kind="Internal").ap()
    bias_d = nc.dram_tensor("bias_rows", [P, 8 * 512], F32, kind="Internal").ap()

    ps = [ctx.enter_context(nc.psum_tensor(f"bank{b}", [P, 512], F32)) for b in range(8)]
    bank_full = [sem(f"bank_full{b}") for b in range(8)]
    bank_free = [sem(f"bank_free{b}") for b in range(8)]
    raw_full = [sem(f"raw_full{r}") for r in range(RAW)]
    out_stored = sem("out_stored")
    named = {}

    def sig(name):
        if name not in named:
            named[name] = sem(name)
        return named[name]

    weight_tiles = []
    where = {}
    uses = [0] * 8
    given = [0] * 8
    turn = {"acc": 0, "work": 0}
    halves = {}

    def result(name):
        b, n, _, _ = where[name]
        return ps[b], b, n

    SUB = []
    for layer in range(2):
        for kind in (("even", "odd")[layer], "cross", "ffn"):
            SUB.append((kind, 1, layer, 0))
    for layer in range(2):
        for kind, which in (("ffn", 0), ("merge", 0), ("cross", 0), ("ffn", 1)):
            SUB.append((kind, 2, layer, which))

    STICK_GATES = {6: 0, 8: 1}
    LATENT_GATES = {-1: 2, 1: 3, 2: 4, 4: 5, 5: 6, 7: 7}

    def open_gate(k):
        return gs[:, k // 2 + 4 * (k % 2), :] if k < 8 else prob[:, k % 2, :]

    def ffn_weights(block_no, layer, which):
        if block_no == 1:
            return A["ffn_w_gu"][layer], A["ffn_w_down"][layer]
        return A["ffn_w_in_2"][layer, which], A["ffn_w_out_2"][layer, which]

    def norm_of(j):
        kind, blk, layer, which = SUB[j]
        if blk == 1:
            return A["ln_g"][layer, j % 3], A["ln_b"][layer, j % 3], 1.0
        n = (j - 6) % 4
        return A["ln_g_2"][layer, n], A["ln_b_2"][layer, n], 0.5 if kind == "ffn" else 1.0

    def cross_of(blk, layer):
        if blk == 1:
            return A["mem"][0], A["mem_wq"][layer], A["mem_wkv"][layer], A["mem_wo"][layer], 2
        return A["mem_2"][0], A["xa_wq_2"][layer], A["xa_wkv_2"][layer], A["xa_wo_2"][layer], 1

    def cross_after(j):
        return j + 1 < LAST and SUB[j + 1][0] == "cross"

    half_names, copies, in_banks, mem_start = [], [], [], {}

    def await_halves(eng, n):
        eng.wait_ge(sig("part_high"), n)
        b, _, _, freed = where[half_names[n - 1]] if in_banks[n - 1] else (None,) * 4
        if in_banks[n - 1]:
            eng.wait_ge(bank_free[b], freed)
        else:
            eng.wait_ge(sig("part_low"), copies[n - 1])

    block = ctx.enter_context(nc.Block())

    @block.tensor
    def _(pe):
        owed = [0]

        def mm(o, a, b, start, stop, full=None, transpose=False):
            ins = pe.transpose(o, a, b) if transpose else pe.matmul(o, a, b, start=start, stop=stop)
            if full is not None:
                bank = where[full][0]
                where[full][2] = len(weight_tiles) - 1
                ins.then_inc(bank_full[bank], 1)
            elif owed[0]:
                ins.then_inc(sig("weights_used"), owed[0])
                owed[0] = 0

        def take(name, ring="work", frees=1):
            b = turn[ring] % 4 + (4 if ring == "work" else 0)
            turn[ring] += 1
            if given[b]:
                pe.wait_ge(bank_free[b], given[b])
            given[b] += frees
            uses[b] += 1
            assert name not in where, name
            where[name] = [b, uses[b], 0, given[b]]
            return ps[b]

        def await_read(*names):
            for name in names:
                pe.wait_ge(bank_free[where[name][0]], where[name][3])

        def weights(pieces, nk):
            n = len(weight_tiles)
            w = sum(piece.shape[-1] for piece in pieces)
            weight_tiles.append((pieces, nk, w))
            pe.wait_ge(sig("w_high"), n + 1)
            pe.wait_ge(sig("w_low"), n + 1)
            s = n % PARTS
            return (wh[:, s, 0:nk * w].rearrange("p (k c) -> p k c", k=nk),
                    wl[:, s, 0:nk * w].rearrange("p (k c) -> p k c", k=nk))

        def three(o, ah, al, bh, bl, first, last, full=None):
            mm(o, ah, bl, first, False)
            mm(o, al, bh, False, False)
            mm(o, ah, bh, False, last, full)

        def parts(name, in_bank=True):
            halves[name] = len(halves)
            half_names.append(name)
            copies.append((copies[-1] if copies else 0) + (not in_bank))
            in_banks.append(in_bank)

        def await_parts(n=None):
            await_halves(pe, len(halves) if n is None else n)

        def proj_T(name, pieces, nk, sh, sl, k0=0, ring="work", frees=1):
            h, l = weights(pieces, nk)
            o = take(name, ring, frees)
            for m in range(2):
                for k in range(nk):
                    c = slice(m * P, m * P + P)
                    three(o[:, m * S:m * S + S], h[:, k, c], l[:, k, c], sh[:, k0 + k, :], sl[:, k0 + k, :],
                          k == 0, k == nk - 1, name if m == 1 and k == nk - 1 else None)
            owed[0] += 1

        def proj_N(names, W, c0, width, k_total, sh, sl, ring="work", frees=1, need=None):
            o = [take(name, ring, frees) for name in names]
            per = min(TILE // width, k_total)
            for k0 in range(0, k_total, per):
                nk = min(per, k_total - k0)
                if need:
                    need(k0 + nk)
                h, l = weights([W[k0 * P:(k0 + nk) * P, c0:c0 + width]], nk)
                for t in range(TB):
                    for k in range(nk):
                        tok = slice(t * P, t * P + P)
                        last = k0 + k == k_total - 1
                        three(o[t][:, 0:width], sh[:, k0 + k, tok], sl[:, k0 + k, tok], h[:, k, :], l[:, k, :],
                              k0 + k == 0, last, names[t] if last else None)
                owed[0] += 1

        def to_T(name, src, ring="work"):
            o = take(name, ring)
            for c in range(4):
                mm(o[:, c * P:c * P + P], src[:, c * P:c * P + P], ident[:, :], True, True,
                   name if c == 3 else None, transpose=True)

        def x_to_T(i):
            for t in range(TB):
                if i == 0:
                    pe.wait_ge(sig("x_loaded"), 16)
                for half in range(2):
                    if i:
                        pe.wait_ge(sig("x_ready"), 4 * (i - 1) + 2 * t + half + 1)
                    to_T(("xT", i, t, half), x[:, t, half * 512:half * 512 + 512])
                    parts(("xT", i, t, half))

        def mem_to_T(j):
            mem_no[0] += 1
            pe.wait_ge(sig("mem_loaded"), 16 * mem_no[0])
            for t in range(TB):
                for half in range(2):
                    to_T(("memT", j, t, half), mem_n[:, t, half * 512:half * 512 + 512])
                    parts(("memT", j, t, half))

        def out_proj(j, W, kc, sh, sl, need=None):
            for half in range(2):
                proj_N([("y", j, t, half) for t in range(TB)], W, half * 512, 512, kc, sh, sl, "acc", need=need)
                if half == 0 and cross_after(j):
                    mem_start[j + 1] = len(halves)
                    mem_to_T(j + 1)
            if cross_after(j):
                cross_kv(j + 1)

        def gate_tile(l_, k):
            n, i = divmod(k, 3)
            c0 = 4296 + 1024 * i + n * S
            proj_T(("bgate", l_, n, i), [A["w_mix_in_2"][l_][:, c0:c0 + S]], KC, xh, xl)

        def conv_tile(l_, i):
            what, c0 = (("cc", 3272), ("ch", 3784), ("cb", 2760))[i % 3]
            n = i // 3
            proj_T((what, l_, n), [A["w_mix_in_2"][l_][:, c0 + n * S:c0 + n * S + S]], KC, xh, xl)
            if what == "cb":
                parts(("yc", l_, n), in_bank=False)

        def cross_kv(j):
            _, blk, layer, _ = SUB[j]
            _, _, wkv, _, c = cross_of(blk, layer)
            await_parts()
            for n in range(2 * c):
                proj_T(("xk", j, n), [wkv[:, n * S:n * S + S]], KC, mh, ml)
            for half in range(c):
                proj_N([("xv", j, t, half) for t in range(TB)], wkv, 512 * c + half * 512, 512, KC, mh, ml)

        def transposed_probs(u, src):
            pe.wait_ge(sig("prob_ready"), unit[0] + u + 1)
            name = ("T", unit[0] + u)
            o = take(name)
            for kb in range(TB):
                for t in range(TB):
                    mm(o[:, kb * S + t * P:kb * S + t * P + P], src(t, kb), ident[:, :], True, True,
                       name if kb == 1 and t == 1 else None, transpose=True)

        def cross(j):
            _, blk, layer, _ = SUB[j]
            _, wq, _, wo, c = cross_of(blk, layer)
            await_parts()
            for n in range(2 * c):
                proj_T(("xq", j, n), [wq[:, n * S:n * S + S]], KC, xh, xl)
            await_read(*[(what, j, n) for what in ("xk", "xq") for n in range(2 * c)])
            await_read(*[("xv", j, t, half) for t in range(TB) for half in range(c)])
            for t in range(4 + 2):
                if t < 4:
                    o = take(("S", unit[0] + t))
                    for tb in range(TB):
                        for i in range(c):
                            mm(o[:, tb * S:tb * S + S], xq[:, c * t + i, tb * P:tb * P + P], xk[:, c * t + i, :],
                               i == 0, i == c - 1, ("S", unit[0] + t) if tb == 1 and i == c - 1 else None)
                if 1 <= t <= 4:
                    u = t - 1
                    transposed_probs(u, lambda tb, kb: prob[:, u % 2, tb * S + kb * P:tb * S + kb * P + P])
                if t >= 2:
                    u = t - 2
                    await_read(("T", unit[0] + u))
                    o = take(("O", unit[0] + u), "acc")
                    for i in range(c):
                        for kb in range(TB):
                            mm(o[:, i * S:i * S + S], xv[:, kb, (c * u + i) * P:(c * u + i + 1) * P],
                               probT[:, u % 2, kb * S:kb * S + S], kb == 0, kb == 1,
                               ("O", unit[0] + u) if i == c - 1 and kb == 1 else None)
                    parts(("O", unit[0] + u))
            unit[0] += 4
            await_parts()
            out_proj(j, wo, 4 * c, oh, ol)

        def ffn(j):
            _, blk, layer, which = SUB[j]
            wgu, wdown = ffn_weights(blk, layer, which)
            await_parts()
            base = len(halves)
            for q in range(HC // 2):
                proj_T(("gate", j, q), [wgu[:, q * S:q * S + S]], KC, xh, xl)
                proj_T(("up", j, q), [wgu[:, FFN + q * S:FFN + q * S + S]], KC, xh, xl)
                parts(("hid", j, q), in_bank=False)
            out_proj(j, wdown, HC, hh, hl, need=lambda k: await_parts(base + (k + 1) // 2))

        def even(j):
            W = A["even_w_in"][0]
            await_parts()
            h, l = weights([W[:, 2048:2064]], KC)
            o = take("gates")
            for t in range(TB):
                for k in range(KC):
                    tok = slice(t * P, t * P + P)
                    three(o[:, t * 16:t * 16 + 16], xh[:, k, tok], xl[:, k, tok], h[:, k, :], l[:, k, :],
                          k == 0, k == KC - 1, "gates" if t == 1 and k == KC - 1 else None)
            owed[0] += 1
            for n in range(4):
                proj_T(("aqk", n), [W[:, n * S:n * S + S]], KC, xh, xl)
            proj_N([("av", t) for t in range(TB)], W, 1024, 512, KC, xh, xl)
            pe.wait_ge(sig("rel_loaded"), 32)
            for hd in range(8):
                o = take(("tab", hd), "acc")
                mm(o[:, :], brel0[:, hd:hd + 1].broadcast_to([BUCKETS, P]), boneh[0:BUCKETS, :], True, True,
                   ("tab", hd))
            for n in range(2):
                proj_T(("ao", n), [W[:, 1536 + n * S:1536 + n * S + S]], KC, xh, xl)
            for n in range(2):
                proj_T(("bq", n), [W[:, 2064 + n * S:2064 + n * S + S]], KC, xh, xl)
            for n in range(2):
                proj_T(("bk", n), [W[:, 2576 + n * S:2576 + n * S + S]], KC, xh, xl)
            proj_N([("bv", t) for t in range(TB)], W, 3088, 512, KC, xh, xl)

            pe.wait_ge(sig("ones_set"), 1)
            pe.wait_ge(sig("even_loaded"), 32)
            pe.wait_ge(sig("logf_ready"), 1)
            o = take("cum")
            for t in range(TB):
                mm(o[:, t * 8:t * 8 + 4], tri_le, lf[:, 3, t, 0:4], True, True)
                mm(o[:, t * 8 + 4:t * 8 + 8], tri_ge, lf[:, 3, t, 4:8], True, True)
                mm(o[:, 16 + t * 8:24 + t * 8], ones[:, :], lf[:, 3, t, :], True, True, "cum" if t == 1 else None)
            pe.wait_ge(sig("decay_cols"), 1)
            for d in range(2):
                for t in range(TB):
                    o = take(("C", d, t))
                    for hd in range(4):
                        mm(o[:, hd * P:hd * P + P], cc_[:, t, d * 4 + hd:d * 4 + hd + 1].broadcast_to([P, P]),
                           ident[:, :], True, True, ("C", d, t) if hd == 3 else None)
            pe.wait_ge(sig("qk_ready"), 1)
            for t in range(TB):
                o = take(("QK", t), "acc")
                for hd in range(4):
                    mm(o[:, hd * P:hd * P + P], qkT[:, hd, t * P:t * P + P], qkT[:, 4 + hd, t * P:t * P + P],
                       True, True, ("QK", t) if hd == 3 else None)
            for d in range(2):
                o = take(("kN", d))
                for hd in range(4):
                    mm(o[:, hd * P:hd * P + P], qkT[:, 4 + hd, d * P:d * P + P], ident[:, :], True, True,
                       ("kN", d) if hd == 3 else None, transpose=True)
            pe.wait_ge(sig("av_ones"), 1)
            await_read(("av", 0), ("av", 1))
            for d in range(2):
                await_read(("kN", d))
                for half in range(2):
                    o = take(("KV", d, half))
                    for i in range(2):
                        hd = half * 2 + i
                        mm(o[:, i * 130:i * 130 + 130], pk[:, d, hd, :], av[:, d, hd, :], True, True,
                           ("KV", d, half) if i == 1 else None)
            for t in range(TB):
                for d in range(2):
                    pe.wait_ge(sig("decayed"), 2 * t + d + 1)
                    o = take(("ST", d, t))
                    for hd in range(4):
                        mm(o[:, hd * P:hd * P + P], cm[:, d, t, hd, :], ident[:, :], True, True,
                           ("ST", d, t) if hd == 3 else None, transpose=True)
            for d in range(2):
                for half in range(2):
                    await_read(("KV", d, half))
                    o = take(("int", d, half))
                    for i in range(2):
                        hd = half * 2 + i
                        t2 = 1 - d
                        mm(o[:, i * 130:i * 130 + 130], qkT[:, hd, t2 * P:t2 * P + P], cn[:, d, hd, :], True, True,
                           ("int", d, half) if i == 1 else None)
            for t in range(TB):
                for d in range(2):
                    await_read(("ST", d, t))
                    o = take(("num", d, t), "acc")
                    for hd in range(4):
                        mm(o[:, hd * P:hd * P + P], smT[:, d, t, hd, :], av[:, t, hd, 0:P], True, True,
                           ("num", d, t) if hd == 3 else None)
            await_read(("bq", 0), ("bq", 1), ("bk", 0), ("bk", 1), ("bv", 0), ("bv", 1))

            def score(u):
                r = slice(64 * (u % 2), 64 * (u % 2) + 64)
                o = take(("S", unit[0] + u))
                for tb in range(TB):
                    mm(o[:, tb * S:tb * S + S], bq[r, u // 2, tb * P:tb * P + P], bk[r, u // 2, :], True, True,
                       ("S", unit[0] + u) if tb == 1 else None)

            for t in range(TB):
                pe.wait_ge(sig("mlstm_out"), t + 1)
                to_T(("hT", t), logit[:, t, :])
                parts(("aT", t), in_bank=False)
            for t in range(8 + 2):
                if t < 8:
                    score(t)
                if 1 <= t <= 8:
                    u = t - 1
                    transposed_probs(u, lambda tb, kb: prob[:, u % 2, tb * S + kb * P:tb * S + kb * P + P])
                if t >= 2:
                    u = t - 2
                    await_read(("T", unit[0] + u))
                    heads_out(("O", unit[0] + u - u % 2), u, lambda kb: bv[:, kb, u * 64:u * 64 + 64],
                              lambda kb: probT[:, u % 2, kb * S:kb * S + S])
            unit[0] += 8
            await_parts()
            out_proj(j, A["even_w_out"][0], KC, oh, ol)

        def heads_out(name, u, v_of, p_of):
            o = take(name, "acc") if u % 2 == 0 else ps[where[name][0]]
            r = slice(64 * (u % 2), 64 * (u % 2) + 64)
            for kb in range(TB):
                mm(o[r, 0:S], v_of(kb), p_of(kb), kb == 0, kb == 1, name if u % 2 and kb == 1 else None)
            if u % 2:
                parts(name)

        def odd(j):
            W = A["odd_w_in"][0]
            await_parts()
            pe.wait_ge(sig("odd_loaded"), 16)
            for n in range(8 + 1):
                if n < 8:
                    proj_T(("rp", n), [W[:, n * S:n * S + S]], KC, xh, xl)
                if n >= 1:
                    await_read(("rp", n - 1))
                    o = take(("rot", n - 1), "acc")
                    mm(o[:, :], oc[:, 0:P], rs[:, (n - 1) % 2, :], True, True, ("rot", n - 1))
            for half in range(2):
                proj_N([("dv", t, half) for t in range(TB)], W, 2048 + half * 512, 512, KC, xh, xl)
            await_read(*[("dv", t, half) for t in range(TB) for half in range(2)])
            pe.wait_ge(sig("rope_done"), 8)
            for t in range(8 + 2):
                if t < 8:
                    for c in range(2):
                        r = slice(64 * c, 64 * c + 64)
                        o = take(("S", unit[0] + t, c))
                        for tb in range(TB):
                            mm(o[:, tb * S:tb * S + S], rq[r, t, tb * P:tb * P + P], rq[r, 8 + t, :], True, True,
                               ("S", unit[0] + t, c) if tb == 1 else None)
                if 1 <= t <= 8:
                    u = t - 1
                    buf = (prob, logit)[u % 2]
                    transposed_probs(u, lambda tb, kb: buf[:, 0, tb * S + kb * P:tb * S + kb * P + P])
                if t >= 2:
                    u = t - 2
                    await_read(("T", unit[0] + u))
                    o = take(("O", unit[0] + u), "acc")
                    for tb in range(TB):
                        for kb in range(TB):
                            mm(o[:, tb * P:tb * P + P], probT[:, u % 2, kb * S + tb * P:kb * S + tb * P + P],
                               dv[:, kb, u * P:u * P + P], kb == 0, kb == 1,
                               ("O", unit[0] + u) if tb == 1 and kb == 1 else None)
            for u in range(8):
                pe.wait_ge(sig("diff_normed"), u + 1)
                o = take(("OT", u))
                for tb in range(TB):
                    mm(o[:, tb * P:tb * P + P], on[:, u, tb, :], ident[:, :], True, True,
                       ("OT", u) if tb == 1 else None, transpose=True)
                parts(("OT", u), in_bank=False)
            unit[0] += 8
            await_parts()
            out_proj(j, A["odd_w_out"][0], KC, oh, ol)

        def merge(j):
            _, _, l_, _ = SUB[j]
            W = A["w_mix_in_2"][l_]
            await_parts()
            proj_N([("ckv", l_, t) for t in range(TB)], W, 512, P, KC, xh, xl)
            h, l = weights([W[:, 1152:1216], W[:, 1152:1216], W[:, 1216:1224]], KC)
            o = take(("ik", l_))
            for k in range(KC):
                three(o[:, 0:S], h[:, k, 0:P], l[:, k, 0:P], xh[:, k, :], xl[:, k, :], k == 0, k == KC - 1,
                      ("ik", l_) if k == KC - 1 else None)
            o = take(("iw", l_))
            for t in range(TB):
                for k in range(KC):
                    tok = slice(t * P, t * P + P)
                    three(o[:, t * 8:t * 8 + 8], xh[:, k, tok], xl[:, k, tok], h[:, k, P:P + 8], l[:, k, P:P + 8],
                          k == 0, k == KC - 1, ("iw", l_) if t == 1 and k == KC - 1 else None)
            owed[0] += 1
            for n in range(2):
                proj_T(("iq", l_, n), [W[:, 640 + n * S:640 + n * S + S]], KC, xh, xl)
            pe.wait_ge(sig("ckv_normed"), 2 * (l_ + 1))
            o = take(("ckT", l_))
            for t in range(TB):
                mm(o[:, t * P:t * P + P], ckn[:, t, :], ident[:, :], True, True, ("ckT", l_) if t == 1 else None,
                   transpose=True)
            await_read(("ik", l_), ("iq", l_, 0), ("iq", l_, 1))
            for u in range(8):
                r = slice(64 * (u % 2), 64 * (u % 2) + 64)
                o = take(("dot", l_, u))
                for tb in range(TB):
                    mm(o[:, tb * S:tb * S + S], iqT[r, u // 2, tb * P:tb * P + P], ikT[r, :], True, True,
                       ("dot", l_, u) if tb == 1 else None)
            for n in range(2):
                proj_T(("qa", l_, n), [W[:, n * S:n * S + S]], KC, xh, xl)
            for n in range(2):
                proj_T(("qs", l_, n), [W[:, 1224 + n * S:1224 + n * S + S]], KC, xh, xl)
            for n in range(2):
                proj_T(("ks", l_, n), [W[:, 1736 + n * S:1736 + n * S + S]], KC, xh, xl)
            proj_N([("vs", l_, t) for t in range(TB)], W, 2248, 512, KC, xh, xl)
            await_read(*[(what, l_, n) for what in ("qs", "ks", "vs") for n in range(2)])
            pe.wait_ge(sig("merge_loaded"), 32 * (l_ + 1))
            for t in range(8 + 2):
                if t < 8:
                    r = slice(64 * (t % 2), 64 * (t % 2) + 64)
                    o = take(("z", l_, t))
                    for kb in range(TB):
                        mm(o[:, kb * S:kb * S + S], ksT[r, t // 2, kb * P:kb * P + P], qsT[r, t // 2, :], True, True,
                           ("z", l_, t) if kb == 1 else None)
                if 1 <= t <= 8:
                    u = t - 1
                    pe.wait_ge(sig("softplus_masked"), 8 * l_ + u + 1)
                    o = take(("later", l_, u))
                    sp = prob[:, u % 2, :]
                    mm(o[:, 0:S], tge[:, :], sp[:, 0:S], True, False)
                    mm(o[:, 0:S], ones[:, :], sp[:, S:2 * S], False, True)
                    mm(o[:, S:2 * S], tge[:, :], sp[:, S:2 * S], True, True, ("later", l_, u))
                if t >= 2:
                    u = t - 2
                    pe.wait_ge(sig("stick_probs"), 8 * l_ + u + 1)
                    heads_out(("yb", l_, u // 2), u, lambda kb: vs[:, kb, u * 64:u * 64 + 64],
                              lambda kb: probT[:, u % 2, kb * S:kb * S + S])
                if t < 6:
                    conv_tile(l_, t)
                elif t in STICK_GATES:
                    gate_tile(l_, STICK_GATES[t])
            await_read(("qa", l_, 0), ("qa", l_, 1), ("ckT", l_))
            pe.wait_ge(sig("latent_weights"), 32 * (l_ + 1))
            pe.wait_ge(sig("merge_loaded"), 32 * (l_ + 1))
            for t in range(-1, 8 + 3):
                if t + 1 < 8:
                    u = t + 1
                    r = slice(64 * (u % 2), 64 * (u % 2) + 64)
                    o = take(("ql", l_, u))
                    mm(o[:, 0:S], uk[r, u // 2, :], qaT[r, u // 2, :], True, True, ("ql", l_, u))
                if 0 <= t < 8:
                    await_read(("ql", l_, t))
                    o = take(("S", unit[0] + t))
                    for tb in range(TB):
                        mm(o[:, tb * S:tb * S + S], ql[:, t % 2, tb * P:tb * P + P], ckT[:, :], True, True,
                           ("S", unit[0] + t) if tb == 1 else None)
                if 1 <= t <= 8:
                    u = t - 1
                    transposed_probs(u, lambda tb, kb: prob[:, u % 2, tb * S + kb * P:tb * S + kb * P + P])
                if 2 <= t <= 9:
                    u = t - 2
                    await_read(("T", unit[0] + u))
                    o = take(("lat", l_, u), "acc")
                    for kb in range(TB):
                        mm(o[:, 0:S], ckn[:, kb, :], probT[:, u % 2, kb * S:kb * S + S], kb == 0, kb == 1,
                           ("lat", l_, u) if kb == 1 else None)
                if t >= 3:
                    u = t - 3
                    await_read(("lat", l_, u))
                    name = ("ya", l_, u // 2)
                    o = take(name, "acc") if u % 2 == 0 else ps[where[name][0]]
                    mm(o[64 * (u % 2):64 * (u % 2) + 64, 0:S], uv[:, u, :], olat[:, u % 2, :], True, True,
                       name if u % 2 else None)
                    if u % 2:
                        parts(name)
                if t in LATENT_GATES:
                    gate_tile(l_, LATENT_GATES[t])
            unit[0] += 8
            await_parts()
            for n in range(4):
                for i in range(3):
                    if 3 * n + i >= 8:
                        gate_tile(l_, 3 * n + i)
                    proj_T(("branch", l_, n, i), [A["w_branch_2"][l_, i][:, n * S:n * S + S]], 4, yh, yl, k0=4 * i)
                parts(("merged", l_, n), in_bank=False)
            await_parts()
            out_proj(j, A["w_mix_out_2"][l_], KC, oh, ol)

        unit = [0]
        mem_no = [0]
        tri_le, tri_ge = ec[:, 0:P], ec[:, P:2 * P]

        pe.wait_ge(sig("ident_loaded"), 16)
        x_to_T(0)
        pe.wait_ge(sig("rows_loaded"), 16 * 5)
        o = take("cols")
        mm(o[:, 0:N_ROWS], prow[0:N_ROWS, :], ident[0:N_ROWS, 0:N_ROWS], True, True, "cols", transpose=True)
        program_of = {"even": even, "odd": odd, "merge": merge, "cross": cross, "ffn": ffn}
        for j, (kind, _, _, _) in enumerate(SUB[:LAST]):
            program_of[kind](j)
            if j + 1 < LAST:
                x_to_T(j + 1)

    raw_done = []
    for n, (pieces, _, _) in enumerate(weight_tiles):
        raw_done.append(16 * len(pieces) + (raw_done[n - RAW] if n >= RAW else 0))

    def raw_tile(n):
        _, nk, w = weight_tiles[n]
        return raw[:, n % RAW, 0:nk * w]

    @block.scalar
    def _(act):
        tile = [0]
        step = [0]
        high_no = [0]
        unit = [0]

        def split_to(n):
            while tile[0] <= min(n, len(weight_tiles) - 1):
                t = tile[0]
                act.wait_ge(raw_full[t % RAW], raw_done[t])
                if t >= PARTS:
                    act.wait_ge(sig("weights_used"), t - PARTS + 1)
                _, nk, w = weight_tiles[t]
                act.activation(wh[:, t % PARTS, 0:nk * w], raw_tile(t), ACT.Copy).then_inc(sig("w_high"), 1)
                tile[0] += 1

        def ahead(name):
            split_to(where[name][2] + PARTS - 1)

        def get(name):
            b, n, _, _ = where[name]
            ahead(name)
            act.wait_ge(bank_full[b], n)
            return ps[b]

        def await_read(name):
            act.wait_ge(bank_free[where[name][0]], where[name][3])

        def free(name, ins):
            ins.then_inc(bank_free[where[name][0]], 1)

        def link(ins):
            step[0] += 1
            ins.then_inc(sig("act_step"), 1)
            act.wait_ge(sig("act_step"), step[0])

        def high(name, dst, src):
            assert halves[name] == high_no[0], name
            high_no[0] += 1
            act.activation(dst, src, ACT.Copy).then_inc(sig("part_high"), 1)

        def wait(name, n):
            act.wait_ge(sig(name), n)

        def quad(ap):
            return ap.rearrange("p (c s) -> p c s", c=4)

        def two(ap):
            return ap.rearrange("p (c s) -> p c s", c=2)

        def x_to_T(i):
            for t in range(TB):
                for half in range(2):
                    o = get(("xT", i, t, half))
                    high(("xT", i, t, half), xh[:, half * 4:half * 4 + 4, t * P:t * P + P], quad(o[:, :]))

        def norm(j):
            ahead(("y", j, 1, 1))
            for t in range(TB):
                wait("var_ready", 2 * j + t + 1)
                act.activation(mv[:, t, 2:3], mv[:, t, 1:2], ACT.Sqrt).then_inc(sig("std_ready"), 1)

        def out_proj(j):
            if cross_after(j):
                for t in range(TB):
                    for half in range(2):
                        name = ("memT", j + 1, t, half)
                        high(name, mh[:, half * 4:half * 4 + 4, t * P:t * P + P], quad(get(name)[:, :]))
            norm(j)
            if cross_after(j):
                c = cross_of(SUB[j + 1][1], 0)[4]
                for n in range(2 * c):
                    name = ("xk", j + 1, n)
                    o = get(name)
                    free(name, act.activation(xk[:, 2 * n:2 * n + 2, :], two(o[:, :]), ACT.Copy))

        def exps(g, src, dst, k0=0):
            for tb in range(TB):
                ins = act.activation(dst[:, tb * S:tb * S + S], src[:, tb * S:tb * S + S], ACT.Exp,
                                     bias=nmax[:, g % 2, k0 + tb:k0 + tb + 1],
                                     accum_out=psum_e[:, g % 2, k0 + tb:k0 + tb + 1])
            return ins

        def probs_T(g):
            name = ("T", g)
            o = get(name)
            free(name, act.activation(probT[:, g % 2, :], o[:, :], ACT.Copy))

        def softmax(n_units, biased, after=None):
            for t in range(n_units + 2):
                if t < n_units:
                    g = unit[0] + t
                    if biased:
                        split_to(where[("S", g)][2] + PARTS - 1)
                        src = logit[:, g % 2, :]
                    else:
                        src = get(("S", g))
                    wait("neg_max", g + 1)
                    ins = exps(g, src, prob[:, g % 2, :])
                    if biased:
                        ins.then_inc(sig("exp_done"), 1)
                    else:
                        free(("S", g), ins)
                if 1 <= t <= n_units:
                    probs_T(unit[0] + t - 1)
                if t >= 2 and after:
                    after(t - 2)
            unit[0] += n_units

        def cross(j):
            c = cross_of(SUB[j][1], 0)[4]
            for n in range(2 * c):
                name = ("xq", j, n)
                o = get(name)
                ins = act.activation(xq[:, 2 * n:2 * n + 2, :], two(o[:, :]), ACT.Copy,
                                     scale=float((c * P) ** -0.5))
                free(name, ins)
            base = unit[0]

            def after(u):
                name = ("O", base + u)
                o = get(name)
                high(name, oh[:, c * u:c * u + c, :], o[:, 0:c * S].rearrange("p (c s) -> p c s", c=c))

            softmax(4, False, after)
            out_proj(j)

        def ffn(j):
            for q in range(HC // 2 + 1):
                if q < HC // 2:
                    o = get(("gate", j, q))
                    free(("gate", j, q), act.activation(gate_s[:, q % 2, :], o[:, :], ACT.Silu))
                if q >= 1:
                    ahead(("up", j, q - 1))
                    await_read(("up", j, q - 1))
                    high(("hid", j, q - 1), hh[:, 2 * q - 2:2 * q, :], two(hid[:, (q - 1) % 2, :]))
            out_proj(j)

        def even(j):
            for n in range(4):
                o = get(("aqk", n))
                if n == 0:
                    wait("pads_set", 1)
                free(("aqk", n),
                       act.activation(cpad[:, 2 * n:2 * n + 2, 2:2 + S], two(o[:, :]), ACT.Copy))
            wait("abs_f", 1)
            link(act.activation(lf[:, 1, :, :], lf[:, 0, :, :], ACT.Exp, scale=-1.0))
            act.activation(lf[:, 2, :, :], lf[:, 1, :, :], ACT.Ln, bias=1.0).then_inc(sig("softplus_f"), 1)
            for hd in range(8):
                o = get(("tab", hd))
                free(("tab", hd), act.activation(btab[:, hd, :], o[:, :], ACT.Copy))
            for n in range(2):
                o = get(("ao", n))
                free(("ao", n), act.activation(ao[:, 2 * n:2 * n + 2, :], two(o[:, :]), ACT.Sigmoid))
            for n in range(2):
                o = get(("bq", n))
                free(("bq", n),
                       act.activation(bq[:, 2 * n:2 * n + 2, :], two(o[:, :]), ACT.Copy, scale=0.125))
            for n in range(2):
                o = get(("bk", n))
                free(("bk", n), act.activation(bk[:, 2 * n:2 * n + 2, :], two(o[:, :]), ACT.Copy))
            ahead("cum")
            wait("conv_done", 1)
            act.activation(qkT[:, :, :], qkT[:, :, :], ACT.Silu).then_inc(sig("silu_done"), 1)
            wait("decay_exponents", 1)
            act.activation(mm_[:, 7, :, :, :], mm_[:, 7, :, :, :], ACT.Exp).then_inc(sig("mlstm_small"), 1)
            act.activation(mm_[:, 5, :, :, :], mm_[:, 5, :, :, :], ACT.Exp, scale=-1.0).then_inc(sig("mlstm_small"), 1)
            act.activation(mm_[:, 6, :, :, :], mm_[:, 6, :, :, :], ACT.Exp).then_inc(sig("mlstm_small"), 1)
            for t in range(TB):
                for d in range(2):
                    for hd in range(4):
                        ins = act.activation(cm[:, d, t, hd, :], cm[:, d, t, hd, :], ACT.Exp,
                                             bias=mm_[:, 4, d, t, hd:hd + 1])
                    ins.then_inc(sig("decay_ready"), 1)
            for d in range(2):
                for half in range(2):
                    name = ("KV", d, half)
                    o = get(name)
                    free(name,
                           act.activation(cn[:, d, 2 * half:2 * half + 2, :],
                                          o[:, 0:260].rearrange("p (h e) -> p h e", h=2), ACT.Copy))
            for t in range(TB):
                for d in range(2):
                    name = ("ST", d, t)
                    o = get(name)
                    free(name, act.activation(smT[:, d, t, :, :], quad(o[:, :]), ACT.Copy))
            for t in range(TB):
                await_read(("hT", t))
                wait("distances_stored", 16)
                high(("aT", t), oh[:, 0:4, t * P:t * P + P], quad(probT[:, t, :]))
            base = unit[0]

            def after(u):
                if u % 2:
                    name = ("O", base + u - 1)
                    o = get(name)
                    high(name, oh[:, 4 + u // 2, :], o[:, 0:S])

            softmax(8, True, after)
            out_proj(j)

        def odd(j):
            wait("lam_sums", 1)
            act.activation(lam[:, 2:4], lam[:, 0:2], ACT.Exp).then_inc(sig("lam_exp"), 1)
            for n in range(8):
                o = get(("rp", n))
                if n >= 2:
                    wait("rope_done", n - 1)
                free(("rp", n), act.activation(rs[:, n % 2, :], o[:, :], ACT.Copy,
                                                            scale=0.125 if n < 4 else 1.0))
            for t in range(8 + 1):
                if t < 8:
                    g = unit[0] + t
                    for c in range(2):
                        src = get(("S", g, c))
                        wait("neg_max", g + 1)
                        free(("S", g, c), exps(g, src, (prob, logit)[t % 2][:, c, :], k0=2 * c))
                if t >= 1:
                    probs_T(unit[0] + t - 1)
            wait("diff_var", 1)
            act.activation(oss[:, 1, :], oss[:, 0, :], ACT.Sqrt).then_inc(sig("diff_std"), 1)
            for u in range(8):
                await_read(("OT", u))
                high(("OT", u), oh[:, u, :], osq[:, u % 2, :])
            unit[0] += 8
            out_proj(j)

        def gate_tile(l_, k):
            n, i = divmod(k, 3)
            name = ("bgate", l_, n, i)
            o = get(name)
            if k >= 10:
                await_read(("branch", l_, (k - 2) // 3, (k - 2) % 3))
            for m in range(2):
                r = ROWS["b_gate_2"] + (l_ * 3 + i) * 8 + 2 * n + m
                ins = act.activation(open_gate(k)[:, m * S:m * S + S], o[:, m * S:m * S + S], ACT.Sigmoid,
                                     bias=pc[:, r:r + 1])
            free(name, ins)

        def conv_tile(l_, i):
            n = i // 3
            if i % 3 == 0:
                o = get(("cc", l_, n))
                if n:
                    wait("part_low", copies[halves[("yc", l_, 0)]])
                free(("cc", l_, n), act.activation(bm[:, 1, :], o[:, :], ACT.Copy))
            elif i % 3 == 2:
                get(("cb", l_, n))
                await_read(("cb", l_, n))
                high(("yc", l_, n), yh[:, 8 + 2 * n:10 + 2 * n, :], two(bm[:, 1, :]))

        def merge(j):
            l_ = SUB[j][2]
            ahead(("ckv", l_, 1))
            wait("ckv_var", l_ + 1)
            act.activation(cks[:, 2:4], cks[:, 0:2], ACT.Sqrt).then_inc(sig("ckv_std"), 1)
            o = get(("ik", l_))
            free(("ik", l_), act.activation(ikT[:, :], o[:, 0:S], ACT.Copy))
            for n in range(2):
                o = get(("iq", l_, n))
                free(("iq", l_, n),
                       act.activation(iqT[:, 2 * n:2 * n + 2, :], two(o[:, :]), ACT.Copy))
            for u in range(8):
                o = get(("dot", l_, u))
                if u >= 2:
                    wait("scored", 8 * l_ + u - 1)
                free(("dot", l_, u), act.activation(prob[:, u % 2, :], o[:, :], ACT.Relu))
            for n in range(2):
                o = get(("qa", l_, n))
                free(("qa", l_, n),
                       act.activation(qaT[:, 2 * n:2 * n + 2, :], two(o[:, :]), ACT.Copy, scale=0.125))
            for n in range(2):
                o = get(("qs", l_, n))
                free(("qs", l_, n),
                       act.activation(qsT[:, 2 * n:2 * n + 2, :], two(o[:, :]), ACT.Copy, scale=0.125))
            for n in range(2):
                o = get(("ks", l_, n))
                free(("ks", l_, n),
                       act.activation(ksT[:, 2 * n:2 * n + 2, :], two(o[:, :]), ACT.Copy))
            for t in range(8 + 2):
                if t < 8:
                    o = get(("z", l_, t))
                    if t >= 2:
                        wait("stick_probs", 8 * l_ + t - 1)
                    link(act.activation(logit[:, t % 2, :], o[:, :], ACT.Abs))
                    link(act.activation(logit[:, t % 2, :], logit[:, t % 2, :], ACT.Exp, scale=-1.0))
                    act.activation(logit[:, t % 2, :], logit[:, t % 2, :], ACT.Ln, bias=1.0)\
                       .then_inc(sig("log1p_ready"), 1)
                if 1 <= t <= 8:
                    u = t - 1
                    await_read(("later", l_, u))
                    act.activation(probT[:, u % 2, :], logit[:, u % 2, :], ACT.Exp).then_inc(sig("stick_probs"), 1)
                if t >= 3 and t % 2:
                    name = ("yb", l_, (t - 3) // 2)
                    o = get(name)
                    high(name, yh[:, 4 + (t - 3) // 2, :], o[:, 0:S])
                if t < 6:
                    conv_tile(l_, t)
                elif t in STICK_GATES:
                    gate_tile(l_, STICK_GATES[t])
            for t in range(-1, 8 + 3):
                if t + 1 < 8:
                    o = get(("ql", l_, t + 1))
                    free(("ql", l_, t + 1),
                           act.activation(ql[:, (t + 1) % 2, :], o[:, 0:S], ACT.Copy))
                if 0 <= t < 8:
                    g = unit[0] + t
                    wait("neg_max", g + 1)
                    exps(g, logit[:, g % 2, :], prob[:, g % 2, :]).then_inc(sig("exp_done"), 1)
                if 1 <= t <= 8:
                    probs_T(unit[0] + t - 1)
                if t >= 4 and t % 2 == 0:
                    name = ("ya", l_, (t - 4) // 2)
                    o = get(name)
                    high(name, yh[:, (t - 4) // 2, :], o[:, 0:S])
                if t in LATENT_GATES:
                    gate_tile(l_, LATENT_GATES[t])
            unit[0] += 8
            for n in range(4):
                for i in range(3):
                    if 3 * n + i >= 8:
                        gate_tile(l_, 3 * n + i)
                ahead(("branch", l_, n, 2))
                wait("merged_ready", 4 * l_ + n + 1)
                high(("merged", l_, n), oh[:, 2 * n:2 * n + 2, :], two(logit[:, n % 2, :]))
            out_proj(j)

        split_to(1)
        x_to_T(0)
        program_of = {"even": even, "odd": odd, "merge": merge, "cross": cross, "ffn": ffn}
        for j, (kind, _, _, _) in enumerate(SUB[:LAST]):
            program_of[kind](j)
            if j + 1 < LAST:
                x_to_T(j + 1)

    @block.vector
    def _(dve):
        tile = [0]
        step = [0]
        low_no = [0]
        unit = [0]
        biased_no = [0]

        def split_to(n):
            while tile[0] <= min(n, len(weight_tiles) - 1):
                t = tile[0]
                dve.wait_ge(raw_full[t % RAW], raw_done[t])
                dve.wait_ge(sig("w_high"), t + 1)
                if t >= PARTS:
                    dve.wait_ge(sig("weights_used"), t - PARTS + 1)
                _, nk, w = weight_tiles[t]
                dve.tensor_tensor(wl[:, t % PARTS, 0:nk * w], raw_tile(t),
                                  wh[:, t % PARTS, 0:nk * w].bitcast(F32), ALU.subtract)\
                   .then_inc(sig("w_low"), 1)
                tile[0] += 1

        def ahead(name):
            split_to(where[name][2] + PARTS - 1)

        def get(name):
            b, n, _, _ = where[name]
            ahead(name)
            dve.wait_ge(bank_full[b], n)
            return ps[b]

        def free(name, ins):
            ins.then_inc(bank_free[where[name][0]], 1)

        def await_read(name):
            dve.wait_ge(bank_free[where[name][0]], where[name][3])

        def wait(name, n):
            dve.wait_ge(sig(name), n)

        def link(ins):
            step[0] += 1
            ins.then_inc(sig("dve_step"), 1)
            dve.wait_ge(sig("dve_step"), step[0])

        def low(name, dst, src, hi, from_bank=True):
            assert halves[name] == low_no[0], name
            low_no[0] += 1
            wait("part_high", low_no[0])
            assert in_banks[low_no[0] - 1] == from_bank, name
            ins = dve.tensor_tensor(dst, src, hi.bitcast(F32), ALU.subtract)
            if from_bank:
                free(name, ins)
            else:
                ins.then_inc(sig("part_low"), 1)

        def copy_used(name):
            wait("part_low", copies[halves[name]])

        def quad(ap):
            return ap.rearrange("p (c s) -> p c s", c=4)

        def two(ap):
            return ap.rearrange("p (c s) -> p c s", c=2)

        def along(v, n):
            return v.unsqueeze(2).broadcast_to([P, v.shape[1], n])

        def x_to_T(i):
            for t in range(TB):
                for half in range(2):
                    name = ("xT", i, t, half)
                    o = get(name)
                    c = slice(half * 4, half * 4 + 4)
                    low(name, xl[:, c, t * P:t * P + P], quad(o[:, :]), xh[:, c, t * P:t * P + P])

        def out_proj(j):
            _, _, c = norm_of(j)

            def residual(t, half):
                f = slice(half * 512, half * 512 + 512)
                name = ("y", j, t, half)
                o = get(name)
                free(name, dve.scalar_tensor_tensor(z[:, t, f], x[:, t, f], ALPHA / c, o[:, :], ALU.mult, ALU.add))
                await_read(name)
                link(dve.bn_stats(stat[:, t, half, :], z[:, t, f]))

            for t in range(TB):
                residual(t, 0)
            if cross_after(j):
                for t in range(TB):
                    for h2 in range(2):
                        name = ("memT", j + 1, t, h2)
                        o = get(name)
                        k = slice(h2 * 4, h2 * 4 + 4)
                        low(name, ml[:, k, t * P:t * P + P], quad(o[:, :]), mh[:, k, t * P:t * P + P])
            ahead(("y", j, 1, 1))
            for t in range(TB):
                residual(t, 1)
                link(dve.bn_aggr(mv[:, t, 0:2], stat[:, t, 0:2, :]))
                dve.tensor_scalar(mv[:, t, 1:2], mv[:, t, 1:2], EPS / c ** 2, None, ALU.add)\
                   .then_inc(sig("var_ready"), 1)
                if t == 0:
                    wait("gains_loaded", 32 * (j + 1))
                link(dve.scalar_tensor_tensor(z[:, t, :], z[:, t, :], mv[:, t, 0:1], gb[:, 0, :],
                                              ALU.subtract, ALU.mult))
                wait("std_ready", 2 * j + t + 1)
                link(dve.reciprocal(mv[:, t, 3:4], mv[:, t, 2:3]))
                for half in range(2):
                    f = slice(half * 512, half * 512 + 512)
                    dve.scalar_tensor_tensor(x[:, t, f], z[:, t, f], mv[:, t, 3:4], gb[:, 1, f],
                                             ALU.mult, ALU.add).then_inc(sig("x_ready"), 1)
            if cross_after(j):
                c = cross_of(SUB[j + 1][1], 0)[4]
                for half in range(c):
                    for t in range(TB):
                        name = ("xv", j + 1, t, half)
                        o = get(name)
                        free(name, dve.tensor_copy(xv[:, t, half * 512:half * 512 + 512], o[:, :]))

        def softmax(n_units, biased, after=None):
            for t in range(n_units + 2):
                if t < n_units:
                    neg_max(unit[0] + t, biased)
                if 1 <= t <= n_units:
                    normalise(unit[0] + t - 1, biased)
                if t >= 2 and after:
                    after(t - 2)
            unit[0] += n_units

        def neg_max(g, biased):
            o = get(("S", g))
            if biased:
                dve.wait_ge(sig("bias_ready"), biased_no[0] + 1)
                if g >= 2:
                    wait("neg_max", g - 1)
                free(("S", g), dve.tensor_tensor(logit[:, g % 2, :], o[:, :], bm[:, g % 2, :], ALU.add))
                await_read(("S", g))
                o = logit[:, g % 2, :]
                biased_no[0] += 1
            dve.tensor_reduce(nmax[:, g % 2, 0:2], two(o[:, :] if not biased else o), AX, ALU.max, negate=True)\
               .then_inc(sig("neg_max"), 1)

        def normalise(g, biased):
            if biased:
                wait("exp_done", biased_done[0] + 1)
                biased_done[0] += 1
            else:
                await_read(("S", g))
            link(dve.reciprocal(rden[:, g % 2, 0:2], psum_e[:, g % 2, 0:2]))
            dve.tensor_tensor(two(prob[:, g % 2, :]), two(prob[:, g % 2, :]), along(rden[:, g % 2, 0:2], S),
                              ALU.mult).then_inc(sig("prob_ready"), 1)

        def cross(j):
            c = cross_of(SUB[j][1], 0)[4]
            base = unit[0]

            def after(u):
                name = ("O", base + u)
                o = get(name)
                k = slice(c * u, c * u + c)
                low(name, ol[:, k, :], o[:, 0:c * S].rearrange("p (c s) -> p c s", c=c), oh[:, k, :])

            split_to(where[("S", base)][2] + PARTS - 1)
            softmax(4, False, after)
            out_proj(j)

        def ffn(j):
            for q in range(HC // 2 + 1):
                if q < HC // 2:
                    name = ("up", j, q)
                    o = get(name)
                    await_read(("gate", j, q))
                    if q >= 2:
                        copy_used(("hid", j, q - 2))
                    free(name, dve.tensor_tensor(hid[:, q % 2, :], gate_s[:, q % 2, :], o[:, :], ALU.mult))
                if q >= 1:
                    k = slice(2 * q - 2, 2 * q)
                    low(("hid", j, q - 1), hl[:, k, :], two(hid[:, (q - 1) % 2, :]), hh[:, k, :], False)
            out_proj(j)

        def even(j):
            o = get("gates")
            wait("even_loaded", 32)
            for t in range(TB):
                ins = dve.tensor_tensor(gt[:, t, :], o[:, t * 16:t * 16 + 16], gbias[:, :], ALU.add)
            free("gates", ins)
            await_read("gates")
            f = gt[:, :, 8:16]
            dve.scalar_tensor_tensor(lf[:, 0, :, :], f, -1.0, f, ALU.mult, ALU.max).then_inc(sig("abs_f"), 1)
            for n in range(4):
                get(("aqk", n))
                await_read(("aqk", n))
                for tap in range(5):
                    for k in (2 * n, 2 * n + 1):
                        w = pc[:, ROWS["even_conv_w"] + tap * 8 + k:ROWS["even_conv_w"] + tap * 8 + k + 1]
                        if tap == 0:
                            ins = dve.tensor_scalar(qkT[:, k, :], cpad[:, k, 0:S], w, None, ALU.mult)
                        else:
                            ins = dve.scalar_tensor_tensor(qkT[:, k, :], cpad[:, k, tap:tap + S], w, qkT[:, k, :],
                                                           ALU.mult, ALU.add)
                    if n == 3 and tap == 4:
                        ins.then_inc(sig("conv_done"), 1)
                    else:
                        link(ins)
            wait("softplus_f", 1)
            dve.scalar_tensor_tensor(lf[:, 3, :, :], f, 0.0, lf[:, 2, :, :], ALU.min, ALU.subtract)\
               .then_inc(sig("logf_ready"), 1)
            for t in range(TB):
                name = ("av", t)
                o = get(name)
                free(name, dve.tensor_copy(av[:, t, :, 0:P], quad(o[:, :])))
            for t in range(TB):
                name = ("bv", t)
                o = get(name)
                free(name, dve.tensor_copy(bv[:, t, :], o[:, :]))
            wait("silu_done", 1)
            dve.tensor_scalar(qkT[:, 4:8, :], qkT[:, 4:8, :], float(P ** -0.5), None, ALU.mult)\
               .then_inc(sig("qk_ready"), 1)
            o = get("cum")
            free("cum", dve.tensor_copy(bs[:, :], o[:, 0:32]))
            await_read("cum")
            dve.tensor_tensor(cc_[:, :, :], gt[:, :, 0:8], two(bs[:, 0:16]), ALU.subtract)\
               .then_inc(sig("decay_cols"), 1)
            wait("decay_cols", 1)
            b_of = bs[:, 0:16].rearrange("p (t d h) -> p t d h", t=TB, d=2)
            tot = bs[:, 16:32].rearrange("p (t d h) -> p t d h", t=TB, d=2)
            c_of = cc_[:, :, :].rearrange("p t (d h) -> p t d h", d=2)
            for d in range(2):
                mask = ec[:, 512 + d * P:640 + d * P].unsqueeze(1).broadcast_to([P, 4, P])
                for t in range(TB):
                    name = ("C", d, t)
                    o = get(name)
                    if t == d:
                        dve.tensor_reduce(mm_[:, 0, d, t, :], quad(o[:, :]), AX, ALU.max)
                    free(name, dve.tensor_tensor(cm[:, d, t, :, :], quad(o[:, :]), mask, ALU.add))
                    await_read(name)
                    link(dve.tensor_reduce(mm_[:, 1, d, t, :], cm[:, d, t, :, :], AX, ALU.max))
            for d in range(2):
                t1, t2 = d, 1 - d
                link(dve.tensor_tensor(mm_[:, 2, d, t2, :], tot[:, t1, d, :], mm_[:, 0, d, t1, :], ALU.add))
                dve.tensor_copy(mm_[:, 3, d, t1, :], mm_[:, 1, d, t1, :])
                link(dve.tensor_tensor(mm_[:, 3, d, t2, :], mm_[:, 1, d, t2, :], mm_[:, 2, d, t2, :], ALU.max))
                link(dve.tensor_scalar(mm_[:, 4, d, :, :], mm_[:, 3, d, :, :], -1.0, None, ALU.mult))
                dve.tensor_tensor(mm_[:, 5, d, :, :], b_of[:, :, d, :], mm_[:, 3, d, :, :], ALU.add)
                dve.tensor_tensor(mm_[:, 6, d, t2, :], mm_[:, 2, d, t2, :], mm_[:, 3, d, t2, :], ALU.subtract)
                link(dve.tensor_tensor(mm_[:, 7, d, t1, :], c_of[:, t1, d, :], mm_[:, 0, d, t1, :], ALU.subtract))
            for d in range(2):
                ins = dve.memset(mm_[:, 6, d, d, :], 0.0)
                ins = dve.memset(mm_[:, 7, d, 1 - d, :], 0.0)
            ins.then_inc(sig("decay_exponents"), 1)
            wait("mlstm_small", 3)
            for d in range(2):
                name = ("kN", d)
                o = get(name)
                free(name, dve.tensor_tensor(pk[:, d, :, :], quad(o[:, :]), along(mm_[:, 7, d, d, :], P), ALU.mult))
            for t in range(TB):
                name = ("QK", t)
                o = get(name)
                for d in range(2):
                    wait("decay_ready", 2 * t + d + 1)
                    ins = dve.tensor_tensor(cm[:, d, t, :, :], cm[:, d, t, :, :], quad(o[:, :]), ALU.mult)
                    ins.then_inc(sig("decayed"), 1)
                    wait("decayed", 2 * t + d + 1)
                    ins = dve.tensor_reduce(mm_[:, 8, d, t, :], cm[:, d, t, :, :], AX, ALU.add)
                free(name, ins)
            for d in range(2):
                t2 = 1 - d
                for half in range(2):
                    name = ("int", d, half)
                    o = get(name)
                    h2 = slice(2 * half, 2 * half + 2)
                    free(name, dve.tensor_tensor(cn[:, d, h2, :], o[:, 0:260].rearrange("p (h e) -> p h e", h=2),
                                                 along(mm_[:, 6, d, t2, h2], 130), ALU.mult))
                    await_read(name)
                link(dve.tensor_tensor(mm_[:, 8, d, t2, :], mm_[:, 8, d, t2, :], cn[:, d, :, P], ALU.add))
            den = mm_[:, 8, :, :, :]
            link(dve.scalar_tensor_tensor(mm_[:, 9, :, :, :], den, -1.0, den, ALU.mult, ALU.max))
            link(dve.tensor_tensor(mm_[:, 9, :, :, :], mm_[:, 9, :, :, :], mm_[:, 5, :, :, :], ALU.max))
            link(dve.reciprocal(mm_[:, 9, :, :, :], mm_[:, 9, :, :, :]))
            for t in range(TB):
                for d in range(2):
                    name = ("num", d, t)
                    o = get(name)
                    h_d = quad(prob[:, d, :])
                    rd = along(mm_[:, 9, d, t, :], P)
                    if d == t:
                        free(name, dve.tensor_tensor(h_d, quad(o[:, :]), rd, ALU.mult))
                        await_read(name)
                    else:
                        free(name, dve.tensor_tensor(h_d, quad(o[:, :]), cn[:, d, :, 0:P], ALU.add))
                        await_read(name)
                        link(dve.tensor_tensor(h_d, h_d, rd, ALU.mult))
                dve.tensor_tensor(logit[:, t, :], prob[:, 0, :], prob[:, 1, :], ALU.add)\
                   .then_inc(sig("mlstm_out"), 1)
                wait("mlstm_out", t + 1)
            dve.wait_ge(bank_free[where[("ao", 1)][0]], where[("ao", 1)][3])
            for t in range(TB):
                name = ("hT", t)
                o = get(name)
                free(name, dve.tensor_tensor(quad(probT[:, t, :]), quad(o[:, :]), ao[:, :, t * P:t * P + P], ALU.mult))
            for t in range(TB):
                low(("aT", t), ol[:, 0:4, t * P:t * P + P], quad(probT[:, t, :]), oh[:, 0:4, t * P:t * P + P], False)
            base = unit[0]

            def after(u):
                if u % 2:
                    name = ("O", base + u - 1)
                    o = get(name)
                    low(name, ol[:, 4 + u // 2, :], o[:, 0:S], oh[:, 4 + u // 2, :])

            softmax(8, True, after)
            out_proj(j)

        def odd(j):
            wait("lam_loaded", 16)
            wait("odd_loaded", 16)
            lt = lamt[:, :, :].rearrange("p (a b) e -> p a b e", b=2)
            link(dve.tensor_tensor(rt[:, 0, 0:128].rearrange("p (a e) -> p a e", a=2), lt[:, :, 0, :], lt[:, :, 1, :],
                                   ALU.mult))
            dve.tensor_reduce(lam[:, 0:2], rt[:, 0, 0:128].rearrange("p (a e) -> p a e", a=2), AX, ALU.add)\
               .then_inc(sig("lam_sums"), 1)
            wait("lam_exp", 1)
            link(dve.tensor_tensor(lam[:, 4:5], lam[:, 3:4], lam[:, 2:3], ALU.subtract))
            link(dve.tensor_scalar(lam[:, 5:6], lam[:, 4:5], -LAM_INIT, None, ALU.add))
            link(dve.tensor_scalar(lam[:, 6:7], pc[:, ROWS["odd_subln_g"]:ROWS["odd_subln_g"] + 1],
                                   1.0 - LAM_INIT, None, ALU.mult))
            cos = oc[:, 128:384].unsqueeze(1).broadcast_to([P, 2, S])
            sin = oc[:, 384:640].unsqueeze(1).broadcast_to([P, 2, S])
            for n in range(8 + 1):
                if n < 8:
                    split_to(where[("rp", n)][2] + PARTS - 1)
                if n >= 1:
                    k = n - 1
                    name = ("rot", k)
                    o = get(name)
                    if k:
                        wait("rope_done", k)
                    free(name, dve.tensor_tensor(two(rt[:, 0, :]), two(o[:, :]), sin, ALU.mult))
                    link(dve.tensor_tensor(two(rt[:, 1, :]), two(rs[:, k % 2, :]), cos, ALU.mult))
                    await_read(name)
                    dve.tensor_tensor(rq[:, 2 * k:2 * k + 2, :], two(rt[:, 0, :]), two(rt[:, 1, :]), ALU.add)\
                       .then_inc(sig("rope_done"), 1)
            for half in range(2):
                for t in range(TB):
                    name = ("dv", t, half)
                    o = get(name)
                    free(name, dve.tensor_copy(dv[:, t, half * 512:half * 512 + 512], o[:, :]))
            for t in range(8 + 2):
                if t < 8:
                    g = unit[0] + t
                    for c in range(2):
                        o = get(("S", g, c))
                        ins = dve.tensor_reduce(nmax[:, g % 2, 2 * c:2 * c + 2], two(o[:, :]), AX, ALU.max,
                                                negate=True)
                    ins.then_inc(sig("neg_max"), 1)
                if 1 <= t <= 8:
                    g = unit[0] + t - 1
                    buf = (prob, logit)[(t - 1) % 2]
                    await_read(("S", g, 0))
                    await_read(("S", g, 1))
                    link(dve.reciprocal(rden[:, g % 2, :], psum_e[:, g % 2, :]))
                    link(dve.tensor_scalar(rden[:, g % 2, 2:4], rden[:, g % 2, 2:4], lam[:, 5:6], None, ALU.mult))
                    for tb in range(TB):
                        sl = slice(tb * S, tb * S + S)
                        ins = dve.tensor_scalar(buf[:, 0, sl], buf[:, 0, sl], rden[:, g % 2, tb:tb + 1], None, ALU.mult)
                    link(ins)
                    for tb in range(TB):
                        sl = slice(tb * S, tb * S + S)
                        ins = dve.scalar_tensor_tensor(buf[:, 0, sl], buf[:, 1, sl], rden[:, g % 2, 2 + tb:3 + tb],
                                                       buf[:, 0, sl], ALU.mult, ALU.add)
                    ins.then_inc(sig("prob_ready"), 1)
                if t >= 2:
                    u = t - 2
                    name = ("O", unit[0] + u)
                    o = get(name)
                    free(name, dve.tensor_copy(on[:, u, :, :], two(o[:, 0:2 * P])))
                    await_read(name)
                    link(dve.tensor_tensor(two(osq[:, u % 2, :]), on[:, u, :, :], on[:, u, :, :], ALU.mult))
                    link(dve.tensor_reduce(oss[:, 2, 2 * u:2 * u + 2], two(osq[:, u % 2, :]), AX, ALU.add))
            dve.tensor_scalar(oss[:, 0, :], oss[:, 2, :], 1.0 / P, EPS, ALU.mult, ALU.add)\
               .then_inc(sig("diff_var"), 1)
            wait("diff_std", 1)
            link(dve.reciprocal(oss[:, 2, :], oss[:, 1, :]))
            for u in range(8):
                dve.tensor_tensor(on[:, u, :, :], on[:, u, :, :], along(oss[:, 2, 2 * u:2 * u + 2], P), ALU.mult)\
                   .then_inc(sig("diff_normed"), 1)
            for u in range(8):
                name = ("OT", u)
                o = get(name)
                if u >= 2:
                    copy_used(("OT", u - 2))
                free(name, dve.tensor_scalar(osq[:, u % 2, :], o[:, 0:S], lam[:, 6:7], None, ALU.mult))
                low(name, ol[:, u, :], osq[:, u % 2, :], oh[:, u, :], False)
            unit[0] += 8
            out_proj(j)

        def conv_tile(l_, i):
            n = i // 3
            y = two(bm[:, 1, :])
            if i % 3 == 0:
                ahead(("cc", l_, n))
            elif i % 3 == 1:
                name = ("ch", l_, n)
                o = get(name)
                wait("zc_pads", l_ + 1)
                await_read(("cc", l_, n))
                free(name, dve.tensor_tensor(zc[:, :, 2:2 + S], y, two(o[:, :]), ALU.mult))
                await_read(name)
                for tap in range(3):
                    for k in range(2):
                        r = ROWS["conv_w_2"] + l_ * 12 + tap * 4 + 2 * n + k
                        w = pc[:, r:r + 1]
                        if tap == 0:
                            ins = dve.tensor_scalar(y[:, k, :], zc[:, k, 0:S], w, None, ALU.mult)
                        else:
                            ins = dve.scalar_tensor_tensor(y[:, k, :], zc[:, k, tap:tap + S], w, y[:, k, :],
                                                           ALU.mult, ALU.add)
                    link(ins)
            else:
                name = ("cb", l_, n)
                o = get(name)
                free(name, dve.tensor_tensor(bm[:, 1, :], bm[:, 1, :], o[:, :], ALU.mult))
                k = slice(8 + 2 * n, 10 + 2 * n)
                low(("yc", l_, n), yl[:, k, :], y, yh[:, k, :], False)

        def merge(j):
            l_ = SUB[j][2]
            for t in range(TB):
                name = ("ckv", l_, t)
                o = get(name)
                free(name, dve.tensor_copy(ckn[:, t, :], o[:, 0:P]))
                await_read(name)
            link(dve.tensor_tensor(cksq[:, :, :], ckn[:, :, :], ckn[:, :, :], ALU.mult))
            link(dve.tensor_reduce(cks[:, 0:2], cksq[:, :, :], AX, ALU.add))
            dve.tensor_scalar(cks[:, 0:2], cks[:, 0:2], 1.0 / P, EPS, ALU.mult, ALU.add).then_inc(sig("ckv_var"), 1)
            wait("ckv_std", l_ + 1)
            link(dve.reciprocal(cks[:, 0:2], cks[:, 2:4]))
            for t in range(TB):
                dve.tensor_scalar(ckn[:, t, :], ckn[:, t, :], cks[:, t:t + 1], None, ALU.mult)\
                   .then_inc(sig("ckv_normed"), 1)
            name = ("iw", l_)
            o = get(name)
            free(name, dve.tensor_scalar(iw[:, :, :], o[:, 0:16].rearrange("p (t h) -> p t h", t=TB),
                                         float(8 ** -0.5 * 64 ** -0.5), None, ALU.mult))
            await_read(name)
            g = pc[:, ROWS["kv_norm_g_2"] + l_:ROWS["kv_norm_g_2"] + l_ + 1]
            name = ("ckT", l_)
            o = get(name)
            free(name, dve.tensor_scalar(ckT[:, :], o[:, 0:S], g, None, ALU.mult))
            wait("merge_loaded", 32 * (l_ + 1))
            for u in range(8):
                split_to(where[("dot", l_, u)][2] + PARTS - 1)
                await_read(("dot", l_, u))
                for tb in range(TB):
                    before = sc_[:, tb * S:tb * S + S] if u == 0 else score[:, tb, :]
                    ins = dve.scalar_tensor_tensor(score[:, tb, :], prob[:, u % 2, tb * S:tb * S + S],
                                                   iw[:, tb, u:u + 1], before, ALU.mult, ALU.add)
                ins.then_inc(sig("scored"), 1)
                wait("scored", 8 * l_ + u + 1)

            def choose(tb):
                w = P * (tb + 1)
                for r in range(TOPK // 8):
                    link(dve.max(top8[:, :], score[:, tb, 0:w]))
                    link(dve.match_replace(score[:, tb, 0:w], top8[:, :], score[:, tb, 0:w], FOUND))
                link(dve.tensor_scalar(selm[:, tb, :], score[:, tb, :], FOUND / 3, NEG, ALU.is_ge, ALU.mult))
                dve.tensor_tensor(selm[:, tb, :], selm[:, tb, :], sc_[:, tb * S:tb * S + S], ALU.add)\
                   .then_inc(sig("chosen"), 1)

            choose(0)
            split_to(where[("qa", l_, 1)][2] + PARTS - 1)
            choose(1)
            for t in range(TB):
                name = ("vs", l_, t)
                o = get(name)
                free(name, dve.tensor_copy(vs[:, t, :], o[:, :]))
            for t in range(8 + 2):
                if t < 8:
                    name = ("z", l_, t)
                    o = get(name)
                    wait("log1p_ready", 8 * l_ + t + 1)
                    dve.scalar_tensor_tensor(prob[:, t % 2, :], o[:, :], 0.0, logit[:, t % 2, :], ALU.max, ALU.add)\
                       .then_inc(sig("softplus_ready"), 1)
                    wait("softplus_ready", 8 * l_ + t + 1)
                    free(name, dve.tensor_tensor(logit[:, t % 2, :], o[:, :], sc_[:, 1024:1536], ALU.add))
                if 1 <= t <= 8:
                    u = t - 1
                    name = ("later", l_, u)
                    o = get(name)
                    await_read(("z", l_, u))
                    free(name, dve.tensor_tensor(logit[:, u % 2, :], logit[:, u % 2, :], o[:, :], ALU.subtract))
                if t >= 3 and t % 2:
                    i = (t - 3) // 2
                    name = ("yb", l_, i)
                    o = get(name)
                    low(name, yl[:, 4 + i, :], o[:, 0:S], yh[:, 4 + i, :])
                if t < 6:
                    conv_tile(l_, t)
                elif t in STICK_GATES:
                    ahead(("bgate", l_, *divmod(STICK_GATES[t], 3)))
            for t in range(-1, 8 + 3):
                if 0 <= t < 8:
                    neg_max(unit[0] + t, True)
                if 1 <= t <= 8:
                    normalise(unit[0] + t - 1, True)
                if 2 <= t <= 9:
                    u = t - 2
                    name = ("lat", l_, u)
                    o = get(name)
                    free(name, dve.tensor_scalar(olat[:, u % 2, :], o[:, 0:S], g, None, ALU.mult))
                if t >= 4 and t % 2 == 0:
                    i = (t - 4) // 2
                    name = ("ya", l_, i)
                    o = get(name)
                    low(name, yl[:, i, :], o[:, 0:S], yh[:, i, :])
                if t in LATENT_GATES:
                    ahead(("bgate", l_, *divmod(LATENT_GATES[t], 3)))
            unit[0] += 8
            for n in range(4):
                for i in range(3):
                    k = 3 * n + i
                    name = ("branch", l_, n, i)
                    o = get(name)
                    await_read(("bgate", l_, n, i))
                    if i == 0 and n >= 2:
                        copy_used(("merged", l_, n - 2))
                    if i == 0 and n >= 1:
                        wait("merged_ready", 4 * l_ + n)
                    dst = logit[:, n % 2, :] if i == 0 else probT[:, k % 2, :]
                    free(name, dve.tensor_tensor(dst, open_gate(k), o[:, :], ALU.mult))
                    await_read(name)
                    if i:
                        ins = dve.tensor_tensor(logit[:, n % 2, :], logit[:, n % 2, :], probT[:, k % 2, :], ALU.add)
                        if i == 1:
                            link(ins)
                        else:
                            ins.then_inc(sig("merged_ready"), 1)
                k = slice(2 * n, 2 * n + 2)
                low(("merged", l_, n), ol[:, k, :], two(logit[:, n % 2, :]), oh[:, k, :], False)
            out_proj(j)

        biased_done = [0]
        dve.memset(ones[:, :], 1.0).then_inc(sig("ones_set"), 1)
        split_to(0)
        x_to_T(0)
        o = get("cols")
        free("cols", dve.tensor_copy(pc[:, 0:N_ROWS], o[:, 0:N_ROWS]))
        await_read("cols")
        program_of = {"even": even, "odd": odd, "merge": merge, "cross": cross, "ffn": ffn}
        for j, (kind, _, _, _) in enumerate(SUB[:LAST]):
            program_of[kind](j)
            if j + 1 < LAST:
                x_to_T(j + 1)

    @block.gpsimd
    def _(pool):
        step = [0]
        unit = [0]
        biased = [0]
        mems = [0]

        def await_read(name):
            pool.wait_ge(bank_free[where[name][0]], where[name][3])

        def link(ins):
            step[0] += 1
            ins.then_inc(sig("pool_step"), 1)
            pool.wait_ge(sig("pool_step"), step[0])

        def const(dst, name, width, what):
            c0 = CONST[name][0]
            pool.dma_start(dst, A["consts"][:, c0:c0 + width]).then_inc(sig(what), 16)

        def gains(j):
            if j:
                pool.wait_ge(sig("x_ready"), 4 * j)
            g, b, _ = norm_of(j)
            for i, v in enumerate((g, b)):
                pool.dma_start(gb[:, i, :], v.partition_broadcast(P)).then_inc(sig("gains_loaded"), 16)

        def mem_load(j):
            if not cross_after(j) or j >= LAST:
                return
            await_halves(pool, mem_start[j + 1])
            pool.dma_start(mem_n[:, :, :], cross_of(SUB[j + 1][1], 0)[0].rearrange("(t p) d -> p t d", p=P))\
                .then_inc(sig("mem_loaded"), 16)

        def cross(j):
            unit[0] += 4

        def ffn(j):
            pass

        def even(j):
            def load(u):
                for r in range(4):
                    src = bass.AP(tensor=rpb_d.tensor, offset=(u * 7 + 3 - r) * P + 63,
                                  ap=[[7 * 8 * P - 1, 64], [P, 4], [1, 64]])
                    q = slice(64 * (r % 2), 64 * (r % 2) + 64)
                    c0 = (r // 2) * S
                    pool.dma_start(bm[q, u % 2, c0:c0 + S].rearrange("p (a c) -> p a c", a=4), src)\
                        .then_inc(sig(f"bias_loaded{u % 2}"), 16)

            def mask(u):
                pool.wait_ge(sig(f"bias_loaded{u % 2}"), 64 * (u // 2 + 1))
                m = ec[:, 256:512].unsqueeze(1).broadcast_to([P, 2, S])
                b = bm[:, u % 2, :].rearrange("p (t s) -> p t s", t=2)
                pool.tensor_tensor(b, b, m, ALU.add).then_inc(sig("bias_ready"), 1)

            pool.memset(av[:, :, :, P:P + 2], 1.0).then_inc(sig("av_ones"), 1)
            pool.memset(cpad[:, :, 0:2], 0.0)
            pool.memset(cpad[:, :, S + 2:S + 4], 0.0).then_inc(sig("pads_set"), 1)
            link(pool.memset(rpad[:, :, :, :], 0.0))
            for pair in range(4):
                for i in range(2):
                    pool.dma_start(rpad[:, i, :, 48:79],
                                   A["even_rpb"][0, 2 * pair + i, 4:11, :].partition_broadcast(64))\
                        .then_inc(sig("rpb_loaded"), 16)
                pool.wait_ge(sig("rpb_loaded"), 32 * (pair + 1))
                pool.dma_start(rpb_d[:, pair * 14 * P:(pair + 1) * 14 * P],
                               rpad[:, :, :, :].rearrange("p h r c -> p (h r c)"))\
                    .then_inc(sig("rpb_stored"), 16)
                pool.wait_ge(sig("rpb_stored"), 16 * (pair + 1))
            await_read(("tab", 7))
            pool.dma_start(bias_d, btab[:, :, :].rearrange("p h c -> p (h c)"))\
                .then_inc(sig("distances_stored"), 16)
            load(0)
            load(1)
            for u in range(8):
                mask(u)
                if u + 2 < 8:
                    await_read(("S", unit[0] + u))
                    load(u + 2)
            unit[0] += 8
            biased[0] += 8

        def odd(j):
            const(oc[:, :], "rot", 640, "odd_loaded")
            pool.dma_start(lamt[:, :, :].rearrange("p a e -> p (a e)"),
                           A["odd_lambda"][0].rearrange("a e -> (a e)").partition_broadcast(P))\
                .then_inc(sig("lam_loaded"), 16)
            unit[0] += 8

        def merge(j):
            l_ = SUB[j][2]
            const(sc_[:, :], "topk_causal", 1536, "merge_loaded")
            const(tge[:, :], "tri_ge", P, "merge_loaded")
            pool.dma_start(uk[:, :, :], A["w_uk_2"][l_].rearrange("(a b) d c -> (b d) a c", b=2))\
                .then_inc(sig("latent_weights"), 16)
            pool.dma_start(uv[:, :, :], A["w_uv_2"][l_].rearrange("h c d -> c h d")).then_inc(sig("latent_weights"), 16)
            pool.memset(zc[:, :, 0:2], 0.0).then_inc(sig("zc_pads"), 1)

            pool.wait_ge(sig("distances_stored"), 16)

            def load(u):
                src = bass.AP(tensor=bias_d.tensor, offset=u * 512 + 127, ap=[[8 * 512 - 1, P], [1, 384]])
                pool.dma_start(gth[:, u % 2, :], src).then_inc(sig(f"distance_loaded{u % 2}"), 16)

            load(0)
            load(1)
            pool.wait_ge(sig("merge_loaded"), 32 * (l_ + 1))
            for u in range(8):
                pool.wait_ge(sig("softplus_ready"), 8 * l_ + u + 1)
                pool.tensor_tensor(prob[:, u % 2, :], prob[:, u % 2, :], sc_[:, 512:1024], ALU.mult)\
                    .then_inc(sig("softplus_masked"), 1)
            pool.wait_ge(sig("chosen"), 2 * (l_ + 1))
            pool.wait_ge(sig("part_low"), copies[halves[("yc", l_, 1)]])
            for u in range(8):
                if u >= 2:
                    await_read(("S", unit[0] + u - 2))
                pool.wait_ge(sig(f"distance_loaded{u % 2}"), 16 * (4 * l_ + u // 2 + 1))
                for tb in range(TB):
                    c0 = P * (1 - tb)
                    ins = pool.tensor_tensor(bm[:, u % 2, tb * S:tb * S + S], gth[:, u % 2, c0:c0 + S],
                                             selm[:, tb, :], ALU.add)
                biased[0] += 1
                ins.then_inc(sig("bias_ready"), 1)
                if u + 2 < 8:
                    pool.wait_ge(sig("bias_ready"), biased[0])
                    load(u + 2)
            unit[0] += 8

        for name, ap in (("even_conv_w", A["even_conv_w"][0].rearrange("j (c p) -> (j c) p", p=P)),
                         ("b_gate_2", A["b_gate_2"].rearrange("l i (c p) -> (l i c) p", p=P)),
                         ("conv_w_2", A["conv_w_2"].rearrange("l j (c p) -> (l j c) p", p=P)),
                         ("kv_norm_g_2", A["kv_norm_g_2"]), ("odd_subln_g", A["odd_subln_g"])):
            r = ROWS[name]
            pool.dma_start(prow[r:r + ap.shape[0], :], ap).then_inc(sig("rows_loaded"), 16)
        const(ec[:, :], "tri_le", 768, "even_loaded")
        pool.dma_start(gbias[:, :], A["even_gate_b"][0].partition_broadcast(P)).then_inc(sig("even_loaded"), 16)
        pool.dma_start(brel0[:, :], A["rel_bias_2"]).then_inc(sig("rel_loaded"), 16)
        const(boneh[:, :], "bucket", 512, "rel_loaded")
        program_of = {"even": even, "odd": odd, "merge": merge, "cross": cross, "ffn": ffn}
        for j, (kind, _, _, _) in enumerate(SUB[:LAST]):
            gains(j)
            program_of[kind](j)
            mem_load(j)

    @block.sync
    def _(sp):
        c0 = CONST["ident"][0]
        sp.dma_start(ident[:, :], A["consts"][:, c0:c0 + P]).then_inc(sig("ident_loaded"), 16)
        sp.dma_start(x[:, :, :], A["x"][0].rearrange("(t p) d -> p t d", p=P)).then_inc(sig("x_loaded"), 16)
        for t, (pieces, nk, w) in enumerate(weight_tiles):
            if t >= RAW:
                sp.wait_ge(sig("w_high"), t - RAW + 1)
                sp.wait_ge(sig("w_low"), t - RAW + 1)
            dst = raw_tile(t).rearrange("p (k c) -> p k c", k=nk)
            c0 = 0
            for piece in pieces:
                c1 = c0 + piece.shape[-1]
                sp.dma_start(dst[:, :, c0:c1], piece.rearrange("(k p) c -> p k c", p=P))\
                  .then_inc(raw_full[t % RAW], 16)
                c0 = c1
        sp.wait_ge(sig("x_ready"), 4 * LAST)
        sp.dma_start(out[0].rearrange("(t p) d -> p t d", p=P), x[:, :, :]).then_inc(out_stored, 16)
        sp.wait_ge(out_stored, 16)


def kernel(**inputs):
    import concourse.bacc as _bacc
    from concourse.bass_utils import run_bass_kernel_spmd as _run

    nc = _bacc.Bacc("TRN2", target_bir_lowering=False, num_devices=1)
    arrays, args = {}, {}
    for name, value in [*inputs.items(), ("consts", shape_constants())]:
        a = np.ascontiguousarray(value)
        arrays[f"in_{name}"] = a
        args[name] = nc.dram_tensor(f"in_{name}", a.shape, mybir.dt.from_np(a.dtype), kind="ExternalInput").ap()
    out = nc.dram_tensor("out_0", (1, S, D), F32, kind="ExternalOutput").ap()
    with ExitStack() as ctx:
        program(nc, ctx, args, out)
    r = _run(nc, [arrays], core_ids=[0])
    return r.results[0]["out_0"]
```

```python
from contextlib import ExitStack

import numpy as np

import concourse.bass as bass
from concourse import mybir

F32 = mybir.dt.float32
F32R = mybir.dt.float32r
ALU = mybir.AluOpType
ACT = mybir.ActivationFunctionType
AX = mybir.AxisListType.X

P = 128
D = 1024
KC = D // P
S = 256
TB = S // P
TILE = 2048
RAW, PARTS = 3, 3
FFN = 2816
HC = FFN // P
ALPHA = 4.0 ** 0.25
EPS = 1e-5
NEG = -1e30
LAM_INIT = 0.8 - 0.6 * float(np.exp(-0.3))
TOPK = 64
FOUND = -3e38
BUCKETS = 32

ROWS = {"even_conv_w": 0, "b_gate_2": 40, "conv_w_2": 88, "kv_norm_g_2": 112, "odd_subln_g": 114}
N_ROWS = 115

CONST = {}
CONST_W = 0
for _name, _w in (("ident", 128), ("tri_le", 128), ("tri_ge", 128), ("na_mask", 256), ("causal_le", 128),
                  ("causal_ge", 128), ("rot", 128), ("cos", 256), ("sin", 256), ("topk_causal", 512),
                  ("strict", 512), ("strict_neg", 512), ("bucket", 512)):
    CONST[_name] = (CONST_W, _w)
    CONST_W += _w


def shape_constants():
    c = {}
    i = np.arange(P)
    c["ident"] = np.eye(P)
    c["tri_le"] = (i[:, None] <= i[None, :])
    c["tri_ge"] = (i[:, None] >= i[None, :])
    qc, kc = (i % 64)[:, None], (np.arange(S) % 64)[None, :]
    start = np.clip(qc - 8, 0, 48)
    c["na_mask"] = np.where((kc >= start) & (kc < start + 16), 0.0, NEG)
    c["causal_le"] = np.where(i[None, :] <= i[:, None], 0.0, NEG)
    c["causal_ge"] = np.where(i[None, :] >= i[:, None], 0.0, NEG)
    rot = np.zeros((P, P))
    for m in range(P):
        if m % 64 < 32:
            rot[m + 32, m] = -1.0
        else:
            rot[m - 32, m] = 1.0
    c["rot"] = rot
    inv = np.float32(10000.0) ** (-np.arange(0, 64, 2, dtype=np.float32) / np.float32(64))
    ang = np.arange(S, dtype=np.float32)[None, :] * inv.astype(np.float32)[:, None]
    c["cos"] = np.tile(np.cos(ang), (4, 1))
    c["sin"] = np.tile(np.sin(ang), (4, 1))
    t = (np.arange(TB)[None, :, None] * P + i[:, None, None])
    c["topk_causal"] = np.where(np.arange(S)[None, None, :] <= t, 0.0, NEG).reshape(P, 512)
    s = (np.arange(TB)[None, :, None] * P + i[:, None, None])
    strict = s < np.arange(S)[None, None, :]
    c["strict"] = strict.reshape(P, 512)
    c["strict_neg"] = np.where(strict, 0.0, NEG).reshape(P, 512)
    n = np.maximum(255 - np.arange(512), 0)
    nf = np.maximum(n, 1).astype(np.float32)
    large = 16 + (np.log(nf / np.float32(16)) / np.float32(np.log(8.0)) * 16).astype(np.int32)
    bucket = np.where(n < 16, n, np.minimum(large, BUCKETS - 1))
    onehot = np.zeros((P, 512))
    onehot[bucket, np.arange(512)] = 1.0
    c["bucket"] = onehot
    return np.concatenate([np.asarray(c[k], np.float32) for k in CONST], axis=1)


def program(nc, ctx, A, out, LAST=14):
    def sb(name, shape, dt=F32, on=None):
        return (on or ctx).enter_context(nc.sbuf_tensor(name, shape, dt))

    def sem(name):
        return ctx.enter_context(nc.semaphore(name))

    x = sb("x", [P, TB, D])
    z = sb("z", [P, TB, D])
    xh = sb("xh", [P, KC, S], F32R)
    xl = sb("xl", [P, KC, S], F32R)
    st = ExitStack()
    btab = sb("btab", [P, 8, 512], F32, st)
    st.close()
    st = ExitStack()
    gs = sb("gs", [P, 8, 512], F32, st)
    st.close()
    oh = sb("oh", [P, KC, S], F32R)
    ol = sb("ol", [P, KC, S], F32R)
    raw = sb("raw", [P, RAW, TILE])
    wh = sb("wh", [P, PARTS, TILE], F32R)
    wl = sb("wl", [P, PARTS, TILE], F32R)
    gb = sb("gb", [P, 2, D])
    ident = sb("ident", [P, P])
    ones = sb("ones", [P, P])
    prob = sb("prob", [P, 2, 512])
    probT = sb("probT", [P, 2, 512])
    logit = sb("logit", [P, 2, 512])
    pc = sb("pc", [P, P])
    stat = sb("stat", [P, TB, 4, 6])
    mv = sb("mv", [P, TB, 4])
    bm = sb("bm", [P, 2, 512])
    nmax = sb("nmax", [P, 2, 4])
    psum_e = sb("psum_e", [P, 2, 4])
    rden = sb("rden", [P, 2, 4])

    st = ExitStack()
    hh = sb("hh", [P, HC, S], F32R, st)
    hl = sb("hl", [P, HC, S], F32R, st)
    gate_s = sb("gate_s", [P, 2, 512], F32, st)
    hid = sb("hid", [P, 2, 512], F32, st)
    st.close()
    st = ExitStack()
    mh = sb("mh", [P, KC, S], F32R, st)
    ml = sb("ml", [P, KC, S], F32R, st)
    mem_n = sb("mem_n", [P, TB, D], F32, st)
    xq = sb("xq", [P, KC, S], F32, st)
    xk = sb("xk", [P, KC, S], F32, st)
    xv = sb("xv", [P, TB, D], F32, st)
    st.close()
    st = ExitStack()
    ec = sb("ec", [P, 768], F32, st)
    qkT = sb("qkT", [P, KC, S], F32, st)
    cpad = sb("cpad", [P, KC, S + 4], F32, st)
    av = sb("av", [P, TB, 4, 130], F32, st)
    ao = sb("ao", [P, 4, S], F32, st)
    bq = sb("bq", [P, 4, S], F32, st)
    bk = sb("bk", [P, 4, S], F32, st)
    bv = sb("bv", [P, TB, 512], F32, st)
    pk = sb("pk", [P, 2, 4, P], F32, st)
    cn = sb("cn", [P, 2, 4, 130], F32, st)
    gt = sb("gt", [P, 2, 16], F32, st)
    gbias = sb("gbias", [P, 16], F32, st)
    lf = sb("lf", [P, 4, TB, 8], F32, st)
    bs = sb("bs", [P, 32], F32, st)
    cc_ = sb("cc_", [P, TB, 8], F32, st)
    mm_ = sb("mm_", [P, 10, 2, 2, 4], F32, st)
    prow = sb("prow", [P, P], F32, st)
    boneh = sb("boneh", [P, 512], F32, st)
    brel0 = sb("brel0", [BUCKETS, 8], F32, st)
    rpad = sb("rpad", [64, 2, 7, P], F32, st)
    st.close()
    st = ExitStack()
    pad_a = sb("pad_a", [P, 768 + KC * S], F32, st)
    cm = sb("cm", [P, 2, 2, 4, P], F32, st)
    st.close()
    st = ExitStack()
    oc = sb("oc", [P, 640], F32, st)
    rq = sb("rq", [P, 16, S], F32, st)
    rt = sb("rt", [P, 3, 512], F32, st)
    rs = sb("rs", [P, 2, 512], F32, st)
    dv = sb("dv", [P, TB, D], F32, st)
    lamt = sb("lamt", [P, 4, 64], F32, st)
    lam = sb("lam", [P, 8], F32, st)
    on = sb("on", [P, 8, TB, P], F32, st)
    osq = sb("osq", [P, 2, TB * P], F32, st)
    oss = sb("oss", [P, 3, 8 * TB], F32, st)
    st.close()
    st = ExitStack()
    sc_ = sb("sc_", [P, 1536], F32, st)
    tge = sb("tge", [P, P], F32, st)
    qaT = sb("qaT", [P, 4, S], F32, st)
    iqT = sb("iqT", [P, 4, S], F32, st)
    ikT = sb("ikT", [P, S], F32, st)
    ckn = sb("ckn", [P, TB, P], F32, st)
    ckT = sb("ckT", [P, S], F32, st)
    iw = sb("iw", [P, TB, 8], F32, st)
    uk = sb("uk", [P, 4, P], F32, st)
    uv = sb("uv", [P, 8, 64], F32, st)
    ql = sb("ql", [P, 2, S], F32, st)
    vs = sb("vs", [P, TB, 512], F32, st)
    top8 = sb("top8", [P, 8], F32, st)
    selm = sb("selm", [P, TB, S], F32, st)
    zc = sb("zc", [P, 2, S + 2], F32, st)
    gth = sb("gth", [P, 2, 384], F32, st)
    olat = sb("olat", [P, 2, S], F32, st)
    yh = sb("yh", [P, 12, S], F32R, st)
    yl = sb("yl", [P, 12, S], F32R, st)
    cks = sb("cks", [P, 4], F32, st)
    st.close()

    def bias_of(g):
        return cm[:, :, :, :, :].rearrange("p d t h l -> p (d t) (h l)")[:, g - 2, :] if 2 <= g < 6 else bm[:, g % 2, :]

    score = bm[:, 0, :].rearrange("p (t s) -> p t s", t=TB)
    cksq = bm[:, 1, 0:2 * P].rearrange("p (t c) -> p t c", t=TB)
    qsT = z[:, 0, :].rearrange("p (c s) -> p c s", c=4)
    ksT = z[:, 1, :].rearrange("p (c s) -> p c s", c=4)
    smT = z[:, :, :].rearrange("p a (b h l) -> p a b h l", b=2, h=4)

    rpb_d = nc.dram_tensor("rpb_rows", [64, 8 * 7 * P], F32, kind="Internal").ap()
    bias_d = nc.dram_tensor("bias_rows", [P, 8 * 512], F32, kind="Internal").ap()

    ps = [ctx.enter_context(nc.psum_tensor(f"bank{b}", [P, 512], F32)) for b in range(8)]
    bank_full = [sem(f"bank_full{b}") for b in range(8)]
    bank_free = [sem(f"bank_free{b}") for b in range(8)]
    raw_full = [sem(f"raw_full{r}") for r in range(RAW)]
    out_stored = sem("out_stored")
    named = {}

    def sig(name):
        if name not in named:
            named[name] = sem(name)
        return named[name]

    weight_tiles = []
    where = {}
    uses = [0] * 8
    given = [0] * 8
    turn = {"acc": 0, "work": 0}
    halves = {}

    def result(name):
        b, n, _, _ = where[name]
        return ps[b], b, n

    SUB = []
    for layer in range(2):
        for kind in (("even", "odd")[layer], "cross", "ffn"):
            SUB.append((kind, 1, layer, 0))
    for layer in range(2):
        for kind, which in (("ffn", 0), ("merge", 0), ("cross", 0), ("ffn", 1)):
            SUB.append((kind, 2, layer, which))

    FILLERS = (("conv", 0), ("conv", 1), ("conv", 2), ("gate", 0), ("conv", 3), ("conv", 4), ("conv", 5), ("gate", 1))
    LATENT_GATES = {0: 2, 1: 3, 3: 4, 5: 5, 8: 6, 9: 7}
    BRANCHES = (1, 2, 0)

    ROPE_ORDER = (0, 4, 1, 5, 2, 6, 3, 7)

    def open_gate(k):
        return gs[:, k // 2 + 4 * (k % 2), :] if k < 8 else prob[:, k % 2, :]

    def ffn_weights(block_no, layer, which):
        if block_no == 1:
            return A["ffn_w_gu"][layer], A["ffn_w_down"][layer]
        return A["ffn_w_in_2"][layer, which], A["ffn_w_out_2"][layer, which]

    def norm_of(j):
        kind, blk, layer, which = SUB[j]
        if blk == 1:
            return A["ln_g"][layer, j % 3], A["ln_b"][layer, j % 3], 1.0
        n = (j - 6) % 4
        return A["ln_g_2"][layer, n], A["ln_b_2"][layer, n], 0.5 if kind == "ffn" else 1.0

    def cross_of(blk, layer):
        if blk == 1:
            return A["mem"][0], A["mem_wq"][layer], A["mem_wkv"][layer], A["mem_wo"][layer], 2
        return A["mem_2"][0], A["xa_wq_2"][layer], A["xa_wkv_2"][layer], A["xa_wo_2"][layer], 1

    def cross_after(j):
        return j + 1 < LAST and SUB[j + 1][0] == "cross"

    half_names, copies, in_banks, mem_start = [], [], [], {}

    def await_halves(eng, n):
        eng.wait_ge(sig("part_high"), n)
        b, _, _, freed = where[half_names[n - 1]] if in_banks[n - 1] else (None,) * 4
        if in_banks[n - 1]:
            eng.wait_ge(bank_free[b], freed)
        else:
            eng.wait_ge(sig("part_low"), copies[n - 1])

    block = ctx.enter_context(nc.Block())

    @block.tensor
    def _(pe):
        owed = [0]
        counted = [0]

        def mm(o, a, b, start, stop, full=None, transpose=False):
            ins = pe.transpose(o, a, b) if transpose else pe.matmul(o, a, b, start=start, stop=stop)
            if full is not None:
                bank = where[full][0]
                where[full][2] = min(len(weight_tiles) - 1, counted[0])
                ins.then_inc(bank_full[bank], 1)
            elif owed[0]:
                ins.then_inc(sig("weights_used"), owed[0])
                counted[0] += owed[0]
                owed[0] = 0

        def take(name, ring="work"):
            b = turn[ring] % 4 + (4 if ring == "work" else 0)
            turn[ring] += 1
            if given[b]:
                pe.wait_ge(bank_free[b], given[b])
            given[b] += 1
            uses[b] += 1
            assert name not in where, name
            where[name] = [b, uses[b], 0, given[b]]
            return ps[b]

        def await_read(*names):
            for name in names:
                pe.wait_ge(bank_free[where[name][0]], where[name][3])

        def weights(pieces, nk):
            n = len(weight_tiles)
            w = sum(piece.shape[-1] for piece in pieces)
            weight_tiles.append((pieces, nk, w))
            pe.wait_ge(sig("w_high"), n + 1)
            pe.wait_ge(sig("w_low"), n + 1)
            s = n % PARTS
            return (wh[:, s, 0:nk * w].rearrange("p (k c) -> p k c", k=nk),
                    wl[:, s, 0:nk * w].rearrange("p (k c) -> p k c", k=nk))

        def three(o, ah, al, bh, bl, first, last, full=None):
            mm(o, ah, bl, first, False)
            mm(o, al, bh, False, False)
            mm(o, ah, bh, False, last, full)

        def parts(name, in_bank=True):
            halves[name] = len(halves)
            half_names.append(name)
            copies.append((copies[-1] if copies else 0) + (not in_bank))
            in_banks.append(in_bank)

        def await_parts(n=None):
            await_halves(pe, len(halves) if n is None else n)

        def proj_T(name, pieces, nk, sh, sl, k0=0, ring="work", entry=False):
            h, l = weights(pieces, nk)
            o = take(name, ring)
            for m in range(2):
                for k in range(nk):
                    if entry and m == 0 and k % 4 == 0:
                        await_parts(len(halves) - 1 + k // 4)
                    c = slice(m * P, m * P + P)
                    three(o[:, m * S:m * S + S], h[:, k, c], l[:, k, c], sh[:, k0 + k, :], sl[:, k0 + k, :],
                          k == 0, k == nk - 1, name if m == 1 and k == nk - 1 else None)
            owed[0] += 1

        def proj_N(names, W, c0, width, k_total, sh, sl, steps=None, ring="work", entry=False):
            per = min(TILE // width, k_total)
            for k0 in steps or range(0, k_total, per):
                nk = min(per, k_total - k0)
                if k0 == 0:
                    for name in names:
                        take(name, ring)
                o = [ps[where[name][0]] for name in names]
                h, l = weights([W[k0 * P:(k0 + nk) * P, c0:c0 + width]], nk)
                for t in range(TB):
                    if entry:
                        await_parts(len(halves) - 2 + 2 * t)
                    for k in range(nk):
                        tok = slice(t * P, t * P + P)
                        last = k0 + k == k_total - 1
                        three(o[t][:, 0:width], sh[:, k0 + k, tok], sl[:, k0 + k, tok], h[:, k, :], l[:, k, :],
                              k0 + k == 0, last, names[t] if last else None)
                owed[0] += 1

        def to_T(name, src, ring="work"):
            o = take(name, ring)
            for c in range(4):
                mm(o[:, c * P:c * P + P], src[:, c * P:c * P + P], ident[:, :], True, True,
                   name if c == 3 else None, transpose=True)

        def x_to_T(i, blocks=range(TB)):
            for t in blocks:
                if i == 0:
                    pe.wait_ge(sig("x_loaded"), 16)
                for half in range(2):
                    if i:
                        pe.wait_ge(sig("x_ready"), 4 * (i - 1) + 2 * t + half + 1)
                    to_T(("xT", i, t, half), x[:, t, half * 512:half * 512 + 512])
                    parts(("xT", i, t, half))

        def mem_to_T(j):
            mem_no[0] += 1
            pe.wait_ge(sig("mem_loaded"), 16 * mem_no[0])
            for t in range(TB):
                for half in range(2):
                    to_T(("memT", j, t, half), mem_n[:, t, half * 512:half * 512 + 512])
                    parts(("memT", j, t, half))

        def y_tile(j, W, half, k0, kc):
            if k0 == 0:
                for t in range(TB):
                    take(("y", j, t, half), "acc")
            return weights([W[k0 * P:min(k0 + 4, kc) * P, half * 512:half * 512 + 512]], min(4, kc - k0))

        def y_products(j, t, half, k0, kc, sh, sl, tile):
            h, l = tile
            name = ("y", j, t, half)
            o = ps[where[name][0]]
            for k in range(k0, min(k0 + 4, kc)):
                tok = slice(t * P, t * P + P)
                three(o[:, :], sh[:, k, tok], sl[:, k, tok], h[:, k - k0, :], l[:, k - k0, :], k == 0, k == kc - 1,
                      name if k == kc - 1 else None)

        def y_step(j, W, half, k0, kc, sh, sl):
            tile = y_tile(j, W, half, k0, kc)
            for t in range(TB):
                y_products(j, t, half, k0, kc, sh, sl, tile)
            owed[0] += 1

        def out_proj(j, W, kc, sh, sl, need=None, steps=None):
            if steps is None:
                steps = [(half, k0) for half in range(2) for k0 in range(0, kc, 4)]
            held = 0 if cross_after(j) else min(PARTS, len(steps))
            for half, k0 in steps[:len(steps) - held]:
                if need:
                    need(min(k0 + 4, kc))
                y_step(j, W, half, k0, kc, sh, sl)
                if half == 0 and k0 + 4 >= kc and cross_after(j):
                    mem_start[j + 1] = len(halves)
                    mem_to_T(j + 1)
            tiles = []
            for half, k0 in steps[len(steps) - held:]:
                if need:
                    need(min(k0 + 4, kc))
                tiles.append(y_tile(j, W, half, k0, kc))
                y_products(j, 0, half, k0, kc, sh, sl, tiles[-1])
            for i, (half, k0) in enumerate(steps[len(steps) - held:]):
                if i == held - 1 and j + 1 < LAST:
                    x_to_T(j + 1, [0])
                y_products(j, 1, half, k0, kc, sh, sl, tiles[i])
                owed[0] += 1
            if cross_after(j):
                cross_kv(j + 1)
            elif j + 1 < LAST:
                x_to_T(j + 1, [1])

        def gate_tile(l_, k):
            n, i = k // 3, BRANCHES[k % 3]
            c0 = 4296 + 1024 * i + n * S
            proj_T(("bgate", l_, n, i), [A["w_mix_in_2"][l_][:, c0:c0 + S]], KC, xh, xl)

        def conv_tile(l_, i):
            what, c0 = (("cc", 3272), ("ch", 3784), ("cb", 2760))[i % 3]
            n = i // 3
            proj_T((what, l_, n), [A["w_mix_in_2"][l_][:, c0 + n * S:c0 + n * S + S]], KC, xh, xl)
            if what == "cb":
                parts(("yc", l_, n), in_bank=False)

        def filler(l_, i):
            what, number = FILLERS[i]
            (conv_tile if what == "conv" else gate_tile)(l_, number)

        def cross_kv(j):
            _, blk, layer, _ = SUB[j]
            _, _, wkv, _, c = cross_of(blk, layer)
            await_parts()
            for n in range(2 * c):
                proj_T(("xk", j, n), [wkv[:, n * S:n * S + S]], KC, mh, ml)
            for half in range(c):
                for k0 in (0, 4):
                    if k0 and half == c - 1:
                        x_to_T(j)
                    proj_N([("xv", j, t, half) for t in range(TB)], wkv, 512 * c + half * 512, 512, KC, mh, ml, [k0],
                           "acc" if half == c - 1 else "work")

        def transposed_probs(u, src):
            pe.wait_ge(sig("prob_ready"), unit[0] + u + 1)
            name = ("T", unit[0] + u)
            o = take(name)
            for kb in range(TB):
                for t in range(TB):
                    mm(o[:, kb * S + t * P:kb * S + t * P + P], src(t, kb), ident[:, :], True, True,
                       name if kb == 1 and t == 1 else None, transpose=True)

        def cross(j):
            _, blk, layer, _ = SUB[j]
            _, wq, _, wo, c = cross_of(blk, layer)
            await_parts()
            for n in range(c):
                proj_T(("xq", j, n), [wq[:, n * S:n * S + S]], KC, xh, xl)
            await_read(*[("xk", j, n) for n in range(2 * c)])
            await_read(*[("xv", j, t, half) for t in range(TB) for half in range(c)])
            base = len(halves)
            steps = [(half, k0) for k0 in range(0, 4 * c, 4) for half in range(2)]
            for t in range(4 + 3):
                if 2 <= t < 6:
                    u = t - 2
                    transposed_probs(u, lambda tb, kb: prob[:, u % 2, tb * S + kb * P:tb * S + kb * P + P])
                if t < 4:
                    await_read(("xq", j, t if c == 2 else t // 2))
                    o = take(("S", unit[0] + t))
                    for tb in range(TB):
                        for i in range(c):
                            mm(o[:, tb * S:tb * S + S], xq[:, c * t + i, tb * P:tb * P + P], xk[:, c * t + i, :],
                               i == 0, i == c - 1, ("S", unit[0] + t) if tb == 1 and i == c - 1 else None)
                if t < c:
                    proj_T(("xq", j, t + c), [wq[:, (t + c) * S:(t + c + 1) * S]], KC, xh, xl)
                if c == 2 and t == 5:
                    await_parts(base + 2)
                    y_step(j, wo, *steps[0], 4 * c, oh, ol)
                if t >= 3:
                    u = t - 3
                    await_read(("T", unit[0] + u))
                    o = take(("O", unit[0] + u), "work" if c == 2 and u >= 2 else "acc")
                    for i in range(c):
                        for kb in range(TB):
                            mm(o[:, i * S:i * S + S], xv[:, kb, (c * u + i) * P:(c * u + i + 1) * P],
                               probT[:, u % 2, kb * S:kb * S + S], kb == 0, kb == 1,
                               ("O", unit[0] + u) if i == c - 1 and kb == 1 else None)
                    parts(("O", unit[0] + u))
            unit[0] += 4
            out_proj(j, wo, 4 * c, oh, ol, steps=steps[c - 1:], need=lambda k: await_parts(base + k // c))

        def ffn(j):
            _, blk, layer, which = SUB[j]
            wgu, wdown = ffn_weights(blk, layer, which)
            base = len(halves)
            for q in range(HC // 2):
                proj_T(("gate", j, q), [wgu[:, q * S:q * S + S]], KC, xh, xl, entry=q == 0)
                proj_T(("up", j, q), [wgu[:, FFN + q * S:FFN + q * S + S]], KC, xh, xl)
                parts(("hid", j, q), in_bank=False)
            out_proj(j, wdown, HC, hh, hl, need=lambda k: await_parts(base + (k + 1) // 2))

        def even(j):
            W = A["even_w_in"][0]
            await_parts()
            h, l = weights([W[:, 2048:2064]], KC)
            o = take("gates")
            for t in range(TB):
                for k in range(KC):
                    tok = slice(t * P, t * P + P)
                    three(o[:, t * 16:t * 16 + 16], xh[:, k, tok], xl[:, k, tok], h[:, k, :], l[:, k, :],
                          k == 0, k == KC - 1, "gates" if t == 1 and k == KC - 1 else None)
            owed[0] += 1
            for n in range(4):
                proj_T(("aqk", n), [W[:, n * S:n * S + S]], KC, xh, xl)
                if n == 0:
                    pe.wait_ge(sig("rows_loaded"), 16 * 5)
                    o = take("cols")
                    mm(o[:, 0:N_ROWS], prow[0:N_ROWS, :], ident[0:N_ROWS, 0:N_ROWS], True, True, "cols", transpose=True)
            proj_N([("av", t) for t in range(TB)], W, 1024, 512, KC, xh, xl)
            pe.wait_ge(sig("rel_loaded"), 32)
            for hd in range(8):
                o = take(("tab", hd), "acc")
                mm(o[:, :], brel0[:, hd:hd + 1].broadcast_to([BUCKETS, P]), boneh[0:BUCKETS, :], True, True,
                   ("tab", hd))
            for n in range(2):
                proj_T(("ao", n), [W[:, 1536 + n * S:1536 + n * S + S]], KC, xh, xl)

            def bq_tile(n):
                proj_T(("bq", n), [W[:, 2064 + n * S:2064 + n * S + S]], KC, xh, xl)

            def bk_tile(n):
                proj_T(("bk", n), [W[:, 2576 + n * S:2576 + n * S + S]], KC, xh, xl)

            bq_tile(0)
            bk_tile(0)
            proj_N([("bv", t) for t in range(TB)], W, 3088, 512, KC, xh, xl)

            pe.wait_ge(sig("ones_set"), 1)
            pe.wait_ge(sig("even_loaded"), 32)
            pe.wait_ge(sig("logf_ready"), 1)
            o = take("cum")
            for t in range(TB):
                mm(o[:, t * 8:t * 8 + 4], tri_le, lf[:, 3, t, 0:4], True, True)
                mm(o[:, t * 8 + 4:t * 8 + 8], tri_ge, lf[:, 3, t, 4:8], True, True)
                mm(o[:, 16 + t * 8:24 + t * 8], ones[:, :], lf[:, 3, t, :], True, True, "cum" if t == 1 else None)
            pe.wait_ge(sig("decay_cols"), 1)
            for d in range(2):
                for t in range(TB):
                    o = take(("C", d, t))
                    for hd in range(4):
                        mm(o[:, hd * P:hd * P + P], cc_[:, t, d * 4 + hd:d * 4 + hd + 1].broadcast_to([P, P]),
                           ident[:, :], True, True, ("C", d, t) if hd == 3 else None)
            pe.wait_ge(sig("qk_ready"), 1)
            for t in range(TB):
                o = take(("QK", t), "acc")
                for hd in range(4):
                    mm(o[:, hd * P:hd * P + P], qkT[:, hd, t * P:t * P + P], qkT[:, 4 + hd, t * P:t * P + P],
                       True, True, ("QK", t) if hd == 3 else None)
            for d in range(2):
                o = take(("kN", d))
                for hd in range(4):
                    mm(o[:, hd * P:hd * P + P], qkT[:, 4 + hd, d * P:d * P + P], ident[:, :], True, True,
                       ("kN", d) if hd == 3 else None, transpose=True)
            bq_tile(1)
            pe.wait_ge(sig("av_ones"), 1)
            await_read(("av", 0), ("av", 1))
            for d in range(2):
                await_read(("kN", d))
                for half in range(2):
                    o = take(("KV", d, half))
                    for i in range(2):
                        hd = half * 2 + i
                        mm(o[:, i * 130:i * 130 + 130], pk[:, d, hd, :], av[:, d, hd, :], True, True,
                           ("KV", d, half) if i == 1 else None)
            for t in range(TB):
                for d in range(2):
                    pe.wait_ge(sig("decayed"), 2 * t + d + 1)
                    o = take(("ST", d, t))
                    for hd in range(4):
                        mm(o[:, hd * P:hd * P + P], cm[:, d, t, hd, :], ident[:, :], True, True,
                           ("ST", d, t) if hd == 3 else None, transpose=True)
            for d in range(2):
                for half in range(2):
                    await_read(("KV", d, half))
                    o = take(("int", d, half))
                    for i in range(2):
                        hd = half * 2 + i
                        t2 = 1 - d
                        mm(o[:, i * 130:i * 130 + 130], qkT[:, hd, t2 * P:t2 * P + P], cn[:, d, hd, :], True, True,
                           ("int", d, half) if i == 1 else None)
            for t in range(TB):
                for d in range(2):
                    await_read(("ST", d, t))
                    o = take(("num", d, t), "acc")
                    for hd in range(4):
                        mm(o[:, hd * P:hd * P + P], smT[:, d, t, hd, :], av[:, t, hd, 0:P], True, True,
                           ("num", d, t) if hd == 3 else None)
            bk_tile(1)
            await_read(("bq", 0), ("bq", 1), ("bk", 0), ("bv", 0), ("bv", 1))

            def score(u):
                r = slice(64 * (u % 2), 64 * (u % 2) + 64)
                o = take(("S", unit[0] + u))
                for tb in range(TB):
                    mm(o[:, tb * S:tb * S + S], bq[r, u // 2, tb * P:tb * P + P], bk[r, u // 2, :], True, True,
                       ("S", unit[0] + u) if tb == 1 else None)

            for t in range(TB):
                pe.wait_ge(sig("mlstm_out"), t + 1)
                to_T(("hT", t), logit[:, t, :])
                parts(("aT", t), in_bank=False)
            mlstm_parts = len(halves)
            for t in range(8 + 3):
                if 2 <= t < 10:
                    u = t - 2
                    transposed_probs(u, lambda tb, kb: prob[:, u % 2, tb * S + kb * P:tb * S + kb * P + P])
                if t >= 3:
                    u = t - 3
                    await_read(("T", unit[0] + u))
                    heads_out(("O", unit[0] + u - u % 2), u, lambda kb: bv[:, kb, u * 64:u * 64 + 64],
                              lambda kb: probT[:, u % 2, kb * S:kb * S + S], "work")
                if t == 4:
                    await_read(("bk", 1))
                if t < 8:
                    score(t)
                if t in (1, 3):
                    await_parts(mlstm_parts)
                    y_step(j, A["even_w_out"][0], t // 2, 0, KC, oh, ol)
            unit[0] += 8
            await_parts()
            out_proj(j, A["even_w_out"][0], KC, oh, ol, steps=[(0, 4), (1, 4)])

        def heads_out(name, u, v_of, p_of, ring="acc"):
            o = take(name, ring) if u % 2 == 0 else ps[where[name][0]]
            r = slice(64 * (u % 2), 64 * (u % 2) + 64)
            for kb in range(TB):
                mm(o[r, 0:S], v_of(kb), p_of(kb), kb == 0, kb == 1, name if u % 2 and kb == 1 else None)
            if u % 2:
                parts(name)

        def odd(j):
            W = A["odd_w_in"][0]
            wo = A["odd_w_out"][0]

            def rope_tile(i):
                n = ROPE_ORDER[i]
                proj_T(("rp", i), [W[:, n * S:n * S + S]], KC, xh, xl, entry=i == 0)

            def rotate(i):
                await_read(("rp", i))
                if i == 0:
                    pe.wait_ge(sig("odd_loaded"), 16)
                o = take(("rot", i), "acc")
                mm(o[:, :], oc[:, 0:P], rs[:, i % 2, :], True, True, ("rot", i))

            def values(half, steps=None):
                proj_N([("dv", t, half) for t in range(TB)], W, 2048 + half * 512, 512, KC, xh, xl, steps,
                       ("work", "acc")[half])

            def normed_to_T(units):
                for u in units:
                    pe.wait_ge(sig("diff_normed"), u + 1)
                    o = take(("OT", u))
                    for tb in range(TB):
                        mm(o[:, tb * P:tb * P + P], on[:, u, tb, :], ident[:, :], True, True,
                           ("OT", u) if tb == 1 else None, transpose=True)
                    parts(("OT", u), in_bank=False)

            rope_tile(0)
            rope_tile(1)
            rotate(0)
            rope_tile(2)
            rotate(1)
            values(0)
            for t in range(8 + 3):
                if 2 <= t < 10:
                    u = t - 2
                    buf = (prob, logit)[u % 2]
                    transposed_probs(u, lambda tb, kb: buf[:, 0, tb * S + kb * P:tb * S + kb * P + P])
                if t + 2 < 8:
                    rotate(t + 2)
                if t < 8:
                    pe.wait_ge(sig("rope_done"), 2 * (t // 2) + 2)
                    for c in range(2):
                        r = slice(64 * c, 64 * c + 64)
                        o = take(("S", unit[0] + t, c))
                        for tb in range(TB):
                            mm(o[:, tb * S:tb * S + S], rq[r, t, tb * P:tb * P + P], rq[r, 8 + t, :], True, True,
                               ("S", unit[0] + t, c) if tb == 1 else None)
                if t + 3 < 8:
                    rope_tile(t + 3)
                elif t + 3 < 10:
                    values(1, [4 * (t - 5)])
                if t >= 3:
                    u = t - 3
                    await_read(("T", unit[0] + u), ("dv", 0, u // 4), ("dv", 1, u // 4))
                    o = take(("O", unit[0] + u), "acc")
                    for tb in range(TB):
                        for kb in range(TB):
                            mm(o[:, tb * P:tb * P + P], probT[:, u % 2, kb * S + tb * P:kb * S + tb * P + P],
                               dv[:, kb, u * P:u * P + P], kb == 0, kb == 1,
                               ("O", unit[0] + u) if tb == 1 and kb == 1 else None)
                if t in (8, 9):
                    normed_to_T(range(2 * t - 16, 2 * t - 14))
            await_parts()
            y_step(j, wo, 0, 0, KC, oh, ol)
            normed_to_T(range(4, 8))
            y_step(j, wo, 1, 0, KC, oh, ol)
            unit[0] += 8
            await_parts()
            out_proj(j, wo, KC, oh, ol, steps=[(0, 4), (1, 4)])

        def merge(j):
            _, _, l_, _ = SUB[j]
            W = A["w_mix_in_2"][l_]
            proj_N([("ckv", l_, t) for t in range(TB)], W, 512, P, KC, xh, xl, entry=True)
            h, l = weights([W[:, 1152:1216], W[:, 1152:1216], W[:, 1216:1224]], KC)
            o = take(("ik", l_))
            for k in range(KC):
                three(o[:, 0:S], h[:, k, 0:P], l[:, k, 0:P], xh[:, k, :], xl[:, k, :], k == 0, k == KC - 1,
                      ("ik", l_) if k == KC - 1 else None)
            o = take(("iw", l_))
            for t in range(TB):
                for k in range(KC):
                    tok = slice(t * P, t * P + P)
                    three(o[:, t * 8:t * 8 + 8], xh[:, k, tok], xl[:, k, tok], h[:, k, P:P + 8], l[:, k, P:P + 8],
                          k == 0, k == KC - 1, ("iw", l_) if t == 1 and k == KC - 1 else None)
            owed[0] += 1
            for n in range(2):
                proj_T(("iq", l_, n), [W[:, 640 + n * S:640 + n * S + S]], KC, xh, xl)
            pe.wait_ge(sig("ckv_normed"), 2 * (l_ + 1))
            o = take(("ckT", l_))
            for t in range(TB):
                mm(o[:, t * P:t * P + P], ckn[:, t, :], ident[:, :], True, True, ("ckT", l_) if t == 1 else None,
                   transpose=True)
            await_read(("ik", l_), ("iq", l_, 0), ("iq", l_, 1))
            for u in range(8):
                r = slice(64 * (u % 2), 64 * (u % 2) + 64)
                o = take(("dot", l_, u))
                for tb in range(TB):
                    mm(o[:, tb * S:tb * S + S], iqT[r, u // 2, tb * P:tb * P + P], ikT[r, :], True, True,
                       ("dot", l_, u) if tb == 1 else None)
            for n in range(2):
                proj_T(("qa", l_, n), [W[:, n * S:n * S + S]], KC, xh, xl)
            for n in range(2):
                proj_T(("qs", l_, n), [W[:, 1224 + n * S:1224 + n * S + S]], KC, xh, xl)
            for n in range(2):
                proj_T(("ks", l_, n), [W[:, 1736 + n * S:1736 + n * S + S]], KC, xh, xl)
            await_read(*[(what, l_, n) for what in ("qs", "ks") for n in range(2)])
            pe.wait_ge(sig("merge_loaded"), 32 * (l_ + 1))
            for pair in range(4 + 1):
                for t in range(2 * pair, min(2 * pair + 2, 8)):
                    r = slice(64 * (t % 2), 64 * (t % 2) + 64)
                    o = take(("z", l_, t))
                    for kb in range(TB):
                        mm(o[:, kb * S:kb * S + S], ksT[r, t // 2, kb * P:kb * P + P], qsT[r, t // 2, :], True, True,
                           ("z", l_, t) if kb == 1 else None)
                if pair == 0:
                    proj_N([("vs", l_, t) for t in range(TB)], W, 2248, 512, KC, xh, xl)
                else:
                    await_read(("vs", l_, 0), ("vs", l_, 1))
                    pe.wait_ge(sig("stick_probs"), 4 * l_ + pair)
                    for u in (2 * pair - 2, 2 * pair - 1):
                        heads_out(("yb", l_, pair - 1), u, lambda kb: vs[:, kb, u * 64:u * 64 + 64],
                                  lambda kb: probT[:, u % 2, kb * S:kb * S + S])
                if pair < 4:
                    filler(l_, 2 * pair)
                    for u in (2 * pair, 2 * pair + 1):
                        pe.wait_ge(sig("softplus_masked"), 8 * l_ + u + 1)
                        o = take(("later", l_, u))
                        sp = prob[:, u % 2, :]
                        mm(o[:, 0:S], tge[:, :], sp[:, 0:S], True, False)
                        mm(o[:, 0:S], ones[:, :], sp[:, S:2 * S], False, True)
                        mm(o[:, S:2 * S], tge[:, :], sp[:, S:2 * S], True, True, ("later", l_, u))
                    filler(l_, 2 * pair + 1)
            await_read(("qa", l_, 0), ("qa", l_, 1), ("ckT", l_))
            pe.wait_ge(sig("latent_weights"), 32 * (l_ + 1))
            pe.wait_ge(sig("merge_loaded"), 32 * (l_ + 1))
            stick_parts = len(halves)
            for t in range(-1, 8 + 4):
                if 2 <= t < 10:
                    u = t - 2
                    transposed_probs(u, lambda tb, kb: prob[:, u % 2, tb * S + kb * P:tb * S + kb * P + P])
                if 0 <= t < 8:
                    await_read(("ql", l_, t))
                    o = take(("S", unit[0] + t))
                    for tb in range(TB):
                        mm(o[:, tb * S:tb * S + S], ql[:, t % 2, tb * P:tb * P + P], ckT[:, :], True, True,
                           ("S", unit[0] + t) if tb == 1 else None)
                if t + 1 < 8:
                    u = t + 1
                    r = slice(64 * (u % 2), 64 * (u % 2) + 64)
                    o = take(("ql", l_, u))
                    mm(o[:, 0:S], uk[r, u // 2, :], qaT[r, u // 2, :], True, True, ("ql", l_, u))
                if 3 <= t <= 10:
                    u = t - 3
                    await_read(("T", unit[0] + u))
                    o = take(("lat", l_, u), "acc")
                    for kb in range(TB):
                        mm(o[:, 0:S], ckn[:, kb, :], probT[:, u % 2, kb * S:kb * S + S], kb == 0, kb == 1,
                           ("lat", l_, u) if kb == 1 else None)
                if t >= 4:
                    u = t - 4
                    await_read(("lat", l_, u))
                    name = ("ya", l_, u // 2)
                    o = take(name, "acc") if u % 2 == 0 else ps[where[name][0]]
                    mm(o[64 * (u % 2):64 * (u % 2) + 64, 0:S], uv[:, u, :], olat[:, u % 2, :], True, True,
                       name if u % 2 else None)
                    if u % 2:
                        parts(name)
                if t in LATENT_GATES:
                    gate_tile(l_, LATENT_GATES[t])
            unit[0] += 8
            base = len(halves)
            for n in range(4):
                for pos, i in enumerate(BRANCHES):
                    if 3 * n + pos >= 8:
                        gate_tile(l_, 3 * n + pos)
                    if n == 0:
                        await_parts(base if i == 0 else stick_parts)
                    proj_T(("branch", l_, n, i), [A["w_branch_2"][l_, i][:, n * S:n * S + S]], 4, yh, yl, k0=4 * i)
                parts(("merged", l_, n), in_bank=False)
            wo = A["w_mix_out_2"][l_]
            await_parts(base + 2)
            y_step(j, wo, 0, 0, KC, oh, ol)
            y_step(j, wo, 1, 0, KC, oh, ol)
            await_parts()
            out_proj(j, wo, KC, oh, ol, steps=[(0, 4), (1, 4)])

        unit = [0]
        mem_no = [0]
        tri_le, tri_ge = ec[:, 0:P], ec[:, P:2 * P]

        pe.wait_ge(sig("ident_loaded"), 16)
        x_to_T(0)
        program_of = {"even": even, "odd": odd, "merge": merge, "cross": cross, "ffn": ffn}
        for j, (kind, _, _, _) in enumerate(SUB[:LAST]):
            program_of[kind](j)

    raw_done = []
    for n, (pieces, _, _) in enumerate(weight_tiles):
        raw_done.append(16 * len(pieces) + (raw_done[n - RAW] if n >= RAW else 0))

    def raw_tile(n):
        _, nk, w = weight_tiles[n]
        return raw[:, n % RAW, 0:nk * w]

    @block.scalar
    def _(act):
        tile = [0]
        step = [0]
        high_no = [0]
        unit = [0]

        def split_to(n):
            while tile[0] <= min(n, len(weight_tiles) - 1):
                t = tile[0]
                act.wait_ge(raw_full[t % RAW], raw_done[t])
                if t >= PARTS:
                    act.wait_ge(sig("weights_used"), t - PARTS + 1)
                _, nk, w = weight_tiles[t]
                act.activation(wh[:, t % PARTS, 0:nk * w], raw_tile(t), ACT.Copy).then_inc(sig("w_high"), 1)
                tile[0] += 1

        def ahead(name, look=PARTS - 1):
            split_to(where[name][2] + look)

        def get(name, look=PARTS - 1):
            b, n, _, _ = where[name]
            ahead(name, look)
            act.wait_ge(bank_full[b], n)
            return ps[b]

        def await_read(name):
            act.wait_ge(bank_free[where[name][0]], where[name][3])

        def free(name, ins):
            ins.then_inc(bank_free[where[name][0]], 1)

        def link(ins):
            step[0] += 1
            ins.then_inc(sig("act_step"), 1)
            act.wait_ge(sig("act_step"), step[0])

        def high(name, dst, src):
            assert halves[name] == high_no[0], name
            high_no[0] += 1
            act.activation(dst, src, ACT.Copy).then_inc(sig("part_high"), 1)

        def wait(name, n):
            act.wait_ge(sig(name), n)

        def quad(ap):
            return ap.rearrange("p (c s) -> p c s", c=4)

        def two(ap):
            return ap.rearrange("p (c s) -> p c s", c=2)

        def x_to_T(i, blocks=range(TB)):
            for t in blocks:
                for half in range(2):
                    o = get(("xT", i, t, half), 1 if i == 0 or len(blocks) < TB else PARTS - 1)
                    high(("xT", i, t, half), xh[:, half * 4:half * 4 + 4, t * P:t * P + P], quad(o[:, :]))

        def norm(j):
            for t in range(TB):
                ahead(("y", j, 1 if cross_after(j) else t, 1))
                wait("var_ready", 2 * j + t + 1)
                act.activation(mv[:, t, 2:3], mv[:, t, 1:2], ACT.Sqrt).then_inc(sig("std_ready"), 1)
                if j + 1 < LAST and not cross_after(j):
                    x_to_T(j + 1, [t])

        def out_proj(j):
            if cross_after(j):
                for t in range(TB):
                    for half in range(2):
                        name = ("memT", j + 1, t, half)
                        high(name, mh[:, half * 4:half * 4 + 4, t * P:t * P + P], quad(get(name)[:, :]))
            norm(j)
            if cross_after(j):
                c = cross_of(SUB[j + 1][1], 0)[4]
                for n in range(2 * c):
                    name = ("xk", j + 1, n)
                    o = get(name)
                    free(name, act.activation(xk[:, 2 * n:2 * n + 2, :], two(o[:, :]), ACT.Copy))
                x_to_T(j + 1)

        def exps(g, src, dst, k0=0):
            for tb in range(TB):
                ins = act.activation(dst[:, tb * S:tb * S + S], src[:, tb * S:tb * S + S], ACT.Exp,
                                     bias=nmax[:, g % 2, k0 + tb:k0 + tb + 1],
                                     accum_out=psum_e[:, g % 2, k0 + tb:k0 + tb + 1])
            return ins

        def probs_T(g):
            name = ("T", g)
            o = get(name)
            free(name, act.activation(probT[:, g % 2, :], o[:, :], ACT.Copy))

        def softmax(n_units, biased, after, beside=None):
            for t in range(n_units + 3):
                if 2 <= t < n_units + 2:
                    probs_T(unit[0] + t - 2)
                if t >= 3 and biased:
                    after(t - 3)
                if t < n_units:
                    g = unit[0] + t
                    if biased:
                        split_to(where[("S", g)][2] + PARTS - 1)
                        src = logit[:, g % 2, :]
                    else:
                        src = get(("S", g))
                    wait("neg_max", g + 1)
                    ins = exps(g, src, prob[:, g % 2, :])
                    if biased:
                        ins.then_inc(sig("exp_done"), 1)
                    else:
                        free(("S", g), ins)
                if beside:
                    beside(t)
                if t >= 3 and not biased:
                    after(t - 3)
            unit[0] += n_units

        def cross(j):
            c = cross_of(SUB[j][1], 0)[4]
            base = unit[0]

            def query(n):
                name = ("xq", j, n)
                o = get(name)
                free(name, act.activation(xq[:, 2 * n:2 * n + 2, :], two(o[:, :]), ACT.Copy,
                                          scale=float((c * P) ** -0.5)))

            def beside(t):
                if t < c:
                    query(t + c)

            def after(u):
                name = ("O", base + u)
                o = get(name)
                high(name, oh[:, c * u:c * u + c, :], o[:, 0:c * S].rearrange("p (c s) -> p c s", c=c))

            for n in range(c):
                query(n)
            softmax(4, False, after, beside)
            out_proj(j)

        def ffn(j):
            for q in range(HC // 2 + 1):
                if q < HC // 2:
                    o = get(("gate", j, q))
                    free(("gate", j, q), act.activation(gate_s[:, q % 2, :], o[:, :], ACT.Silu))
                if q >= 1:
                    ahead(("up", j, q - 1))
                    await_read(("up", j, q - 1))
                    high(("hid", j, q - 1), hh[:, 2 * q - 2:2 * q, :], two(hid[:, (q - 1) % 2, :]))
            out_proj(j)

        def even(j):
            for n in range(4):
                o = get(("aqk", n))
                if n == 0:
                    wait("pads_set", 1)
                free(("aqk", n),
                       act.activation(cpad[:, 2 * n:2 * n + 2, 2:2 + S], two(o[:, :]), ACT.Copy))
            wait("abs_f", 1)
            link(act.activation(lf[:, 1, :, :], lf[:, 0, :, :], ACT.Exp, scale=-1.0))
            act.activation(lf[:, 2, :, :], lf[:, 1, :, :], ACT.Ln, bias=1.0).then_inc(sig("softplus_f"), 1)
            for hd in range(8):
                o = get(("tab", hd))
                free(("tab", hd), act.activation(btab[:, hd, :], o[:, :], ACT.Copy))
            for n in range(2):
                o = get(("ao", n))
                free(("ao", n), act.activation(ao[:, 2 * n:2 * n + 2, :], two(o[:, :]), ACT.Sigmoid))

            def query(n):
                o = get(("bq", n))
                free(("bq", n), act.activation(bq[:, 2 * n:2 * n + 2, :], two(o[:, :]), ACT.Copy, scale=0.125))

            def key(n):
                o = get(("bk", n))
                free(("bk", n), act.activation(bk[:, 2 * n:2 * n + 2, :], two(o[:, :]), ACT.Copy))

            query(0)
            key(0)
            ahead("cum")
            wait("conv_done", 1)
            act.activation(qkT[:, :, :], qkT[:, :, :], ACT.Silu).then_inc(sig("silu_done"), 1)
            wait("decay_exponents", 1)
            act.activation(mm_[:, 7, :, :, :], mm_[:, 7, :, :, :], ACT.Exp).then_inc(sig("mlstm_small"), 1)
            act.activation(mm_[:, 5, :, :, :], mm_[:, 5, :, :, :], ACT.Exp, scale=-1.0).then_inc(sig("mlstm_small"), 1)
            act.activation(mm_[:, 6, :, :, :], mm_[:, 6, :, :, :], ACT.Exp).then_inc(sig("mlstm_small"), 1)
            for t in range(TB):
                for d in range(2):
                    for hd in range(4):
                        ins = act.activation(cm[:, d, t, hd, :], cm[:, d, t, hd, :], ACT.Exp,
                                             bias=mm_[:, 4, d, t, hd:hd + 1])
                    ins.then_inc(sig("decay_ready"), 1)
            query(1)
            for d in range(2):
                for half in range(2):
                    name = ("KV", d, half)
                    o = get(name)
                    free(name,
                           act.activation(cn[:, d, 2 * half:2 * half + 2, :],
                                          o[:, 0:260].rearrange("p (h e) -> p h e", h=2), ACT.Copy))
            for t in range(TB):
                for d in range(2):
                    name = ("ST", d, t)
                    o = get(name)
                    free(name, act.activation(smT[:, d, t, :, :], quad(o[:, :]), ACT.Copy))
            key(1)
            for t in range(TB):
                await_read(("hT", t))
                wait("distances_stored", 16)
                high(("aT", t), oh[:, 0:4, t * P:t * P + P], quad(probT[:, t, :]))
            base = unit[0]

            def after(u):
                if u % 2:
                    name = ("O", base + u - 1)
                    o = get(name)
                    high(name, oh[:, 4 + u // 2, :], o[:, 0:S])

            softmax(8, True, after)
            out_proj(j)

        def odd(j):
            ahead(("rp", 0))
            wait("lam_sums", 1)
            act.activation(lam[:, 2:4], lam[:, 0:2], ACT.Exp).then_inc(sig("lam_exp"), 1)

            def rope_tile(i):
                o = get(("rp", i))
                if i >= 2:
                    wait("rope_done", i - 1)
                free(("rp", i), act.activation(rs[:, i % 2, :], o[:, :], ACT.Copy,
                                               scale=0.125 if ROPE_ORDER[i] < 4 else 1.0))

            def deviations(half):
                wait("diff_var", half + 1)
                v = slice(8 * half, 8 * half + 8)
                act.activation(oss[:, 1, v], oss[:, 0, v], ACT.Sqrt).then_inc(sig("diff_std"), 1)

            def normed(u):
                ahead(("OT", u))
                await_read(("OT", u))
                high(("OT", u), oh[:, u, :], osq[:, u % 2, :])

            def values(half):
                for t in range(TB):
                    name = ("dv", t, half)
                    o = get(name)
                    free(name, act.activation(dv[:, t, half * 512:half * 512 + 512], o[:, :], ACT.Copy))

            for i in range(3):
                rope_tile(i)
            values(0)
            for t in range(8 + 2):
                if t >= 2:
                    probs_T(unit[0] + t - 2)
                if t < 8:
                    g = unit[0] + t
                    for c in range(2):
                        src = get(("S", g, c))
                        wait("neg_max", g + 1)
                        free(("S", g, c), exps(g, src, (prob, logit)[t % 2][:, c, :], k0=2 * c))
                if t + 3 < 8:
                    rope_tile(t + 3)
                if t == 6:
                    values(1)
                if t == 7:
                    ahead(("O", unit[0] + 4))
                    deviations(0)
                if t in (8, 9):
                    normed(2 * t - 16)
                    normed(2 * t - 15)
            ahead(("O", unit[0] + 7))
            deviations(1)
            for u in range(4, 8):
                normed(u)
            unit[0] += 8
            out_proj(j)

        def gate_tile(l_, k):
            n, i = k // 3, BRANCHES[k % 3]
            name = ("bgate", l_, n, i)
            o = get(name)
            if k >= 10:
                await_read(("branch", l_, (k - 2) // 3, BRANCHES[(k - 2) % 3]))
            for m in range(2):
                r = ROWS["b_gate_2"] + (l_ * 3 + i) * 8 + 2 * n + m
                ins = act.activation(open_gate(k)[:, m * S:m * S + S], o[:, m * S:m * S + S],
                                     ACT.Sigmoid if k >= 8 else ACT.Identity, bias=pc[:, r:r + 1])
            free(name, ins)

        def open_gates(l_, ks):
            for k in ks:
                await_read(("bgate", l_, k // 3, BRANCHES[k % 3]))
                act.activation(open_gate(k), open_gate(k), ACT.Sigmoid).then_inc(sig("gates_open"), 1)

        def conv_tile(l_, i):
            n = i // 3
            if i % 3 == 0:
                o = get(("cc", l_, n))
                if n:
                    wait("part_low", copies[halves[("yc", l_, 0)]])
                free(("cc", l_, n), act.activation(bm[:, 1, :], o[:, :], ACT.Copy))
            elif i % 3 == 2:
                get(("cb", l_, n))
                await_read(("cb", l_, n))
                high(("yc", l_, n), yh[:, 8 + 2 * n:10 + 2 * n, :], two(bm[:, 1, :]))

        def filler(l_, i):
            what, number = FILLERS[i]
            (conv_tile if what == "conv" else gate_tile)(l_, number)

        def merge(j):
            l_ = SUB[j][2]
            ahead(("ckv", l_, 1))
            wait("ckv_var", l_ + 1)
            act.activation(cks[:, 2:4], cks[:, 0:2], ACT.Sqrt).then_inc(sig("ckv_std"), 1)
            o = get(("ik", l_))
            free(("ik", l_), act.activation(ikT[:, :], o[:, 0:S], ACT.Copy))
            for n in range(2):
                o = get(("iq", l_, n))
                free(("iq", l_, n),
                       act.activation(iqT[:, 2 * n:2 * n + 2, :], two(o[:, :]), ACT.Copy))
            for u in range(8):
                o = get(("dot", l_, u))
                if u >= 2:
                    wait("scored", 8 * l_ + u - 1)
                free(("dot", l_, u), act.activation(prob[:, u % 2, :], o[:, :], ACT.Relu))
            for n in range(2):
                o = get(("qa", l_, n))
                free(("qa", l_, n),
                       act.activation(qaT[:, 2 * n:2 * n + 2, :], two(o[:, :]), ACT.Copy, scale=0.125))
            for n in range(2):
                o = get(("qs", l_, n))
                free(("qs", l_, n),
                       act.activation(qsT[:, 2 * n:2 * n + 2, :], two(o[:, :]), ACT.Copy, scale=0.125))
            for n in range(2):
                o = get(("ks", l_, n))
                free(("ks", l_, n),
                       act.activation(ksT[:, 2 * n:2 * n + 2, :], two(o[:, :]), ACT.Copy))
            for pair in range(4 + 1):
                if pair < 4:
                    for u in (0, 1):
                        o = get(("z", l_, 2 * pair + u))
                        if pair and u == 0:
                            wait("stick_probs", 4 * l_ + pair)
                        ins = act.activation(logit[:, u, :], o[:, :], ACT.Abs)
                    link(ins)
                    link(act.activation(logit[:, :, :], logit[:, :, :], ACT.Exp, scale=-1.0))
                    act.activation(logit[:, :, :], logit[:, :, :], ACT.Ln, bias=1.0).then_inc(sig("log1p_ready"), 1)
                if pair:
                    name = ("yb", l_, pair - 1)
                    o = get(name)
                    high(name, yh[:, 4 + pair - 1, :], o[:, 0:S])
                if pair < 4:
                    filler(l_, 2 * pair)
                    ahead(("later", l_, 2 * pair + 1))
                    await_read(("later", l_, 2 * pair))
                    await_read(("later", l_, 2 * pair + 1))
                    act.activation(probT[:, :, :], logit[:, :, :], ACT.Exp).then_inc(sig("stick_probs"), 1)
                    filler(l_, 2 * pair + 1)
            for t in range(-1, 8 + 4):
                if 2 <= t < 10:
                    probs_T(unit[0] + t - 2)
                if 0 <= t < 8:
                    g = unit[0] + t
                    ahead(("S", g))
                    wait("neg_max", g + 1)
                    exps(g, logit[:, g % 2, :], prob[:, g % 2, :]).then_inc(sig("exp_done"), 1)
                if t + 1 < 8:
                    o = get(("ql", l_, t + 1))
                    free(("ql", l_, t + 1), act.activation(ql[:, (t + 1) % 2, :], o[:, 0:S], ACT.Copy))
                if t >= 4 and t % 2:
                    name = ("ya", l_, (t - 4) // 2)
                    o = get(name)
                    high(name, yh[:, (t - 4) // 2, :], o[:, 0:S])
                if t in (8, 9):
                    open_gates(l_, range(3 * t - 24, 3 * t - 21))
                if t in LATENT_GATES:
                    gate_tile(l_, LATENT_GATES[t])
            unit[0] += 8
            ahead(("branch", l_, 0, BRANCHES[0]))
            open_gates(l_, range(6, 8))
            for n in range(4):
                for pos in range(3):
                    if 3 * n + pos >= 8:
                        gate_tile(l_, 3 * n + pos)
                ahead(("branch", l_, n, BRANCHES[2]))
                wait("merged_ready", 4 * l_ + n + 1)
                high(("merged", l_, n), oh[:, 2 * n:2 * n + 2, :], two(logit[:, n % 2, :]))
            out_proj(j)

        split_to(0)
        x_to_T(0)
        program_of = {"even": even, "odd": odd, "merge": merge, "cross": cross, "ffn": ffn}
        for j, (kind, _, _, _) in enumerate(SUB[:LAST]):
            program_of[kind](j)

    @block.vector
    def _(dve):
        tile = [0]
        step = [0]
        low_no = [0]
        unit = [0]
        biased_no = [0]

        def split_to(n):
            while tile[0] <= min(n, len(weight_tiles) - 1):
                t = tile[0]
                dve.wait_ge(raw_full[t % RAW], raw_done[t])
                dve.wait_ge(sig("w_high"), t + 1)
                if t >= PARTS:
                    dve.wait_ge(sig("weights_used"), t - PARTS + 1)
                _, nk, w = weight_tiles[t]
                dve.tensor_tensor(wl[:, t % PARTS, 0:nk * w], raw_tile(t),
                                  wh[:, t % PARTS, 0:nk * w].bitcast(F32), ALU.subtract)\
                   .then_inc(sig("w_low"), 1)
                tile[0] += 1

        def ahead(name, look=PARTS - 1):
            split_to(where[name][2] + look)

        def get(name, look=PARTS - 1):
            b, n, _, _ = where[name]
            ahead(name, look)
            dve.wait_ge(bank_full[b], n)
            return ps[b]

        def free(name, ins):
            ins.then_inc(bank_free[where[name][0]], 1)

        def await_read(name):
            dve.wait_ge(bank_free[where[name][0]], where[name][3])

        def wait(name, n):
            dve.wait_ge(sig(name), n)

        def link(ins):
            step[0] += 1
            ins.then_inc(sig("dve_step"), 1)
            dve.wait_ge(sig("dve_step"), step[0])

        def low(name, dst, src, hi, from_bank=True):
            assert halves[name] == low_no[0], name
            low_no[0] += 1
            wait("part_high", low_no[0])
            assert in_banks[low_no[0] - 1] == from_bank, name
            ins = dve.tensor_tensor(dst, src, hi.bitcast(F32), ALU.subtract)
            if from_bank:
                free(name, ins)
            else:
                ins.then_inc(sig("part_low"), 1)

        def copy_used(name):
            wait("part_low", copies[halves[name]])

        def quad(ap):
            return ap.rearrange("p (c s) -> p c s", c=4)

        def two(ap):
            return ap.rearrange("p (c s) -> p c s", c=2)

        def along(v, n):
            return v.unsqueeze(2).broadcast_to([P, v.shape[1], n])

        def x_to_T(i, blocks=range(TB)):
            for t in blocks:
                for half in range(2):
                    name = ("xT", i, t, half)
                    o = get(name, 1 if i == 0 or len(blocks) < TB else PARTS - 1)
                    c = slice(half * 4, half * 4 + 4)
                    low(name, xl[:, c, t * P:t * P + P], quad(o[:, :]), xh[:, c, t * P:t * P + P])

        def out_proj(j):
            _, _, c = norm_of(j)

            def residual(t, half):
                f = slice(half * 512, half * 512 + 512)
                name = ("y", j, t, half)
                o = get(name, 1 if t and half and not cross_after(j) else PARTS - 1)
                free(name, dve.scalar_tensor_tensor(z[:, t, f], x[:, t, f], ALPHA / c, o[:, :], ALU.mult, ALU.add))
                await_read(name)
                link(dve.bn_stats(stat[:, t, half, :], z[:, t, f]))

            by_block = not cross_after(j) and SUB[j][0] != "ffn"
            if not by_block:
                for t in range(TB):
                    residual(t, 0)
            if cross_after(j):
                for t in range(TB):
                    for h2 in range(2):
                        name = ("memT", j + 1, t, h2)
                        o = get(name)
                        k = slice(h2 * 4, h2 * 4 + 4)
                        low(name, ml[:, k, t * P:t * P + P], quad(o[:, :]), mh[:, k, t * P:t * P + P])
            for t in range(TB):
                if cross_after(j):
                    ahead(("y", j, 1, 1))
                if by_block:
                    residual(t, 0)
                residual(t, 1)
                link(dve.bn_aggr(mv[:, t, 0:2], stat[:, t, 0:2, :]))
                dve.tensor_scalar(mv[:, t, 1:2], mv[:, t, 1:2], EPS / c ** 2, None, ALU.add)\
                   .then_inc(sig("var_ready"), 1)
                if t == 0:
                    wait("gains_loaded", 32 * (j + 1))
                for half in range(2):
                    f = slice(half * 512, half * 512 + 512)
                    link(dve.scalar_tensor_tensor(z[:, t, f], z[:, t, f], mv[:, t, 0:1], gb[:, 0, f],
                                                  ALU.subtract, ALU.mult))
                    if half == 0:
                        wait("std_ready", 2 * j + t + 1)
                        link(dve.reciprocal(mv[:, t, 3:4], mv[:, t, 2:3]))
                    dve.scalar_tensor_tensor(x[:, t, f], z[:, t, f], mv[:, t, 3:4], gb[:, 1, f],
                                             ALU.mult, ALU.add).then_inc(sig("x_ready"), 1)
                if j + 1 < LAST and not cross_after(j):
                    x_to_T(j + 1, [t])
            if cross_after(j):
                c = cross_of(SUB[j + 1][1], 0)[4]
                for half in range(c):
                    if half == c - 1:
                        x_to_T(j + 1)
                    for t in range(TB):
                        name = ("xv", j + 1, t, half)
                        o = get(name)
                        free(name, dve.tensor_copy(xv[:, t, half * 512:half * 512 + 512], o[:, :]))

        def softmax(n_units, biased, after):
            for t in range(n_units + 3):
                if 1 <= t <= n_units:
                    normalise(unit[0] + t - 1, biased)
                if t >= 3 and biased:
                    after(t - 3)
                if t < n_units:
                    neg_max(unit[0] + t, biased)
                if t >= 3 and not biased:
                    after(t - 3)
            unit[0] += n_units

        def neg_max(g, biased):
            o = get(("S", g))
            if biased:
                dve.wait_ge(sig("bias_ready"), biased_no[0] + 1)
                if g >= 2:
                    wait("neg_max", g - 1)
                free(("S", g), dve.tensor_tensor(logit[:, g % 2, :], o[:, :], bias_of(g), ALU.add))
                await_read(("S", g))
                o = logit[:, g % 2, :]
                biased_no[0] += 1
            dve.tensor_reduce(nmax[:, g % 2, 0:2], two(o[:, :] if not biased else o), AX, ALU.max, negate=True)\
               .then_inc(sig("neg_max"), 1)

        def normalise(g, biased):
            if biased:
                wait("exp_done", biased_done[0] + 1)
                biased_done[0] += 1
            else:
                await_read(("S", g))
            link(dve.reciprocal(rden[:, g % 2, 0:2], psum_e[:, g % 2, 0:2]))
            dve.tensor_tensor(two(prob[:, g % 2, :]), two(prob[:, g % 2, :]), along(rden[:, g % 2, 0:2], S),
                              ALU.mult).then_inc(sig("prob_ready"), 1)

        def cross(j):
            c = cross_of(SUB[j][1], 0)[4]
            base = unit[0]

            def after(u):
                name = ("O", base + u)
                o = get(name)
                k = slice(c * u, c * u + c)
                low(name, ol[:, k, :], o[:, 0:c * S].rearrange("p (c s) -> p c s", c=c), oh[:, k, :])

            split_to(where[("S", base)][2] + PARTS - 1)
            softmax(4, False, after)
            out_proj(j)

        def ffn(j):
            for q in range(HC // 2 + 1):
                if q < HC // 2:
                    name = ("up", j, q)
                    o = get(name)
                    await_read(("gate", j, q))
                    if q >= 2:
                        copy_used(("hid", j, q - 2))
                    free(name, dve.tensor_tensor(hid[:, q % 2, :], gate_s[:, q % 2, :], o[:, :], ALU.mult))
                if q >= 1:
                    k = slice(2 * q - 2, 2 * q)
                    low(("hid", j, q - 1), hl[:, k, :], two(hid[:, (q - 1) % 2, :]), hh[:, k, :], False)
            out_proj(j)

        def even(j):
            o = get("gates")
            wait("even_loaded", 32)
            for t in range(TB):
                ins = dve.tensor_tensor(gt[:, t, :], o[:, t * 16:t * 16 + 16], gbias[:, :], ALU.add)
            free("gates", ins)
            await_read("gates")
            f = gt[:, :, 8:16]
            dve.scalar_tensor_tensor(lf[:, 0, :, :], f, -1.0, f, ALU.mult, ALU.max).then_inc(sig("abs_f"), 1)
            for n in range(4):
                get(("aqk", n))
                await_read(("aqk", n))
                if n == 0:
                    o = get("cols")
                    free("cols", dve.tensor_copy(pc[:, 0:N_ROWS], o[:, 0:N_ROWS]))
                    await_read("cols")
                for tap in range(5):
                    for k in (2 * n, 2 * n + 1):
                        w = pc[:, ROWS["even_conv_w"] + tap * 8 + k:ROWS["even_conv_w"] + tap * 8 + k + 1]
                        if tap == 0:
                            ins = dve.tensor_scalar(qkT[:, k, :], cpad[:, k, 0:S], w, None, ALU.mult)
                        else:
                            ins = dve.scalar_tensor_tensor(qkT[:, k, :], cpad[:, k, tap:tap + S], w, qkT[:, k, :],
                                                           ALU.mult, ALU.add)
                    if n == 3 and tap == 4:
                        ins.then_inc(sig("conv_done"), 1)
                    else:
                        link(ins)
            wait("softplus_f", 1)
            dve.scalar_tensor_tensor(lf[:, 3, :, :], f, 0.0, lf[:, 2, :, :], ALU.min, ALU.subtract)\
               .then_inc(sig("logf_ready"), 1)
            for t in range(TB):
                name = ("av", t)
                o = get(name)
                free(name, dve.tensor_copy(av[:, t, :, 0:P], quad(o[:, :])))
            for t in range(TB):
                name = ("bv", t)
                o = get(name)
                free(name, dve.tensor_copy(bv[:, t, :], o[:, :]))
            wait("silu_done", 1)
            dve.tensor_scalar(qkT[:, 4:8, :], qkT[:, 4:8, :], float(P ** -0.5), None, ALU.mult)\
               .then_inc(sig("qk_ready"), 1)
            o = get("cum")
            free("cum", dve.tensor_copy(bs[:, :], o[:, 0:32]))
            await_read("cum")
            dve.tensor_tensor(cc_[:, :, :], gt[:, :, 0:8], two(bs[:, 0:16]), ALU.subtract)\
               .then_inc(sig("decay_cols"), 1)
            wait("decay_cols", 1)
            b_of = bs[:, 0:16].rearrange("p (t d h) -> p t d h", t=TB, d=2)
            tot = bs[:, 16:32].rearrange("p (t d h) -> p t d h", t=TB, d=2)
            c_of = cc_[:, :, :].rearrange("p t (d h) -> p t d h", d=2)
            for d in range(2):
                mask = ec[:, 512 + d * P:640 + d * P].unsqueeze(1).broadcast_to([P, 4, P])
                for t in range(TB):
                    name = ("C", d, t)
                    o = get(name)
                    if t == d:
                        dve.tensor_reduce(mm_[:, 0, d, t, :], quad(o[:, :]), AX, ALU.max)
                    free(name, dve.tensor_tensor(cm[:, d, t, :, :], quad(o[:, :]), mask, ALU.add))
                    await_read(name)
                    link(dve.tensor_reduce(mm_[:, 1, d, t, :], cm[:, d, t, :, :], AX, ALU.max))
            for d in range(2):
                t1, t2 = d, 1 - d
                link(dve.tensor_tensor(mm_[:, 2, d, t2, :], tot[:, t1, d, :], mm_[:, 0, d, t1, :], ALU.add))
                dve.tensor_copy(mm_[:, 3, d, t1, :], mm_[:, 1, d, t1, :])
                link(dve.tensor_tensor(mm_[:, 3, d, t2, :], mm_[:, 1, d, t2, :], mm_[:, 2, d, t2, :], ALU.max))
                link(dve.tensor_scalar(mm_[:, 4, d, :, :], mm_[:, 3, d, :, :], -1.0, None, ALU.mult))
                dve.tensor_tensor(mm_[:, 5, d, :, :], b_of[:, :, d, :], mm_[:, 3, d, :, :], ALU.add)
                dve.tensor_tensor(mm_[:, 6, d, t2, :], mm_[:, 2, d, t2, :], mm_[:, 3, d, t2, :], ALU.subtract)
                link(dve.tensor_tensor(mm_[:, 7, d, t1, :], c_of[:, t1, d, :], mm_[:, 0, d, t1, :], ALU.subtract))
            for d in range(2):
                ins = dve.memset(mm_[:, 6, d, d, :], 0.0)
                ins = dve.memset(mm_[:, 7, d, 1 - d, :], 0.0)
            ins.then_inc(sig("decay_exponents"), 1)
            wait("mlstm_small", 3)
            for d in range(2):
                name = ("kN", d)
                o = get(name)
                free(name, dve.tensor_tensor(pk[:, d, :, :], quad(o[:, :]), along(mm_[:, 7, d, d, :], P), ALU.mult))
            for t in range(TB):
                name = ("QK", t)
                o = get(name)
                for d in range(2):
                    wait("decay_ready", 2 * t + d + 1)
                    ins = dve.tensor_tensor(cm[:, d, t, :, :], cm[:, d, t, :, :], quad(o[:, :]), ALU.mult)
                    ins.then_inc(sig("decayed"), 1)
                    wait("decayed", 2 * t + d + 1)
                    ins = dve.tensor_reduce(mm_[:, 8, d, t, :], cm[:, d, t, :, :], AX, ALU.add)
                free(name, ins)
            for d in range(2):
                t2 = 1 - d
                for half in range(2):
                    name = ("int", d, half)
                    o = get(name)
                    h2 = slice(2 * half, 2 * half + 2)
                    free(name, dve.tensor_tensor(cn[:, d, h2, :], o[:, 0:260].rearrange("p (h e) -> p h e", h=2),
                                                 along(mm_[:, 6, d, t2, h2], 130), ALU.mult))
                    await_read(name)
                link(dve.tensor_tensor(mm_[:, 8, d, t2, :], mm_[:, 8, d, t2, :], cn[:, d, :, P], ALU.add))
            den = mm_[:, 8, :, :, :]
            link(dve.scalar_tensor_tensor(mm_[:, 9, :, :, :], den, -1.0, den, ALU.mult, ALU.max))
            link(dve.tensor_tensor(mm_[:, 9, :, :, :], mm_[:, 9, :, :, :], mm_[:, 5, :, :, :], ALU.max))
            link(dve.reciprocal(mm_[:, 9, :, :, :], mm_[:, 9, :, :, :]))
            for t in range(TB):
                for d in range(2):
                    name = ("num", d, t)
                    o = get(name)
                    h_d = quad(prob[:, d, :])
                    rd = along(mm_[:, 9, d, t, :], P)
                    if d == t:
                        free(name, dve.tensor_tensor(h_d, quad(o[:, :]), rd, ALU.mult))
                        await_read(name)
                    else:
                        free(name, dve.tensor_tensor(h_d, quad(o[:, :]), cn[:, d, :, 0:P], ALU.add))
                        await_read(name)
                        link(dve.tensor_tensor(h_d, h_d, rd, ALU.mult))
                dve.tensor_tensor(logit[:, t, :], prob[:, 0, :], prob[:, 1, :], ALU.add)\
                   .then_inc(sig("mlstm_out"), 1)
                wait("mlstm_out", t + 1)
            dve.wait_ge(bank_free[where[("ao", 1)][0]], where[("ao", 1)][3])
            for t in range(TB):
                name = ("hT", t)
                o = get(name)
                free(name, dve.tensor_tensor(quad(probT[:, t, :]), quad(o[:, :]), ao[:, :, t * P:t * P + P], ALU.mult))
            for t in range(TB):
                low(("aT", t), ol[:, 0:4, t * P:t * P + P], quad(probT[:, t, :]), oh[:, 0:4, t * P:t * P + P], False)
            base = unit[0]

            def after(u):
                if u % 2:
                    name = ("O", base + u - 1)
                    o = get(name)
                    low(name, ol[:, 4 + u // 2, :], o[:, 0:S], oh[:, 4 + u // 2, :])

            softmax(8, True, after)
            out_proj(j)

        def odd(j):
            ahead(("rp", 0))
            wait("lam_loaded", 16)
            lt = lamt[:, :, :].rearrange("p (a b) e -> p a b e", b=2)
            link(dve.tensor_tensor(rt[:, 0, 0:128].rearrange("p (a e) -> p a e", a=2), lt[:, :, 0, :], lt[:, :, 1, :],
                                   ALU.mult))
            dve.tensor_reduce(lam[:, 0:2], rt[:, 0, 0:128].rearrange("p (a e) -> p a e", a=2), AX, ALU.add)\
               .then_inc(sig("lam_sums"), 1)
            wait("lam_exp", 1)
            link(dve.tensor_tensor(lam[:, 4:5], lam[:, 3:4], lam[:, 2:3], ALU.subtract))
            link(dve.tensor_scalar(lam[:, 5:6], lam[:, 4:5], -LAM_INIT, None, ALU.add))
            link(dve.tensor_scalar(lam[:, 6:7], pc[:, ROWS["odd_subln_g"]:ROWS["odd_subln_g"] + 1],
                                   1.0 - LAM_INIT, None, ALU.mult))
            cos = oc[:, 128:384].unsqueeze(1).broadcast_to([P, 2, S])
            sin = oc[:, 384:640].unsqueeze(1).broadcast_to([P, 2, S])

            def rope(k):
                name = ("rot", k)
                ahead(("rp", k))
                o = get(name)
                n = ROPE_ORDER[k]
                if k == 0:
                    wait("odd_loaded", 16)
                else:
                    wait("rope_done", k)
                free(name, dve.tensor_tensor(two(rt[:, 0, :]), two(o[:, :]), sin, ALU.mult))
                link(dve.tensor_tensor(two(rt[:, 1, :]), two(rs[:, k % 2, :]), cos, ALU.mult))
                await_read(name)
                dve.tensor_tensor(rq[:, 2 * n:2 * n + 2, :], two(rt[:, 0, :]), two(rt[:, 1, :]), ALU.add)\
                   .then_inc(sig("rope_done"), 1)

            def variances(half):
                v = slice(8 * half, 8 * half + 8)
                dve.tensor_scalar(oss[:, 0, v], oss[:, 2, v], 1.0 / P, EPS, ALU.mult, ALU.add)\
                   .then_inc(sig("diff_var"), 1)

            def norm_heads(half):
                wait("diff_std", half + 1)
                v = slice(8 * half, 8 * half + 8)
                link(dve.reciprocal(oss[:, 2, v], oss[:, 1, v]))
                for u in range(4 * half, 4 * half + 4):
                    dve.tensor_tensor(on[:, u, :, :], on[:, u, :, :], along(oss[:, 2, 2 * u:2 * u + 2], P), ALU.mult)\
                       .then_inc(sig("diff_normed"), 1)

            def normed(u):
                name = ("OT", u)
                o = get(name)
                if u >= 2:
                    copy_used(("OT", u - 2))
                free(name, dve.tensor_scalar(osq[:, u % 2, :], o[:, 0:S], lam[:, 6:7], None, ALU.mult))
                low(name, ol[:, u, :], osq[:, u % 2, :], oh[:, u, :], False)

            rope(0)
            rope(1)
            for t in range(8 + 3):
                if t < 8:
                    g = unit[0] + t
                    for c in range(2):
                        o = get(("S", g, c))
                        ins = dve.tensor_reduce(nmax[:, g % 2, 2 * c:2 * c + 2], two(o[:, :]), AX, ALU.max,
                                                negate=True)
                    ins.then_inc(sig("neg_max"), 1)
                if t + 2 < 8:
                    rope(t + 2)
                if 1 <= t <= 8:
                    g = unit[0] + t - 1
                    buf = (prob, logit)[(t - 1) % 2]
                    await_read(("S", g, 0))
                    await_read(("S", g, 1))
                    link(dve.reciprocal(rden[:, g % 2, :], psum_e[:, g % 2, :]))
                    link(dve.tensor_scalar(rden[:, g % 2, 2:4], rden[:, g % 2, 2:4], lam[:, 5:6], None, ALU.mult))
                    for tb in range(TB):
                        sl = slice(tb * S, tb * S + S)
                        ins = dve.tensor_scalar(buf[:, 0, sl], buf[:, 0, sl], rden[:, g % 2, tb:tb + 1], None, ALU.mult)
                    link(ins)
                    for tb in range(TB):
                        sl = slice(tb * S, tb * S + S)
                        ins = dve.scalar_tensor_tensor(buf[:, 0, sl], buf[:, 1, sl], rden[:, g % 2, 2 + tb:3 + tb],
                                                       buf[:, 0, sl], ALU.mult, ALU.add)
                    ins.then_inc(sig("prob_ready"), 1)
                if t >= 3:
                    u = t - 3
                    name = ("O", unit[0] + u)
                    o = get(name)
                    free(name, dve.tensor_copy(on[:, u, :, :], two(o[:, 0:2 * P])))
                    await_read(name)
                    if u >= 6:
                        copy_used(("OT", 2 * u - 11))
                    link(dve.tensor_tensor(two(osq[:, u % 2, :]), on[:, u, :, :], on[:, u, :, :], ALU.mult))
                    link(dve.tensor_reduce(oss[:, 2, 2 * u:2 * u + 2], two(osq[:, u % 2, :]), AX, ALU.add))
                if t == 6:
                    variances(0)
                if t == 7:
                    norm_heads(0)
                if t in (8, 9):
                    normed(2 * t - 16)
                    normed(2 * t - 15)
            variances(1)
            norm_heads(1)
            for u in range(4, 8):
                normed(u)
            unit[0] += 8
            out_proj(j)

        def conv_tile(l_, i):
            n = i // 3
            y = two(bm[:, 1, :])
            if i % 3 == 0:
                ahead(("cc", l_, n))
            elif i % 3 == 1:
                name = ("ch", l_, n)
                o = get(name)
                wait("zc_pads", l_ + 1)
                await_read(("cc", l_, n))
                free(name, dve.tensor_tensor(zc[:, :, 2:2 + S], y, two(o[:, :]), ALU.mult))
                await_read(name)
                for tap in range(3):
                    for k in range(2):
                        r = ROWS["conv_w_2"] + l_ * 12 + tap * 4 + 2 * n + k
                        w = pc[:, r:r + 1]
                        if tap == 0:
                            ins = dve.tensor_scalar(y[:, k, :], zc[:, k, 0:S], w, None, ALU.mult)
                        else:
                            ins = dve.scalar_tensor_tensor(y[:, k, :], zc[:, k, tap:tap + S], w, y[:, k, :],
                                                           ALU.mult, ALU.add)
                    link(ins)
            else:
                name = ("cb", l_, n)
                o = get(name)
                free(name, dve.tensor_tensor(bm[:, 1, :], bm[:, 1, :], o[:, :], ALU.mult))
                k = slice(8 + 2 * n, 10 + 2 * n)
                low(("yc", l_, n), yl[:, k, :], y, yh[:, k, :], False)

        def filler(l_, i):
            what, number = FILLERS[i]
            if what == "conv":
                conv_tile(l_, number)
            else:
                ahead(("bgate", l_, number // 3, BRANCHES[number % 3]))

        def merge(j):
            l_ = SUB[j][2]
            for t in range(TB):
                name = ("ckv", l_, t)
                o = get(name)
                free(name, dve.tensor_copy(ckn[:, t, :], o[:, 0:P]))
                await_read(name)
            link(dve.tensor_tensor(cksq[:, :, :], ckn[:, :, :], ckn[:, :, :], ALU.mult))
            link(dve.tensor_reduce(cks[:, 0:2], cksq[:, :, :], AX, ALU.add))
            dve.tensor_scalar(cks[:, 0:2], cks[:, 0:2], 1.0 / P, EPS, ALU.mult, ALU.add).then_inc(sig("ckv_var"), 1)
            wait("ckv_std", l_ + 1)
            link(dve.reciprocal(cks[:, 0:2], cks[:, 2:4]))
            for t in range(TB):
                dve.tensor_scalar(ckn[:, t, :], ckn[:, t, :], cks[:, t:t + 1], None, ALU.mult)\
                   .then_inc(sig("ckv_normed"), 1)
            name = ("iw", l_)
            o = get(name)
            free(name, dve.tensor_scalar(iw[:, :, :], o[:, 0:16].rearrange("p (t h) -> p t h", t=TB),
                                         float(8 ** -0.5 * 64 ** -0.5), None, ALU.mult))
            await_read(name)
            g = pc[:, ROWS["kv_norm_g_2"] + l_:ROWS["kv_norm_g_2"] + l_ + 1]
            name = ("ckT", l_)
            o = get(name)
            free(name, dve.tensor_scalar(ckT[:, :], o[:, 0:S], g, None, ALU.mult))
            wait("merge_loaded", 32 * (l_ + 1))
            for u in range(8):
                split_to(where[("dot", l_, u)][2] + PARTS - 1)
                await_read(("dot", l_, u))
                for tb in range(TB):
                    before = sc_[:, tb * S:tb * S + S] if u == 0 else score[:, tb, :]
                    ins = dve.scalar_tensor_tensor(score[:, tb, :], prob[:, u % 2, tb * S:tb * S + S],
                                                   iw[:, tb, u:u + 1], before, ALU.mult, ALU.add)
                ins.then_inc(sig("scored"), 1)
                wait("scored", 8 * l_ + u + 1)

            def choose(tb):
                w = P * (tb + 1)
                for r in range(TOPK // 8):
                    link(dve.max(top8[:, :], score[:, tb, 0:w]))
                    link(dve.match_replace(score[:, tb, 0:w], top8[:, :], score[:, tb, 0:w], FOUND))
                link(dve.tensor_scalar(selm[:, tb, :], score[:, tb, :], FOUND / 3, NEG, ALU.is_ge, ALU.mult))
                dve.tensor_tensor(selm[:, tb, :], selm[:, tb, :], sc_[:, tb * S:tb * S + S], ALU.add)\
                   .then_inc(sig("chosen"), 1)

            choose(0)
            split_to(where[("qa", l_, 1)][2] + PARTS - 1)
            choose(1)
            for pair in range(4 + 1):
                units = (2 * pair, 2 * pair + 1) if pair < 4 else ()
                for u in units:
                    name = ("z", l_, u)
                    o = get(name)
                    wait("log1p_ready", 4 * l_ + pair + 1)
                    dve.scalar_tensor_tensor(prob[:, u % 2, :], o[:, :], 0.0, logit[:, u % 2, :], ALU.max, ALU.add)\
                       .then_inc(sig("softplus_ready"), 1)
                for u in units:
                    name = ("z", l_, u)
                    o = get(name)
                    wait("softplus_ready", 8 * l_ + u + 1)
                    free(name, dve.tensor_tensor(logit[:, u % 2, :], o[:, :], sc_[:, 1024:1536], ALU.add))
                if pair == 0:
                    for t in range(TB):
                        name = ("vs", l_, t)
                        o = get(name)
                        free(name, dve.tensor_copy(vs[:, t, :], o[:, :]))
                if pair:
                    name = ("yb", l_, pair - 1)
                    o = get(name)
                    low(name, yl[:, 4 + pair - 1, :], o[:, 0:S], yh[:, 4 + pair - 1, :])
                if pair < 4:
                    filler(l_, 2 * pair)
                for u in units:
                    name = ("later", l_, u)
                    o = get(name)
                    await_read(("z", l_, u))
                    free(name, dve.tensor_tensor(logit[:, u % 2, :], logit[:, u % 2, :], o[:, :], ALU.subtract))
                if pair < 4:
                    filler(l_, 2 * pair + 1)
            for t in range(-1, 8 + 4):
                if 1 <= t <= 8:
                    normalise(unit[0] + t - 1, True)
                if 0 <= t < 8:
                    neg_max(unit[0] + t, True)
                if 3 <= t <= 10:
                    u = t - 3
                    name = ("lat", l_, u)
                    o = get(name)
                    free(name, dve.tensor_scalar(olat[:, u % 2, :], o[:, 0:S], g, None, ALU.mult))
                if t >= 4 and t % 2:
                    i = (t - 4) // 2
                    name = ("ya", l_, i)
                    o = get(name)
                    low(name, yl[:, i, :], o[:, 0:S], yh[:, i, :])
                if t in LATENT_GATES:
                    k = LATENT_GATES[t]
                    ahead(("bgate", l_, k // 3, BRANCHES[k % 3]))
            unit[0] += 8
            for n in range(4):
                for pos, i in enumerate(BRANCHES):
                    k = 3 * n + pos
                    name = ("branch", l_, n, i)
                    o = get(name)
                    if k < 8:
                        wait("gates_open", 8 * l_ + k + 1)
                    else:
                        await_read(("bgate", l_, n, i))
                    if pos == 0 and n >= 2:
                        copy_used(("merged", l_, n - 2))
                    if pos == 0 and n >= 1:
                        wait("merged_ready", 4 * l_ + n)
                    dst = logit[:, n % 2, :] if pos == 0 else probT[:, k % 2, :]
                    free(name, dve.tensor_tensor(dst, open_gate(k), o[:, :], ALU.mult))
                    await_read(name)
                    if pos:
                        ins = dve.tensor_tensor(logit[:, n % 2, :], logit[:, n % 2, :], probT[:, k % 2, :], ALU.add)
                        if pos == 1:
                            link(ins)
                        else:
                            ins.then_inc(sig("merged_ready"), 1)
                k = slice(2 * n, 2 * n + 2)
                low(("merged", l_, n), ol[:, k, :], two(logit[:, n % 2, :]), oh[:, k, :], False)
            out_proj(j)

        biased_done = [0]
        dve.memset(ones[:, :], 1.0).then_inc(sig("ones_set"), 1)
        split_to(0)
        x_to_T(0)
        program_of = {"even": even, "odd": odd, "merge": merge, "cross": cross, "ffn": ffn}
        for j, (kind, _, _, _) in enumerate(SUB[:LAST]):
            program_of[kind](j)

    @block.gpsimd
    def _(pool):
        step = [0]
        unit = [0]
        biased = [0]
        mems = [0]

        def await_read(name):
            pool.wait_ge(bank_free[where[name][0]], where[name][3])

        def link(ins):
            step[0] += 1
            ins.then_inc(sig("pool_step"), 1)
            pool.wait_ge(sig("pool_step"), step[0])

        def const(dst, name, width, what):
            c0 = CONST[name][0]
            pool.dma_start(dst, A["consts"][:, c0:c0 + width]).then_inc(sig(what), 16)

        def gains(j):
            if j:
                pool.wait_ge(sig("x_ready"), 4 * j)
            g, b, _ = norm_of(j)
            for i, v in enumerate((g, b)):
                pool.dma_start(gb[:, i, :], v.partition_broadcast(P)).then_inc(sig("gains_loaded"), 16)

        def mem_load(j):
            if not cross_after(j) or j >= LAST:
                return
            await_halves(pool, mem_start[j + 1])
            pool.dma_start(mem_n[:, :, :], cross_of(SUB[j + 1][1], 0)[0].rearrange("(t p) d -> p t d", p=P))\
                .then_inc(sig("mem_loaded"), 16)

        def cross(j):
            unit[0] += 4

        def ffn(j):
            pass

        def even(j):
            def load(u):
                for r in range(4):
                    src = bass.AP(tensor=rpb_d.tensor, offset=(u * 7 + 3 - r) * P + 63,
                                  ap=[[7 * 8 * P - 1, 64], [P, 4], [1, 64]])
                    q = slice(64 * (r % 2), 64 * (r % 2) + 64)
                    c0 = (r // 2) * S
                    pool.dma_start(bias_of(u)[q, c0:c0 + S].rearrange("p (a c) -> p a c", a=4), src)\
                        .then_inc(sig(f"bias_loaded{u}"), 16)

            def mask(u):
                pool.wait_ge(sig(f"bias_loaded{u}"), 64)
                m = ec[:, 256:512].unsqueeze(1).broadcast_to([P, 2, S])
                b = bias_of(u).rearrange("p (t s) -> p t s", t=2)
                pool.tensor_tensor(b, b, m, ALU.add).then_inc(sig("bias_ready"), 1)

            pool.memset(av[:, :, :, P:P + 2], 1.0).then_inc(sig("av_ones"), 1)
            pool.memset(cpad[:, :, 0:2], 0.0)
            pool.memset(cpad[:, :, S + 2:S + 4], 0.0).then_inc(sig("pads_set"), 1)
            link(pool.memset(rpad[:, :, :, :], 0.0))
            for pair in range(4):
                for i in range(2):
                    pool.dma_start(rpad[:, i, :, 48:79],
                                   A["even_rpb"][0, 2 * pair + i, 4:11, :].partition_broadcast(64))\
                        .then_inc(sig("rpb_loaded"), 16)
                pool.wait_ge(sig("rpb_loaded"), 32 * (pair + 1))
                pool.dma_start(rpb_d[:, pair * 14 * P:(pair + 1) * 14 * P],
                               rpad[:, :, :, :].rearrange("p h r c -> p (h r c)"))\
                    .then_inc(sig("rpb_stored"), 16)
                pool.wait_ge(sig("rpb_stored"), 16 * (pair + 1))
            await_read(("tab", 7))
            pool.dma_start(bias_d, btab[:, :, :].rearrange("p h c -> p (h c)"))\
                .then_inc(sig("distances_stored"), 16)
            load(0)
            load(1)
            mask(0)
            mask(1)
            for t in range(TB):
                await_read(("QK", t))
                for d in range(2):
                    await_read(("ST", d, t))
            for u in range(2, 8):
                if u >= 6:
                    await_read(("S", u - 6))
                load(u)
                if u >= 3:
                    mask(u - 1)
            mask(7)
            unit[0] += 8
            biased[0] += 8

        def odd(j):
            const(oc[:, :], "rot", 640, "odd_loaded")
            pool.dma_start(lamt[:, :, :].rearrange("p a e -> p (a e)"),
                           A["odd_lambda"][0].rearrange("a e -> (a e)").partition_broadcast(P))\
                .then_inc(sig("lam_loaded"), 16)
            unit[0] += 8

        def merge(j):
            l_ = SUB[j][2]
            const(sc_[:, :], "topk_causal", 1536, "merge_loaded")
            const(tge[:, :], "tri_ge", P, "merge_loaded")
            pool.dma_start(uk[:, :, :], A["w_uk_2"][l_].rearrange("(a b) d c -> (b d) a c", b=2))\
                .then_inc(sig("latent_weights"), 16)
            pool.dma_start(uv[:, :, :], A["w_uv_2"][l_].rearrange("h c d -> c h d")).then_inc(sig("latent_weights"), 16)
            pool.memset(zc[:, :, 0:2], 0.0).then_inc(sig("zc_pads"), 1)

            pool.wait_ge(sig("distances_stored"), 16)

            def load(u):
                src = bass.AP(tensor=bias_d.tensor, offset=u * 512 + 127, ap=[[8 * 512 - 1, P], [1, 384]])
                pool.dma_start(gth[:, u % 2, :], src).then_inc(sig(f"distance_loaded{u % 2}"), 16)

            load(0)
            load(1)
            pool.wait_ge(sig("merge_loaded"), 32 * (l_ + 1))
            for u in range(8):
                pool.wait_ge(sig("softplus_ready"), 8 * l_ + u + 1)
                pool.tensor_tensor(prob[:, u % 2, :], prob[:, u % 2, :], sc_[:, 512:1024], ALU.mult)\
                    .then_inc(sig("softplus_masked"), 1)
            pool.wait_ge(sig("chosen"), 2 * (l_ + 1))
            pool.wait_ge(sig("part_low"), copies[halves[("yc", l_, 1)]])
            for u in range(8):
                if u >= 2:
                    await_read(("S", unit[0] + u - 2))
                pool.wait_ge(sig(f"distance_loaded{u % 2}"), 16 * (4 * l_ + u // 2 + 1))
                for tb in range(TB):
                    c0 = P * (1 - tb)
                    ins = pool.tensor_tensor(bm[:, u % 2, tb * S:tb * S + S], gth[:, u % 2, c0:c0 + S],
                                             selm[:, tb, :], ALU.add)
                biased[0] += 1
                ins.then_inc(sig("bias_ready"), 1)
                if u + 2 < 8:
                    pool.wait_ge(sig("bias_ready"), biased[0])
                    load(u + 2)
            unit[0] += 8

        for name, ap in (("even_conv_w", A["even_conv_w"][0].rearrange("j (c p) -> (j c) p", p=P)),
                         ("b_gate_2", A["b_gate_2"].rearrange("l i (c p) -> (l i c) p", p=P)),
                         ("conv_w_2", A["conv_w_2"].rearrange("l j (c p) -> (l j c) p", p=P)),
                         ("kv_norm_g_2", A["kv_norm_g_2"]), ("odd_subln_g", A["odd_subln_g"])):
            r = ROWS[name]
            pool.dma_start(prow[r:r + ap.shape[0], :], ap).then_inc(sig("rows_loaded"), 16)
        const(ec[:, :], "tri_le", 768, "even_loaded")
        pool.dma_start(gbias[:, :], A["even_gate_b"][0].partition_broadcast(P)).then_inc(sig("even_loaded"), 16)
        pool.dma_start(brel0[:, :], A["rel_bias_2"]).then_inc(sig("rel_loaded"), 16)
        const(boneh[:, :], "bucket", 512, "rel_loaded")
        program_of = {"even": even, "odd": odd, "merge": merge, "cross": cross, "ffn": ffn}
        for j, (kind, _, _, _) in enumerate(SUB[:LAST]):
            gains(j)
            program_of[kind](j)
            mem_load(j)

    @block.sync
    def _(sp):
        c0 = CONST["ident"][0]
        sp.dma_start(ident[:, :], A["consts"][:, c0:c0 + P]).then_inc(sig("ident_loaded"), 16)
        sp.dma_start(x[:, :, :], A["x"][0].rearrange("(t p) d -> p t d", p=P)).then_inc(sig("x_loaded"), 16)
        for t, (pieces, nk, w) in enumerate(weight_tiles):
            if t >= RAW:
                sp.wait_ge(sig("w_high"), t - RAW + 1)
                sp.wait_ge(sig("w_low"), t - RAW + 1)
            dst = raw_tile(t).rearrange("p (k c) -> p k c", k=nk)
            c0 = 0
            for piece in pieces:
                c1 = c0 + piece.shape[-1]
                sp.dma_start(dst[:, :, c0:c1], piece.rearrange("(k p) c -> p k c", p=P))\
                  .then_inc(raw_full[t % RAW], 16)
                c0 = c1
        sp.wait_ge(sig("x_ready"), 4 * LAST)
        sp.dma_start(out[0].rearrange("(t p) d -> p t d", p=P), x[:, :, :]).then_inc(out_stored, 16)
        sp.wait_ge(out_stored, 16)


def kernel(**inputs):
    import concourse.bacc as _bacc
    from concourse.bass_utils import run_bass_kernel_spmd as _run

    nc = _bacc.Bacc("TRN2", target_bir_lowering=False, num_devices=1)
    arrays, args = {}, {}
    for name, value in [*inputs.items(), ("consts", shape_constants())]:
        a = np.ascontiguousarray(value)
        arrays[f"in_{name}"] = a
        args[name] = nc.dram_tensor(f"in_{name}", a.shape, mybir.dt.from_np(a.dtype), kind="ExternalInput").ap()
    out = nc.dram_tensor("out_0", (1, S, D), F32, kind="ExternalOutput").ap()
    with ExitStack() as ctx:
        program(nc, ctx, args, out)
    r = _run(nc, [arrays], core_ids=[0])
    return r.results[0]["out_0"]
```
